# Optimizing a Trainium2 kernel written in Bass

```python
import jax, jax.numpy as jnp
from jax import lax
import numpy as np

D_MODEL = 1024
BATCH = 1
SEQ = 256
DEPTH = 2

BRANCH_W = 512
N_BRANCH = 3
CONV_K = 3
POOL_WINDOWS = (2, 4, 8, 16)
N_POOL_GROUPS = 4
POOL_GROUP_W = BRANCH_W // N_POOL_GROUPS
N_HEADS = 8
N_KV_HEADS = 2
HEAD_DIM = 64
KV_W = N_KV_HEADS * HEAD_DIM
WINDOW = 128
BLOCK = 128
ROPE_THETA = 10000.0
NEG_INF = -1e30
D_FF = 3584
N_EXPERTS = 8
TOP_K = 2
D_FF_EXPERT = 1792
PLE_DIM = 256
EPS = 1e-6

OFF_CONV_C = BRANCH_W
OFF_CONV_U = 2 * BRANCH_W
OFF_POOL = 3 * BRANCH_W
OFF_Q = OFF_POOL + BRANCH_W
OFF_K = OFF_Q + N_HEADS * HEAD_DIM
OFF_V = OFF_K + KV_W
OFF_GATE = OFF_V + KV_W
D_IN = OFF_GATE + N_BRANCH * D_MODEL

kernel_name = 'hybrid_conv_pool_swa_moe_trunk'

def rms_norm(x, g):
    xf = x.astype(jnp.float32)
    y = xf * lax.rsqrt(jnp.mean(xf * xf, axis=-1, keepdims=True) + EPS)
    return (y * g.astype(jnp.float32)).astype(x.dtype)

def rotary(x, positions):
    half = HEAD_DIM // 2
    inv_freq = ROPE_THETA ** (-2.0 * jnp.arange(half, dtype=jnp.float32) / HEAD_DIM)
    ang = positions.astype(jnp.float32)[..., None] * inv_freq
    cos = jnp.cos(ang)[:, :, None, :]
    sin = jnp.sin(ang)[:, :, None, :]
    xf = x.astype(jnp.float32)
    x1, x2 = xf[..., :half], xf[..., half:]
    return jnp.concatenate([x1 * cos - x2 * sin, x2 * cos + x1 * sin], axis=-1).astype(x.dtype)

def short_conv_mixer(b_gate, c_gate, u, conv_w):
    v = c_gate * u
    y = lax.conv_general_dilated(
        v, conv_w.astype(v.dtype)[:, None, :], window_strides=(1,),
        padding=((CONV_K - 1, 0),), dimension_numbers=('NWC', 'WIO', 'NWC'),
        feature_group_count=BRANCH_W)
    return b_gate * y

def pool_mixer(u, pool_w, pool_scale):
    B, S, _ = u.shape
    uf = u.astype(jnp.float32).reshape(B, S, N_POOL_GROUPS, POOL_GROUP_W)
    cs = jnp.cumsum(uf, axis=1)
    cs0 = jnp.pad(cs, ((0, 0), (1, 0), (0, 0), (0, 0)))
    t1 = jnp.arange(1, S + 1)
    lo = jnp.maximum(t1[:, None] - jnp.array(POOL_WINDOWS, dtype=jnp.int32)[None, :], 0)
    g_idx = jnp.arange(N_POOL_GROUPS)[None, :]
    cs_lo = cs0[:, lo, g_idx, :]
    count = (t1[:, None] - lo).astype(jnp.float32)[None, :, :, None]
    pooled = (cs - cs_lo) / count - uf
    mixed = jnp.einsum('bsgc,gcd->bsgd', pooled.astype(u.dtype), pool_w)
    return mixed.reshape(B, S, BRANCH_W) * pool_scale

def sliding_window_attention(q, k, v, sinks):
    B, S = q.shape[0], q.shape[1]
    nb = S // BLOCK
    G = N_HEADS // N_KV_HEADS
    qb = q.reshape(B, nb, BLOCK, N_KV_HEADS, G, HEAD_DIM)

    def band(t):
        prev = jnp.pad(t, ((0, 0), (BLOCK, 0), (0, 0), (0, 0)))[:, :S]
        return jnp.concatenate(
            [prev.reshape(B, nb, BLOCK, N_KV_HEADS, HEAD_DIM),
             t.reshape(B, nb, BLOCK, N_KV_HEADS, HEAD_DIM)], axis=2)

    kb, vb = band(k), band(v)
    scores = jnp.einsum('bnqkgd,bnjkd->bnkgqj', qb, kb,
                        preferred_element_type=jnp.float32) * (HEAD_DIM ** -0.5)
    qi = jnp.arange(BLOCK)[:, None] + BLOCK
    kj = jnp.arange(2 * BLOCK)[None, :]
    dist = qi - kj
    blk = jnp.arange(nb)[:, None, None]
    valid = (dist >= 0) & (dist < WINDOW) & (blk * BLOCK - BLOCK + kj >= 0)
    scores = jnp.where(valid[None, :, None, None], scores, NEG_INF)
    sink = sinks.astype(jnp.float32).reshape(1, 1, N_KV_HEADS, G, 1, 1)
    m = jnp.maximum(jnp.max(scores, axis=-1, keepdims=True), sink)
    pexp = jnp.exp(scores - m)
    denom = jnp.sum(pexp, axis=-1, keepdims=True) + jnp.exp(sink - m)
    probs = (pexp / denom).astype(v.dtype)
    out = jnp.einsum('bnkgqj,bnjkd->bnqkgd', probs, vb)
    return out.reshape(B, S, N_HEADS * HEAD_DIM)

def token_mixing(h, positions, w_in, conv_w, pool_w, pool_scale, sinks, w_branch, w_out):
    B, S, _ = h.shape
    proj = h @ w_in
    a_b, a_c, a_u, pool_u, q, k, v, gate_logits = jnp.split(
        proj, [OFF_CONV_C, OFF_CONV_U, OFF_POOL, OFF_Q, OFF_K, OFF_V, OFF_GATE], axis=-1)
    y_conv = short_conv_mixer(a_b, a_c, a_u, conv_w)
    y_pool = pool_mixer(pool_u, pool_w, pool_scale)
    q = rotary(q.reshape(B, S, N_HEADS, HEAD_DIM), positions)
    k = rotary(k.reshape(B, S, N_KV_HEADS, HEAD_DIM), positions)
    v = v.reshape(B, S, N_KV_HEADS, HEAD_DIM)
    y_att = sliding_window_attention(q, k, v, sinks)
    branches = jnp.stack([y_conv, y_pool, y_att], axis=2)
    branches = jnp.einsum('bsrc,rcd->bsrd', branches, w_branch)
    gates = jax.nn.sigmoid(gate_logits.reshape(B, S, N_BRANCH, D_MODEL))
    merged = jnp.sum(gates * branches, axis=2)
    return merged @ w_out

def swiglu(h, w_gu, w_down, d_ff):
    gu = h @ w_gu
    return (jax.nn.silu(gu[..., :d_ff]) * gu[..., d_ff:]) @ w_down

def moe_ffn(h, w_router, w_gu, w_down):
    B, S, D = h.shape
    ht = h.reshape(B * S, D)
    logits = (ht @ w_router).astype(jnp.float32)
    top_vals, top_idx = lax.top_k(logits, TOP_K)
    top_w = jax.nn.softmax(top_vals, axis=-1)
    combine = jnp.sum(jax.nn.one_hot(top_idx, N_EXPERTS, dtype=jnp.float32) * top_w[..., None], axis=1)
    out = jnp.zeros((B * S, D), jnp.float32)
    for e in range(N_EXPERTS):
        y = swiglu(ht, w_gu[e], w_down[e], D_FF_EXPERT)
        out = out + combine[:, e:e + 1] * y.astype(jnp.float32)
    return out.astype(h.dtype).reshape(B, S, D)

def setup_inputs(seed: int = 0) -> dict:
    key = jax.random.key(seed)
    ks = jax.random.split(key, 24)

    def nrm(k, shape, scale):
        return jax.random.normal(k, shape, jnp.float32) * scale

    def gain(k, shape):
        return 1.0 + 0.01 * jax.random.normal(k, shape, jnp.float32)

    n_dense = (DEPTH + 1) // 2
    n_moe = DEPTH // 2
    return {
        'x': nrm(ks[0], (BATCH, SEQ, D_MODEL), 1.0),
        'p': nrm(ks[1], (DEPTH, BATCH, SEQ, PLE_DIM), 1.0),
        'positions': jnp.broadcast_to(jnp.arange(SEQ, dtype=jnp.int32), (BATCH, SEQ)),
        'norm_mix_g': gain(ks[2], (DEPTH, D_MODEL)),
        'w_in': nrm(ks[3], (DEPTH, D_MODEL, D_IN), D_MODEL ** -0.5),
        'conv_w': nrm(ks[4], (DEPTH, CONV_K, BRANCH_W), CONV_K ** -0.5),
        'pool_w': nrm(ks[5], (DEPTH, N_POOL_GROUPS, POOL_GROUP_W, POOL_GROUP_W), POOL_GROUP_W ** -0.5),
        'pool_scale': 1.0 + 0.1 * jax.random.normal(ks[6], (DEPTH, BRANCH_W), jnp.float32),
        'attn_sinks': nrm(ks[7], (DEPTH, N_HEADS), 1.0),
        'w_branch': nrm(ks[8], (DEPTH, N_BRANCH, BRANCH_W, D_MODEL), BRANCH_W ** -0.5),
        'w_out': nrm(ks[9], (DEPTH, D_MODEL, D_MODEL), D_MODEL ** -0.5),
        'norm_ffn_g': gain(ks[10], (DEPTH, D_MODEL)),
        'ffn_w_gu': nrm(ks[11], (n_dense, D_MODEL, 2 * D_FF), D_MODEL ** -0.5),
        'ffn_w_down': nrm(ks[12], (n_dense, D_FF, D_MODEL), D_FF ** -0.5),
        'moe_router': nrm(ks[13], (n_moe, D_MODEL, N_EXPERTS), D_MODEL ** -0.5),
        'moe_w_gu': nrm(ks[14], (n_moe, N_EXPERTS, D_MODEL, 2 * D_FF_EXPERT), D_MODEL ** -0.5),
        'moe_w_down': nrm(ks[15], (n_moe, N_EXPERTS, D_FF_EXPERT, D_MODEL), D_FF_EXPERT ** -0.5),
        'norm_ple_g': gain(ks[16], (DEPTH, D_MODEL)),
        'ple_w_proj': nrm(ks[17], (DEPTH, PLE_DIM, D_MODEL), PLE_DIM ** -0.5),
        'ple_w_gate': nrm(ks[18], (DEPTH, D_MODEL, D_MODEL), D_MODEL ** -0.5),
        'final_norm_g': gain(ks[19], (D_MODEL,)),
    }

def reference(x, p, positions, norm_mix_g, w_in, conv_w, pool_w, pool_scale, attn_sinks,
              w_branch, w_out, norm_ffn_g, ffn_w_gu, ffn_w_down, moe_router, moe_w_gu,
              moe_w_down, norm_ple_g, ple_w_proj, ple_w_gate, final_norm_g):
    for i in range(DEPTH):
        h = rms_norm(x, norm_mix_g[i])
        x = x + token_mixing(h, positions, w_in[i], conv_w[i], pool_w[i], pool_scale[i],
                             attn_sinks[i], w_branch[i], w_out[i])
        h = rms_norm(x, norm_ffn_g[i])
        if i % 2 == 0:
            x = x + swiglu(h, ffn_w_gu[i // 2], ffn_w_down[i // 2], D_FF)
        else:
            x = x + moe_ffn(h, moe_router[i // 2], moe_w_gu[i // 2], moe_w_down[i // 2])
        h = rms_norm(x, norm_ple_g[i])
        x = x + jax.nn.sigmoid(h @ ple_w_gate[i]) * (p[i] @ ple_w_proj[i])
    return rms_norm(x, final_norm_g)


_drawn_inputs = setup_inputs


def setup_inputs(seed=0):
    import zlib

    import numpy as np

    out = dict(_drawn_inputs(seed))
    spreads = {}
    factors = {'norm_mix_g': 2.716,
     'attn_sinks': 19.205,
     'norm_ffn_g': 13.046,
     'norm_ple_g': 200.0,
     'final_norm_g': 182.558,
     'p': 3.937,
     'ple_w_proj': 3.944,
     'ple_w_gate': 5.795}
    for name, (base, spread) in spreads.items():
        noise = np.random.default_rng([zlib.crc32(name.encode()), seed]).standard_normal(out[name].shape)
        drawn = base * np.exp(spread * noise) if base else spread * noise
        out[name] = __import__('jax').numpy.asarray(drawn.astype(out[name].dtype))
    for name, factor in factors.items():
        out[name] = (out[name] * factor).astype(out[name].dtype)
    return out
```

```python
from contextlib import ExitStack

import numpy as np

import concourse.bass as bass
from concourse import mybir

F32 = mybir.dt.float32
F32R = mybir.dt.float32r
I32 = mybir.dt.int32
U32 = mybir.dt.uint32
ALU = mybir.AluOpType
ACT = mybir.ActivationFunctionType
AX = mybir.AxisListType

P = 128
D = 1024
SEQ = 256
NB = SEQ // P
KD = D // P
DEPTH = 2
BW = 512
CH = BW // P
HEADS, KV_HEADS, HD = 8, 2, 64
HALF = HD // 2
D_FF = 3584
EXPERTS = 8
D_FFE = 1792
PLE = 256
EPS = 1e-6
NEG = -1e30
OFF_POOL, OFF_Q, OFF_K, OFF_GATE = 1536, 2048, 2560, 2816

RAW, SPLIT = 7, 3
TILE = 2048
BODY_F = 7
BODY_TILES = 3 * BODY_F

T_CHAN = 3
T_GATE = T_CHAN + 8
T_OUT = T_GATE + 18
T_FFN = T_OUT + 4
FFN_BODIES = [D_FF // (256 * BODY_F), EXPERTS]
T_PLE = [T_FFN + BODY_TILES * n for n in FFN_BODIES]
LAYER_T0 = [0, T_PLE[0] + 5]
N_TILES = LAYER_T0[1] + T_PLE[1] + 5


def body_schedule(moe):
    s = []
    for f in range(BODY_F):
        s.append(("tile", "a", f))
        if moe and f == 0:
            s.append(("scatter", "", 0))
        if f:
            s.append(("turn", "", f - 1))
        s.append(("tile", "b", f))
        s.append(("swiglu", "", f))
        if moe and f == 0:
            s.append(("scatter", "", 1))
        if moe and f == 1:
            s.append(("route", "", 0))
        if f:
            s.append(("tile", "d", f - 1))
    if moe:
        s.append(("gather", "", 0))
    s.append(("turn", "", BODY_F - 1))
    s.append(("tile", "d", BODY_F - 1))
    s.append(("close", "", 0))
    return s


def turn_bank(blk, half):
    return (6, 2)[half] + blk


def trunk(nc, x, p, positions, norm_mix_g, w_in, conv_w, pool_w, pool_scale, attn_sinks, w_branch,
          w_out, norm_ffn_g, ffn_w_gu, ffn_w_down, moe_router, moe_w_gu, moe_w_down, norm_ple_g,
          ple_w_proj, ple_w_gate, final_norm_g, inv_freq, out):
    ctx = ExitStack()
    with ctx:
        def sb(name, shape, dt=F32):
            return ctx.enter_context(nc.sbuf_tensor(name, shape, dt))

        def sem(name):
            return ctx.enter_context(nc.semaphore(name))

        raw = sb("raw", [P, RAW, TILE])
        split = sb("split", [P, SPLIT, 2, TILE], F32R)
        X = sb("X", [P, NB, D])
        Y = sb("Y", [P, NB, D])
        M = sb("M", [P, NB, D])
        g_row = sb("g_row", [P, D])
        hT = sb("hT", [P, 2, KD, SEQ], F32R)
        br = sb("br", [P, 6, CH * SEQ], F32R)
        pT = sb("pT", [P, 2, 2, SEQ], F32R)
        upool = sb("upool", [P, CH, 16 + SEQ])
        wsum = sb("wsum", [P, 2, 16 + SEQ])
        kdup = sb("kdup", [P, NB, KV_HEADS, 2, HD])
        v_sb = sb("v_sb", [P, NB, KV_HEADS * HD])
        qT = sb("qT", [P, CH, SEQ])
        kT = sb("kT", [P, KV_HEADS, 2, SEQ])
        sc = sb("sc", [P, 512])
        prT = sb("prT", [P, 4, P])
        sg = sb("sg", [P, NB, 512])
        tmp = sb("tmp", [P, D])
        poolw_sb = sb("poolw_sb", [P, CH, P])
        convw_sb = sb("convw_sb", [P, CH, 3])
        pscale_sb = sb("pscale_sb", [P, CH])
        sinks_sb = sb("sinks_sb", [P, HEADS])
        router_sb = sb("router_sb", [P, KD, EXPERTS])
        ident = sb("ident", [P, P])
        below = sb("below", [P, P])
        ones = sb("ones", [P, P])
        slot_row = sb("slot_row", [P, P])
        mask = sb("mask", [P, SEQ])
        rcount = sb("rcount", [P, 16])
        pos_i = sb("pos_i", [P, NB], I32)
        pos_f = sb("pos_f", [P, NB])
        freq = sb("freq", [P, HALF])
        ang = sb("ang", [P, 2, NB, HALF])
        turns = sb("turns", [P, 2, NB, HALF])
        sin2 = sb("sin2", [P, NB, 2, HALF])
        cos1 = sb("cos1", [P, NB, HALF])
        ms = sb("ms", [P, 4])
        rstd = sb("rstd", [P, 2])
        power = sb("power", [P, 1])
        mx = sb("mx", [P, 4])
        nmx = sb("nmx", [P, 4])
        den = sb("den", [P, 4])
        esk = sb("esk", [P, 4])
        rden = sb("rden", [P, 4])
        logit = sb("logit", [P, NB, EXPERTS])
        top = sb("top", [P, NB, 8])
        topi = sb("topi", [P, NB, 8], U32)
        topf = sb("topf", [P, NB, 8])
        hot = sb("hot", [P, NB, 2, EXPERTS])
        wts = sb("wts", [P, NB, 4])
        comb = sb("comb", [P, NB, 2 * EXPERTS])
        sel = sb("sel", [P, NB, EXPERTS])
        rank = sb("rank", [P, NB, 2 * EXPERTS + 1])
        load = sb("load", [P, EXPERTS])
        most = sb("most", [P, 2])
        more_i = sb("more_i", [P, 1], I32)
        G = sb("G", [P, NB, P], F32R)
        GT = sb("GT", [P, SEQ], F32R)
        w_slot = sb("w_slot", [P, 1])

        q_rot = Y[:, 0, :].rearrange("p (b n) -> p b n", b=NB)
        c_sb = Y[:, 1, :].rearrange("p (c n) -> p c n", c=CH)
        pooled = c_sb
        vpad = M[:, 0:2, :].rearrange("p b n -> p (b n)")[:, 0:CH * (SEQ + 2)].rearrange(
            "p (c n) -> p c n", c=CH)
        cacc = M[:, 0:2, :].rearrange("p b n -> p (b n)")[:, 1536:2048].rearrange(
            "p (c n) -> p c n", c=2)
        ctmp = tmp[:, 0:512].rearrange("p (c n) -> p c n", c=2)
        brv = br[:, :, :].rearrange("p r (c n) -> p r c n", c=CH)
        yn = br[:, 0:4, :].rearrange("p (s b) n -> p s b n", s=2)
        xe = br[:, 4:6, :].rearrange("p s (k n) -> p s k n", k=KD)
        hTf = hT[:, :, :, :].rearrange("p s k n -> p (s k n)")
        ye = hTf[:, 0:2 * D].rearrange("p (s n) -> p s n", s=2)
        aT_moe = hTf[:, 2 * D:2 * D + 1024].rearrange("p (u s k n) -> p u s k n", u=2, s=2, k=2)
        brf = br[:, :, :].rearrange("p r n -> p (r n)")
        aT_dense = brf[:, 0:2048].rearrange("p (u s k n) -> p u s k n", u=2, s=2, k=2)

        ps = ctx.enter_context(nc.psum_tensor("ps", [P, 8, 512], F32))

        landed = [sem(f"landed{i}") for i in range(RAW)]
        hi_ready, lo_ready, tile_used = sem("hi_ready"), sem("lo_ready"), sem("tile_used")
        consts = sem("consts")
        cstep = sem("cstep")
        x_in, pos_in, small_in, g_in = sem("x_in"), sem("pos_in"), sem("small_in"), sem("g_in")
        p_in = sem("p_in")
        dve_step, act_step = sem("dve_step"), sem("act_step")
        rope_ang, rope_ready = sem("rope_ang"), sem("rope_ready")
        ms_ready, rstd_ready, y_ready = sem("ms_ready"), sem("rstd_ready"), sem("y_ready")
        turned, hT_hi, hT_lo = sem("turned"), sem("hT_hi"), sem("hT_lo")
        p_turned, pT_hi, pT_lo = sem("p_turned"), sem("pT_hi"), sem("pT_lo")
        q_done, kv_done, rot_ready, v_ready = sem("q_done"), sem("kv_done"), sem("rot_ready"), sem("v_ready")
        chan_out = sem("chan_out")
        c_copied = sem("c_copied")
        conv_y, conv_hi, conv_lo = sem("conv_y"), sem("conv_hi"), sem("conv_lo")
        pooled_ready, mixed_done = sem("pooled_ready"), sem("mixed_done")
        pool_hi, pool_lo = sem("pool_hi"), sem("pool_lo")
        qk_turned, qT_ready, kT_ready = sem("qk_turned"), sem("qT_ready"), sem("kT_ready")
        s_done, masked, exped, probs, pr_turned, prT_ready = (
            sem("s_done"), sem("masked"), sem("exped"), sem("probs"), sem("pr_turned"), sem("prT_ready"))
        att_done, att_hi, att_lo = sem("att_done"), sem("att_hi"), sem("att_lo")
        gate_done, sig_ready, branch_done, merged = (
            sem("gate_done"), sem("sig_ready"), sem("branch_done"), sem("merged"))
        out_done, x_out = sem("out_done"), sem("x_out")
        proj_done, proj_out = sem("proj_done"), sem("proj_out")
        pg_done, psig, x_ple = sem("pg_done"), sem("psig"), sem("x_ple")
        gu_done, down_done = sem("gu_done"), sem("down_done")
        silu_ready = [sem(f"silu_ready{i}") for i in range(3)]
        act_ready = [sem(f"act_ready{i}") for i in range(3)]
        a_turned = [sem(f"a_turned{i}") for i in range(3)]
        aT_hi = [sem(f"aT_hi{i}") for i in range(3)]
        aT_lo = [sem(f"aT_lo{i}") for i in range(3)]
        x_ffn = [sem(f"x_ffn{i}") for i in range(3)]
        logit_done, route_step, sel_ready, rank_done = (
            sem("logit_done"), sem("route_step"), sem("sel_ready"), sem("rank_done"))
        routed, yn_hi, yn_lo = sem("routed"), sem("yn_hi"), sem("yn_lo")
        g_ready = [None] + [sem(f"g_ready{i}") for i in (1, 2)]
        route_done = [None] + [sem(f"route_done{i}") for i in (1, 2)]
        gT_ready = [None] + [sem(f"gT_ready{i}") for i in (1, 2)]
        ws_ready = [None] + [sem(f"ws_ready{i}") for i in (1, 2)]
        gathered = [None] + [sem(f"gathered{i}") for i in (1, 2)]
        xe_hi = [None] + [sem(f"xe_hi{i}") for i in (1, 2)]
        xe_lo = [None] + [sem(f"xe_lo{i}") for i in (1, 2)]
        ye_hi = [None] + [sem(f"ye_hi{i}") for i in (1, 2)]
        ye_lo = [None] + [sem(f"ye_lo{i}") for i in (1, 2)]
        scattered = [None] + [sem(f"scattered{i}") for i in (1, 2)]
        landed2 = [sem(f"landed2_{i}") for i in range(RAW)]
        hi_ready2, lo_ready2, tile_used2 = sem("hi_ready2"), sem("lo_ready2"), sem("tile_used2")
        stored = sem("stored")

        STREAMS = {1: (landed, hi_ready, lo_ready, tile_used),
                   2: (landed2, hi_ready2, lo_ready2, tile_used2)}

        def slot(t, s, n):
            return split[:, t % SPLIT, s, :].rearrange("p (k n) -> p k n", n=n)

        def raw_slot(t, n):
            return raw[:, t % RAW, :].rearrange("p (k n) -> p k n", n=n)

        def wait_product(eng, b, last, signal, n, t, i=0, per=0, stream=1):
            if b == last:
                eng.wait_ge(STREAMS[stream][3], t + 1 + i * per)
            else:
                eng.wait_ge(signal, n)

        block = ctx.enter_context(nc.Block())

        @block.sync
        def _(sp):
            def fetch(t, parts, i=0, per=0, stream=1):
                land, _, lo, _ = STREAMS[stream]
                if t >= RAW:
                    sp.wait_ge(lo, t - RAW + 1 + i * per)
                for dst, src in parts:
                    sp.dma_start(dst, src).then_inc(land[t % RAW], 32 // len(parts))

            def rows(w, k0, nk, c0, n):
                return w[k0 * P:(k0 + nk) * P, c0:c0 + n].rearrange("(k p) n -> p k n", p=P)

            def ffn(stream, t0, w_gu, w_down, d_ff, f0, i=0):
                j = 0
                for step, kind, f in body_schedule(False):
                    if step != "tile":
                        continue
                    t = t0 + j
                    if kind == "d":
                        src = w_down[bass.ds((f0 + f) * 256, 256), :].rearrange("(k p) n -> p k n", p=P)
                        fetch(t, [(raw_slot(t, D), src)], i, BODY_TILES, stream)
                    else:
                        k0 = 0 if kind == "a" else 4
                        parts = []
                        for s in range(2):
                            src = w_gu[k0 * P:(k0 + 4) * P, bass.ds(s * d_ff + (f0 + f) * 256, 256)]
                            parts.append((raw_slot(t, 512)[:, :, s * 256:(s + 1) * 256],
                                          src.rearrange("(k p) n -> p k n", p=P)))
                        fetch(t, parts, i, BODY_TILES, stream)
                    j += 1

            def experts(stream, t0):
                with sp.Fori(0, EXPERTS) as e:
                    gu = moe_w_gu[0, bass.ds(e, 1)].rearrange("e k n -> (e k) n")
                    dn = moe_w_down[0, bass.ds(e, 1)].rearrange("e k n -> (e k) n")
                    ffn(stream, t0, gu, dn, D_FFE, 0, e)

            for l in range(DEPTH):
                t = LAYER_T0[l]
                w = w_in[l]
                for i in range(2):
                    fetch(t + i, [(raw_slot(t + i, 512), rows(w, 4 * i, 4, OFF_Q, 512))])
                fetch(t + 2, [(raw_slot(t + 2, 256), rows(w, 0, KD, OFF_K, 256))])
                for j, c0 in enumerate((512, 768, 1024, 1280, 0, 256, OFF_POOL, OFF_POOL + 256)):
                    u = t + T_CHAN + j
                    fetch(u, [(raw_slot(u, 256), rows(w, 0, KD, c0, 256))])
                for r in range(3):
                    for nh in range(2):
                        u = t + T_GATE + 3 * (2 * r + nh)
                        for i in range(2):
                            fetch(u + i, [(raw_slot(u + i, 512),
                                           rows(w, 4 * i, 4, OFF_GATE + r * D + nh * 512, 512))])
                        fetch(u + 2, [(raw_slot(u + 2, 512), rows(w_branch[l, r], 0, CH, nh * 512, 512))])
                for i in range(4):
                    fetch(t + T_OUT + i, [(raw_slot(t + T_OUT + i, D), rows(w_out[l], 2 * i, 2, 0, D))])
                if l == 0:
                    with sp.Fori(0, FFN_BODIES[0]) as i:
                        ffn(1, t + T_FFN, ffn_w_gu[0], ffn_w_down[0], D_FF, i * BODY_F, i)
                else:
                    experts(1, t + T_FFN)
                    sp.wait_ge(routed, 1)
                    more = sp.value_load(more_i[0:1, 0:1], min_val=0, max_val=1)
                    with sp.If(more > 0):
                        sp.wait_ge(lo_ready, t + T_PLE[1])
                        for land in landed2:
                            sp.sem_inc(land, 32 * (BODY_TILES // RAW))
                        experts(2, BODY_TILES)
                        sp.wait_ge(lo_ready2, (EXPERTS + 1) * BODY_TILES)
                u = t + T_PLE[l]
                fetch(u, [(raw_slot(u, D), rows(ple_w_proj[l], 0, 2, 0, D))])
                for i in range(4):
                    fetch(u + 1 + i, [(raw_slot(u + 1 + i, D), rows(ple_w_gate[l], 2 * i, 2, 0, D))])
            for b in range(NB):
                sp.wait_ge(y_ready, 6 * NB + b + 1)
                sp.dma_start(out[0, b * P:(b + 1) * P, :], Y[:, b, :]).then_inc(stored, 16)
            sp.wait_ge(stored, 16 * NB)

        gains = [norm_mix_g[0:1, :], norm_ffn_g[0:1, :], norm_ple_g[0:1, :],
                 norm_mix_g[1:2, :], norm_ffn_g[1:2, :], norm_ple_g[1:2, :],
                 final_norm_g.rearrange("(a n) -> a n", a=1)]

        def on_all(row):
            return row.broadcast_to([P, row.shape[-1]])

        @block.gpsimd
        def _(pool):
            pool.dma_start(X[:, :, :], x[0].rearrange("(b p) n -> p b n", p=P)).then_inc(x_in, 16)
            pool.dma_start(g_row[:, :], on_all(gains[0])).then_inc(g_in, 16)
            pool.dma_start(pos_i[:, :], positions[0].rearrange("(b p) -> p b", p=P),
                           allow_slow_non_contiguous=True).then_inc(pos_in, 16)
            pool.dma_start(freq[:, :], on_all(inv_freq)).then_inc(pos_in, 16)
            pool.dma_start(router_sb[:, :, :],
                           moe_router[0].rearrange("(k p) e -> p k e", p=P)).then_inc(small_in, 16)
            pool.memset(power[:, :], -0.5).then_inc(consts, 1)
            pool.memset(ident[:, :], 0.0).then_inc(cstep, 1)
            pool.memset(below[:, :], 1.0).then_inc(cstep, 1)
            pool.memset(mask[:, :], 0.0).then_inc(cstep, 1)
            pool.memset(ones[:, :], 1.0).then_inc(consts, 1)
            pool.memset(upool[:, :, 0:16], 0.0).then_inc(consts, 1)
            pool.memset(wsum[:, :, 0:16], 0.0).then_inc(consts, 1)
            pool.memset(kT[:, :, :, :], 0.0).then_inc(consts, 1)
            pool.iota(slot_row[:, :], pattern=[[1, P]], base=0, channel_multiplier=0,
                      allow_small_or_imprecise_dtypes=True).then_inc(consts, 1)
            pool.wait_ge(cstep, 3)
            pool.affine_select(out=ident[:, :], in_=ident[:, :], compare_op=ALU.not_equal, fill=1.0,
                               base=0, pattern=[[-1, P]], channel_multiplier=1).then_inc(consts, 1)
            pool.affine_select(out=below[:, :], in_=below[:, :], compare_op=ALU.is_gt, fill=0.0,
                               base=0, pattern=[[1, P]], channel_multiplier=-1).then_inc(consts, 1)
            pool.affine_select(out=mask[:, :], in_=mask[:, :], compare_op=ALU.is_gt, fill=NEG,
                               base=0, pattern=[[1, SEQ]], channel_multiplier=-1).then_inc(cstep, 1)
            pool.wait_ge(cstep, 4)
            pool.affine_select(out=mask[:, :], in_=mask[:, :], compare_op=ALU.is_ge, fill=NEG,
                               base=P, pattern=[[-1, SEQ]], channel_multiplier=1).then_inc(consts, 1)
            pool.wait_ge(consts, 9)

            def layer_loads(l):
                if l:
                    pool.wait_ge(mixed_done, l)
                    pool.wait_ge(pool_lo, 2 * l)
                    pool.wait_ge(conv_lo, 2 * l)
                    pool.wait_ge(probs, 6 * l)
                pool.dma_start(poolw_sb[:, :, :], pool_w[l].rearrange("g c d -> c g d")).then_inc(small_in, 16)
                for k in range(3):
                    pool.dma_start(convw_sb[:, :, k], conv_w[l, k].rearrange("(c p) -> p c", p=P),
                                   allow_slow_non_contiguous=True
                                   ).then_inc(small_in, 16)
                pool.dma_start(pscale_sb[:, :], pool_scale[l].rearrange("(c p) -> p c", p=P),
                               allow_slow_non_contiguous=True
                               ).then_inc(small_in, 16)
                pool.dma_start(sinks_sb[:, :], on_all(attn_sinks[l:l + 1, :])).then_inc(small_in, 16)

            def load_p(l):
                if l:
                    pool.wait_ge(x_ple, NB)
                pool.dma_start(tmp[:, 0:2 * PLE].rearrange("p (b n) -> p b n", b=NB),
                               p[l, 0].rearrange("(b p) n -> p b n", p=P)).then_inc(p_in, 16)

            def rms(n):
                for b in range(NB):
                    pool.wait_ge(ms_ready, NB * n + b + 1)
                    pool.tensor_tensor(rstd[:, b:b + 1], ms[:, 2 + b:3 + b], power[:, :], ALU.pow
                                       ).then_inc(rstd_ready, 1)
                if n + 1 < len(gains):
                    pool.wait_ge(y_ready, NB * (n + 1))
                    pool.dma_start(g_row[:, :], on_all(gains[n + 1])).then_inc(g_in, 16)

            load_p(0)
            layer_loads(0)
            for l in range(DEPTH):
                for n in range(3):
                    rms(3 * l + n)
                    if l == 0 and n == 1:
                        layer_loads(1)
                if l == 0:
                    load_p(1)
            rms(6)

        @block.scalar
        def _(act):
            done = [0]

            def chain(ins):
                done[0] += 1
                ins.then_inc(act_step, 1)
                act.wait_ge(act_step, done[0])

            def split_hi(t, i=0, per=0, stream=1):
                land, hi, _, used = STREAMS[stream]
                visits = BODY_TILES // RAW if per else 0
                act.wait_ge(land[t % RAW], 32 * (t // RAW + 1) + i * (32 * visits))
                if t >= SPLIT:
                    act.wait_ge(used, t - SPLIT + 1 + i * per)
                act.activation(split[:, t % SPLIT, 0, :], raw[:, t % RAW, :], ACT.Copy).then_inc(hi, 1)

            def turn_hi(n):
                for half in range(2):
                    for b in range(NB):
                        k = 4 * n + 2 * half + b
                        act.wait_ge(turned, k + 1)
                        act.activation(hT[:, 0, 4 * half:4 * half + 4, b * P:(b + 1) * P],
                                       ps[:, turn_bank(b, half), :].rearrange("p (k n) -> p k n", k=4),
                                       ACT.Copy).then_inc(hT_hi, 1)

            def softmax_exp(l, u):
                nh, n = (4, P) if u < 2 else (2, SEQ)
                h0 = 4 * u if u < 2 else 2 * (u - 2)
                act.wait_ge(masked, 6 * l + u + 1)
                for h in range(nh):
                    act.activation(sc[:, h * n:(h + 1) * n], sc[:, h * n:(h + 1) * n], ACT.Exp,
                                   bias=nmx[:, h:h + 1], accum_out=den[:, h:h + 1])
                    ins = act.activation(esk[:, h:h + 1], sinks_sb[:, h0 + h:h0 + h + 1], ACT.Exp,
                                         bias=nmx[:, h:h + 1])
                ins.then_inc(exped, 1)

            def body(s, nb, moe, t0, i, last_split):
                stream = 2 if s == 2 else 1
                aT = aT_moe if moe else aT_dense
                j = 0
                for step, kind, f in body_schedule(moe):
                    if step == "tile":
                        if j + 2 < BODY_TILES + last_split:
                            split_hi(t0 + j + 2, i, BODY_TILES, stream)
                        j += 1
                    elif step == "swiglu":
                        for b in range(nb):
                            wait_product(act, b, nb - 1, gu_done, f + 1 + i * BODY_F, t0 + j - 1, i,
                                         BODY_TILES, stream)
                            bank = 4 + (f % 2 if moe else b)
                            act.activation(sg[:, b, 0:256], ps[:, bank, 0:256], ACT.Silu
                                           ).then_inc(silu_ready[s], 1)
                    elif step == "turn":
                        act.wait_ge(a_turned[s], f + 1 + i * BODY_F)
                        act.activation(aT[:, f % 2, 0], ps[:, 6 + f % 2, 0:nb * SEQ].rearrange(
                            "p (k n) -> p k n", k=2), ACT.Copy).then_inc(aT_hi[s], 1)
                    elif step == "route":
                        act.wait_ge(route_done[s], 1 + i)
                        act.activation(GT[:, :], ps[:, 2, 0:SEQ], ACT.Copy).then_inc(gT_ready[s], 1)
                    elif step == "gather":
                        gather_hi(s, 2 + i * 2)
                    elif step == "close" and moe:
                        act.wait_ge(STREAMS[stream][3], t0 + BODY_TILES + i * BODY_TILES)
                        act.wait_ge(ws_ready[s], 1 + i)
                        for nh in range(2):
                            act.activation(ye[:, 0, nh * 512:(nh + 1) * 512], ps[:, nh, :], ACT.Copy,
                                           scale=w_slot[:, 0:1]).then_inc(ye_hi[s], 1)

            def gather_hi(s, n):
                for half in range(2):
                    act.wait_ge(gathered[s], n + half + 1)
                    act.activation(xe[:, 0, 4 * half:4 * half + 4, :],
                                   ps[:, 2 + half, :].rearrange("p (k n) -> p k n", k=4), ACT.Copy
                                   ).then_inc(xe_hi[s], 1)

            def experts(s, t0):
                gather_hi(s, 0)
                if s == 2:
                    act.wait_ge(tile_used, LAYER_T0[1] + T_PLE[1])
                    act.sem_inc(hi_ready2, BODY_TILES)
                    for t in range(2):
                        split_hi(BODY_TILES + t, stream=2)
                with act.Fori(0, EXPERTS - 1) as e:
                    body(s, 1, True, t0, e, 2)
                body(s, 1, True, t0, EXPERTS - 1, 0)

            act.wait_ge(rope_ang, 1)
            act.activation(sin2[:, :, 1, :], ang[:, 0], ACT.Sin).then_inc(rope_ready, 1)
            act.activation(sin2[:, :, 0, :], ang[:, 0], ACT.Sin, scale=-1.0).then_inc(rope_ready, 1)
            act.activation(cos1[:, :, :], ang[:, 1], ACT.Sin).then_inc(rope_ready, 1)
            split_hi(0)
            split_hi(1)
            for l in range(DEPTH):
                t0 = LAYER_T0[l]
                act.wait_ge(p_turned, l + 1)
                act.activation(pT[:, 0], ps[:, 5, :].rearrange("p (k n) -> p k n", k=2), ACT.Copy
                               ).then_inc(pT_hi, 1)
                turn_hi(4 * l)
                for j in range(T_CHAN):
                    split_hi(t0 + j + 2)
                for b in range(NB):
                    wait_product(act, b, NB - 1, kv_done, l + 1, t0 + 2)
                    act.activation(v_sb[:, b, :], ps[:, b, P:2 * P], ACT.Copy).then_inc(v_ready, 1)
                for j in range(8):
                    split_hi(t0 + T_CHAN + j + 2)
                    if j < 2:
                        act.wait_ge(tile_used, t0 + T_CHAN + j + 1)
                        act.activation(c_sb[:, 2 * j:2 * j + 2, :],
                                       ps[:, 2 + j, :].rearrange("p (c n) -> p c n", c=2), ACT.Copy
                                       ).then_inc(c_copied, 1)
                    if j in (4, 5):
                        act.wait_ge(conv_y, 2 * l + j - 3)
                        act.activation(brv[:, 0, 2 * (j - 4):2 * (j - 4) + 2, :], ctmp, ACT.Copy
                                       ).then_inc(conv_hi, 1)
                    if j == 5:
                        act.wait_ge(qk_turned, 3 * l + 3)
                        for c in range(2):
                            act.activation(qT[:, 2 * c:2 * c + 2, :],
                                           ps[:, 6 + c, :].rearrange("p (c n) -> p c n", c=2), ACT.Copy
                                           ).then_inc(qT_ready, 1)
                    if j in (6, 7):
                        act.wait_ge(tile_used, t0 + T_CHAN + j + 1)
                        act.activation(upool[:, 2 * (j - 6):2 * (j - 6) + 2, 16:],
                                       ps[:, j - 2, :].rearrange("p (c n) -> p c n", c=2), ACT.Copy
                                       ).then_inc(chan_out, 1)
                for c in range(6):
                    for step in range(3):
                        split_hi(t0 + T_GATE + 3 * c + step + 2)
                        at = 3 * c + step
                        if at == 0:
                            act.wait_ge(mixed_done, l + 1)
                            for g in range(CH):
                                ins = act.activation(
                                    brv[:, 2, g, :], ps[:, 2 + g // 2, g % 2 * SEQ:(g % 2 + 1) * SEQ],
                                    ACT.Copy, scale=pscale_sb[:, g:g + 1])
                            ins.then_inc(pool_hi, 1)
                        if step == 1:
                            for b in range(NB):
                                wait_product(act, b, NB - 1, gate_done, 6 * l + c + 1,
                                             t0 + T_GATE + 3 * c + 1)
                                if NB * c + b >= NB:
                                    act.wait_ge(merged, 12 * l + NB * (c - 1) + b + 1)
                                act.activation(sg[:, b, :], ps[:, 4 + b, :], ACT.Sigmoid
                                               ).then_inc(sig_ready, 1)
                        if 1 <= at <= 6:
                            softmax_exp(l, at - 1)
                        if at == 8:
                            act.wait_ge(att_done, l + 1)
                            for h in range(2):
                                act.activation(brv[:, 4, 2 * h:2 * h + 2, :],
                                               ps[:, 2 + h, :].rearrange("p (c n) -> p c n", c=2), ACT.Copy
                                               ).then_inc(att_hi, 1)
                turn_hi(4 * l + 1)
                for i in range(4):
                    split_hi(t0 + T_OUT + i + 2)
                turn_hi(4 * l + 2)
                if l == 0:
                    with act.Fori(0, FFN_BODIES[0]) as i:
                        body(0, NB, False, t0 + T_FFN, i, 2)
                else:
                    act.wait_ge(y_ready, NB * 5)
                    act.activation(yn[:, 0], Y[:, :, :], ACT.Copy).then_inc(yn_hi, 1)
                    for b in range(NB):
                        act.wait_ge(sel_ready, b + 1)
                        act.activation(wts[:, b, 1:2], wts[:, b, 0:1], ACT.Exp).then_inc(route_step, 1)
                    experts(1, t0 + T_FFN)
                    act.wait_ge(routed, 1)
                    more = act.value_load(more_i[0:1, 0:1], min_val=0, max_val=1)
                    with act.If(more > 0):
                        experts(2, BODY_TILES)
                        act.wait_ge(tile_used2, (EXPERTS + 1) * BODY_TILES)
                u = t0 + T_PLE[l]
                if l:
                    split_hi(u)
                    split_hi(u + 1)
                split_hi(u + 2)
                for b in range(NB):
                    wait_product(act, b, NB - 1, proj_done, l + 1, u)
                    act.activation(M[:, b, :].rearrange("p (h n) -> p h n", h=2), ps[:, 4 * b:4 * b + 2, :],
                                   ACT.Copy).then_inc(proj_out, 1)
                turn_hi(4 * l + 3)
                for i in range(4):
                    if u + 3 + i < N_TILES:
                        split_hi(u + 3 + i)
                for b in range(NB):
                    wait_product(act, b, NB - 1, pg_done, l + 1, u + 4)
                    if b:
                        act.wait_ge(x_ple, NB * l + b)
                    act.activation(sg[:, :, :], ps[:, 2 * b:2 * b + 2, :], ACT.Sigmoid).then_inc(psig, 1)

        @block.vector
        def _(dve):
            done = [0]

            def chain(ins):
                done[0] += 1
                ins.then_inc(dve_step, 1)
                dve.wait_ge(dve_step, done[0])

            def split_lo(t, i=0, per=0, stream=1):
                _, hi, lo, _ = STREAMS[stream]
                dve.wait_ge(hi, t + 1 + i * per)
                dve.tensor_tensor(split[:, t % SPLIT, 1, :], raw[:, t % RAW, :],
                                  split[:, t % SPLIT, 0, :].bitcast(F32), ALU.subtract).then_inc(lo, 1)

            def norm(n):
                for b in range(NB):
                    chain(dve.tensor_tensor_reduce(Y[:, b, :], X[:, b, :], X[:, b, :], 1.0, 0.0, ALU.mult,
                                                   ALU.add, ms[:, b:b + 1]))
                    dve.tensor_scalar(ms[:, 2 + b:3 + b], ms[:, b:b + 1], 1.0 / D, EPS, ALU.mult, ALU.add
                                      ).then_inc(ms_ready, 1)
                dve.wait_ge(g_in, 16 * (n + 1))
                for b in range(NB):
                    dve.wait_ge(rstd_ready, NB * n + b + 1)
                    dve.scalar_tensor_tensor(out=Y[:, b, :], in0=X[:, b, :], scalar=rstd[:, b:b + 1],
                                             in1=g_row[:, :], op0=ALU.mult, op1=ALU.mult
                                             ).then_inc(y_ready, 1)

            def turn_lo(n):
                for half in range(2):
                    for b in range(NB):
                        k = 4 * n + 2 * half + b
                        dve.wait_ge(hT_hi, k + 1)
                        ks = slice(4 * half, 4 * half + 4)
                        dve.tensor_tensor(hT[:, 1, ks, b * P:(b + 1) * P],
                                          ps[:, turn_bank(b, half), :].rearrange("p (k n) -> p k n", k=4),
                                          hT[:, 0, ks, b * P:(b + 1) * P].bitcast(F32), ALU.subtract
                                          ).then_inc(hT_lo, 1)

            def two_banks(b0):
                return ps[:, b0:b0 + 2, :]

            def halves(a):
                return a.rearrange("p (h n) -> p h n", h=2)

            def add_to_x(b, b0, signal):
                dve.tensor_tensor(halves(X[:, b, :]), two_banks(b0), halves(X[:, b, :]), ALU.add
                                  ).then_inc(signal, 1)

            def rotate(src, dst, nh, b, nth):
                if nth:
                    dve.wait_ge(rot_ready, nth)
                s4 = src.rearrange("p (h s d) -> p h s d", h=nh, s=2)
                n = nh * HD
                t1 = tmp[:, 0:n].rearrange("p (h s d) -> p h s d", h=nh, s=2)
                t2 = tmp[:, 512:512 + n].rearrange("p (h s d) -> p h s d", h=nh, s=2)
                for s in range(2):
                    cosb = cos1[:, b, :].unsqueeze(1).broadcast_to([P, nh, HALF])
                    sinb = sin2[:, b, s, :].unsqueeze(1).broadcast_to([P, nh, HALF])
                    dve.tensor_tensor(t1[:, :, s, :], s4[:, :, s, :], cosb, ALU.mult)
                    ins = dve.tensor_tensor(t2[:, :, s, :], s4[:, :, 1 - s, :], sinb, ALU.mult)
                chain(ins)
                for d in dst:
                    ins = dve.tensor_tensor(d, t1.rearrange("p h s d -> p h (s d)"),
                                            t2.rearrange("p h s d -> p h (s d)"), ALU.add)
                ins.then_inc(rot_ready, 1)

            def mask_scores(l, u):
                nh, n = (4, P) if u < 2 else (2, SEQ)
                h0 = 4 * u if u < 2 else 2 * (u - 2)
                dve.wait_ge(s_done, 6 * l + u + 1)
                s3 = sc[:, :].rearrange("p (h n) -> p h n", h=nh)
                for h in range(nh):
                    ins = dve.scalar_tensor_tensor(out=s3[:, h, :], in0=ps[:, 6, h * n:(h + 1) * n],
                                                   scalar=HD ** -0.5, in1=mask[:, SEQ - n:SEQ],
                                                   op0=ALU.mult, op1=ALU.add)
                chain(ins)
                chain(dve.tensor_reduce(mx[:, 0:nh], s3, AX.X, ALU.max))
                chain(dve.tensor_tensor(mx[:, 0:nh], mx[:, 0:nh], sinks_sb[:, h0:h0 + nh], ALU.max))
                dve.tensor_scalar(nmx[:, 0:nh], mx[:, 0:nh], -1.0, None, ALU.mult).then_inc(masked, 1)

            def scale_probs(l, u):
                nh = 4 if u < 2 else 2
                dve.wait_ge(exped, 6 * l + u + 1)
                chain(dve.tensor_tensor(rden[:, 0:nh], den[:, 0:nh], esk[:, 0:nh], ALU.add))
                chain(dve.reciprocal(rden[:, 0:nh], rden[:, 0:nh]))
                s3 = sc[:, :].rearrange("p (h n) -> p h n", h=nh)
                for h in range(nh):
                    ins = dve.tensor_scalar(s3[:, h, :], s3[:, h, :], rden[:, h:h + 1], None, ALU.mult)
                ins.then_inc(probs, 1)

            def build_g(s, col, signal):
                for b in range(NB):
                    ins = dve.tensor_scalar(G[:, b, :], slot_row[:, :], rank[:, b, bass.ds(col, 1)], None,
                                            ALU.is_equal)
                ins.then_inc(signal, 1)

            def gather_lo(s, n):
                for half in range(2):
                    dve.wait_ge(xe_hi[s], n + half + 1)
                    ks = slice(4 * half, 4 * half + 4)
                    dve.tensor_tensor(xe[:, 1, ks, :], ps[:, 2 + half, :].rearrange("p (k n) -> p k n", k=4),
                                      xe[:, 0, ks, :].bitcast(F32), ALU.subtract).then_inc(xe_lo[s], 1)

            def body(s, nb, moe, t0, i, last_split):
                stream = 2 if s == 2 else 1
                aT = aT_moe if moe else aT_dense
                j = 0
                for step, kind, f in body_schedule(moe):
                    if step == "tile":
                        if j + 2 < BODY_TILES + last_split:
                            split_lo(t0 + j + 2, i, BODY_TILES, stream)
                        j += 1
                    elif step == "swiglu":
                        for b in range(nb):
                            dve.wait_ge(silu_ready[s], nb * f + b + 1 + i * (nb * BODY_F))
                            bank = 4 + (f % 2 if moe else b)
                            dve.tensor_tensor(tmp[:, b * 256:(b + 1) * 256], ps[:, bank, 256:512],
                                              sg[:, b, 0:256], ALU.mult).then_inc(act_ready[s], 1)
                    elif step == "turn":
                        dve.wait_ge(aT_hi[s], f + 1 + i * BODY_F)
                        dve.tensor_tensor(aT[:, f % 2, 1], ps[:, 6 + f % 2, 0:nb * SEQ].rearrange(
                            "p (k n) -> p k n", k=2), aT[:, f % 2, 0].bitcast(F32), ALU.subtract
                            ).then_inc(aT_lo[s], 1)
                    elif step == "scatter":
                        dve.wait_ge(scattered[s], f + 1 + i * NB)
                        add_to_x(f, 2, x_ffn[s])
                    elif step == "route":
                        dve.wait_ge(gT_ready[s], 2 + i)
                        dve.tensor_copy(w_slot[:, :], ps[:, 2, SEQ:SEQ + 1]).then_inc(ws_ready[s], 1)
                        build_g(s, i + 1 + (EXPERTS if s == 2 else 0), g_ready[s])
                    elif step == "gather":
                        gather_lo(s, 2 + i * 2)
                    elif step == "close" and moe:
                        for nh in range(2):
                            dve.wait_ge(ye_hi[s], nh + 1 + i * 2)
                            cols = slice(nh * 512, (nh + 1) * 512)
                            dve.scalar_tensor_tensor(out=ye[:, 1, cols], in0=ps[:, nh, :],
                                                     scalar=w_slot[:, 0:1], in1=ye[:, 0, cols].bitcast(F32),
                                                     op0=ALU.mult, op1=ALU.subtract).then_inc(ye_lo[s], 1)
                    elif step == "close":
                        for b in range(nb):
                            wait_product(dve, b, nb - 1, down_done, 1 + i, t0 + BODY_TILES - 1, i, BODY_TILES)
                            add_to_x(b, 2 * b, x_ffn[s])

            def experts(s, t0):
                dve.sem_inc(x_ffn[s], 1)
                dve.memset(ye[:, :, :].bitcast(U32), 0).then_inc(ye_lo[s], 2)
                dve.memset(GT[:, :].bitcast(U32), 0).then_inc(gT_ready[s], 1)
                build_g(s, 0 if s == 1 else EXPERTS, g_ready[s])
                gather_lo(s, 0)
                if s == 2:
                    dve.sem_inc(lo_ready2, BODY_TILES)
                    for t in range(2):
                        split_lo(BODY_TILES + t, stream=2)
                with dve.Fori(0, EXPERTS - 1) as e:
                    body(s, 1, True, t0, e, 2)
                body(s, 1, True, t0, EXPERTS - 1, 0)
                for b in range(NB):
                    dve.wait_ge(scattered[s], EXPERTS * NB + b + 1)
                    add_to_x(b, 2, x_ffn[s])

            PI = float(np.pi)

            def parts(value, bits, count):
                got = []
                for _ in range(count):
                    e = int(np.floor(np.log2(abs(value))))
                    q = 2.0 ** (e - bits + 1)
                    got.append(float(np.floor(value / q) * q))
                    value -= got[-1]
                return got

            dve.wait_ge(pos_in, 32)
            chain(dve.tensor_copy(pos_f[:, :], pos_i[:, :]))
            for b in range(NB):
                ins = dve.tensor_scalar(ang[:, 0, b, :], freq[:, :], pos_f[:, b:b + 1], None, ALU.mult)
            chain(ins)
            for period, bits, count in ((4096 * 2 * PI, 7, 6), (2 * PI, 11, 4)):
                chain(dve.tensor_scalar(turns[:, 0], ang[:, 0], 1.0 / period, 12582912.0, ALU.mult, ALU.add))
                chain(dve.tensor_scalar(turns[:, 0], turns[:, 0], -12582912.0, None, ALU.add))
                for part in parts(period, bits, count):
                    chain(dve.scalar_tensor_tensor(out=ang[:, 0], in0=turns[:, 0], scalar=-part, in1=ang[:, 0],
                                                   op0=ALU.mult, op1=ALU.add))
            chain(dve.tensor_scalar(ang[:, 1], ang[:, 0], PI / 2, None, ALU.add))
            chain(dve.tensor_scalar(turns[:, 1], ang[:, 1], PI, -2 * PI, ALU.is_gt, ALU.mult))
            chain(dve.tensor_tensor(ang[:, 1], ang[:, 1], turns[:, 1], ALU.add))
            dve.tensor_scalar(ang[:, :, :, :], ang[:, :, :, :], 3.1415925, -3.1415925, ALU.min, ALU.max
                              ).then_inc(rope_ang, 1)
            dve.wait_ge(consts, 9)
            chain(dve.tensor_scalar(rcount[:, :], slot_row[:, 0:16], 1.0, None, ALU.add))
            chain(dve.reciprocal(rcount[:, :], rcount[:, :]))
            dve.wait_ge(x_in, 16)
            for l in range(DEPTH):
                t0 = LAYER_T0[l]
                norm(3 * l)
                if l == 0:
                    split_lo(0)
                    split_lo(1)
                dve.wait_ge(pT_hi, l + 1)
                dve.tensor_tensor(pT[:, 1], ps[:, 5, :].rearrange("p (k n) -> p k n", k=2),
                                  pT[:, 0].bitcast(F32), ALU.subtract).then_inc(pT_lo, 1)
                turn_lo(4 * l)
                for j in range(2):
                    split_lo(t0 + j + 2)
                if l == 0:
                    dve.wait_ge(rope_ready, 3)
                for b in range(NB):
                    wait_product(dve, b, NB - 1, q_done, l + 1, t0 + 1)
                    rotate(ps[:, 4 + b, :], [q_rot[:, b, :].rearrange("p (h d) -> p h d", h=HEADS)], HEADS, b, 4 * l + b)
                split_lo(t0 + 4)
                for b in range(NB):
                    wait_product(dve, b, NB - 1, kv_done, l + 1, t0 + 2)
                    dve.wait_ge(v_ready, NB * l + b + 1)
                    rotate(ps[:, b, 0:P], [kdup[:, b, :, c, :] for c in range(2)], KV_HEADS, b,
                           4 * l + NB + b)
                chain(dve.memset(vpad[:, :, 0:2], 0.0))
                for j in range(8):
                    split_lo(t0 + T_CHAN + j + 2)
                    cs = slice(2 * (j % 2), 2 * (j % 2) + 2)
                    if j in (2, 3):
                        dve.wait_ge(tile_used, t0 + T_CHAN + j + 1)
                        dve.wait_ge(c_copied, 2 * l + j - 1)
                        chain(dve.tensor_tensor(vpad[:, cs, 2:], ps[:, 4 + j, :].rearrange(
                            "p (c n) -> p c n", c=2), c_sb[:, cs, :], ALU.mult))
                    if j in (4, 5):
                        dve.wait_ge(small_in, 16 + 96 * (l + 1))
                        for c in range(2):
                            ch = 2 * (j - 4) + c
                            chain(dve.tensor_scalar(cacc[:, c, :], vpad[:, ch, 0:SEQ], convw_sb[:, ch, 0:1],
                                                    None, ALU.mult))
                            for k in (1, 2):
                                chain(dve.scalar_tensor_tensor(
                                    out=cacc[:, c, :], in0=vpad[:, ch, k:k + SEQ],
                                    scalar=convw_sb[:, ch, k:k + 1], in1=cacc[:, c, :],
                                    op0=ALU.mult, op1=ALU.add))
                        dve.wait_ge(tile_used, t0 + T_CHAN + j + 1)
                        dve.tensor_tensor(ctmp, ps[:, j - 2, :].rearrange("p (c n) -> p c n", c=2), cacc,
                                          ALU.mult).then_inc(conv_y, 1)
                        dve.wait_ge(conv_hi, 2 * l + j - 3)
                        dve.tensor_tensor(brv[:, 1, cs, :], ctmp, brv[:, 0, cs, :].bitcast(F32),
                                          ALU.subtract).then_inc(conv_lo, 1)
                    if j == 5:
                        dve.wait_ge(qk_turned, 3 * l + 3)
                        for s in range(2):
                            half = slice(s * HD, (s + 1) * HD)
                            dve.tensor_copy(kT[half, :, s, :], ps[half, 0, :].rearrange(
                                "p (c n) -> p c n", c=2)).then_inc(kT_ready, 1)
                    if j in (6, 7):
                        dve.wait_ge(chan_out, 2 * l + j - 5)
                        for g in (2 * (j - 6), 2 * (j - 6) + 1):
                            if g:
                                dve.wait_ge(pooled_ready, CH * l + g)
                            src, w = upool[:, g, :], 1
                            for k in range(g + 1):
                                dst = wsum[:, k % 2, :]
                                chain(dve.tensor_tensor(dst[:, 16:], src[:, 16:], src[:, 16 - w:16 - w + SEQ],
                                                        ALU.add))
                                src, w = dst, 2 * w
                            chain(dve.scalar_tensor_tensor(out=pooled[:, g, :], in0=src[:, 16:],
                                                           scalar=1.0 / w, in1=upool[:, g, 16:],
                                                           op0=ALU.mult, op1=ALU.subtract))
                            chain(dve.tensor_tensor(src[:, 16:15 + w], src[:, 16:15 + w], rcount[:, 0:w - 1],
                                                    ALU.mult))
                            ins = dve.tensor_tensor(pooled[:, g, 0:w - 1], src[:, 16:15 + w],
                                                    upool[:, g, 16:15 + w], ALU.subtract)
                            ins.then_inc(pooled_ready, 1)
                for c in range(6):
                    for step in range(3):
                        split_lo(t0 + T_GATE + 3 * c + step + 2)
                        at = 3 * c + step
                        if at == 0:
                            dve.wait_ge(pool_hi, l + 1)
                            for g in range(CH):
                                ins = dve.scalar_tensor_tensor(
                                    out=brv[:, 3, g, :], in0=ps[:, 2 + g // 2, g % 2 * SEQ:(g % 2 + 1) * SEQ],
                                    scalar=pscale_sb[:, g:g + 1], in1=brv[:, 2, g, :].bitcast(F32),
                                    op0=ALU.mult, op1=ALU.subtract)
                            ins.then_inc(pool_lo, 2)
                        if step == 2:
                            r, nh = c // 2, c % 2
                            for b in range(NB):
                                dve.wait_ge(sig_ready, 12 * l + NB * c + b + 1)
                                wait_product(dve, b, NB - 1, branch_done, 6 * l + c + 1,
                                             t0 + T_GATE + 3 * c + 2)
                                m = M[:, b, nh * 512:(nh + 1) * 512]
                                if r == 0:
                                    dve.tensor_tensor(m, ps[:, b, :], sg[:, b, :], ALU.mult
                                                      ).then_inc(merged, 1)
                                else:
                                    dve.wait_ge(merged, 12 * l + NB * (c - 1) + b + 1)
                                    chain(dve.tensor_tensor(tmp[:, b * 512:(b + 1) * 512], ps[:, b, :],
                                                            sg[:, b, :], ALU.mult))
                                    dve.tensor_tensor(m, m, tmp[:, b * 512:(b + 1) * 512], ALU.add
                                                      ).then_inc(merged, 1)
                        if 2 <= at <= 7:
                            dve.wait_ge(pr_turned, 6 * l + at - 1)
                            dve.tensor_copy(prT[:, :, :], ps[:, 7, :].rearrange("p (c n) -> p c n", c=4)
                                            ).then_inc(prT_ready, 1)
                        if 1 <= at <= 6:
                            mask_scores(l, at - 1)
                            scale_probs(l, at - 1)
                        if at == 8:
                            for h in range(2):
                                dve.wait_ge(att_hi, 2 * l + h + 1)
                                dve.tensor_tensor(brv[:, 5, 2 * h:2 * h + 2, :],
                                                  ps[:, 2 + h, :].rearrange("p (c n) -> p c n", c=2),
                                                  brv[:, 4, 2 * h:2 * h + 2, :].bitcast(F32), ALU.subtract
                                                  ).then_inc(att_lo, 1)
                turn_lo(4 * l + 1)
                for i in range(4):
                    split_lo(t0 + T_OUT + i + 2)
                for b in range(NB):
                    wait_product(dve, b, NB - 1, out_done, l + 1, t0 + T_OUT + 3)
                    add_to_x(b, 2 * b, x_out)
                dve.wait_ge(x_out, NB * (l + 1))
                norm(3 * l + 1)
                turn_lo(4 * l + 2)
                if l == 0:
                    dve.sem_inc(x_ffn[0], 1)
                    with dve.Fori(0, FFN_BODIES[0]) as i:
                        body(0, NB, False, t0 + T_FFN, i, 2)
                    dve.wait_ge(x_ffn[0], 1 + NB * FFN_BODIES[0])
                else:
                    dve.wait_ge(yn_hi, 1)
                    dve.tensor_tensor(yn[:, 1], Y[:, :, :], yn[:, 0].bitcast(F32), ALU.subtract
                                      ).then_inc(yn_lo, 1)
                    for b in range(NB):
                        dve.wait_ge(logit_done, b + 1)
                        chain(dve.tensor_copy(logit[:, b, :], ps[:, 4 + b, 0:EXPERTS]))
                        chain(dve.max(top[:, b, :], logit[:, b, :]))
                        chain(dve.max_index(topi[:, b, :], top[:, b, :], logit[:, b, :]))
                        chain(dve.tensor_copy(topf[:, b, :], topi[:, b, :]))
                        for k in range(2):
                            ins = dve.tensor_scalar(hot[:, b, k, :], slot_row[:, 0:EXPERTS],
                                                    topf[:, b, k:k + 1], None, ALU.is_equal)
                        chain(ins)
                        chain(dve.tensor_tensor(sel[:, b, :], hot[:, b, 0, :], hot[:, b, 1, :], ALU.add))
                        dve.tensor_tensor(wts[:, b, 0:1], top[:, b, 1:2], top[:, b, 0:1], ALU.subtract
                                          ).then_inc(sel_ready, 1)
                    for b in range(NB):
                        dve.wait_ge(route_step, b + 1)
                        chain(dve.tensor_scalar(wts[:, b, 2:3], wts[:, b, 1:2], 1.0, None, ALU.add))
                        chain(dve.reciprocal(wts[:, b, 2:3], wts[:, b, 2:3]))
                        chain(dve.tensor_tensor(wts[:, b, 3:4], wts[:, b, 1:2], wts[:, b, 2:3], ALU.mult))
                        chain(dve.tensor_scalar(comb[:, b, 0:EXPERTS], hot[:, b, 0, :], wts[:, b, 2:3], None,
                                                ALU.mult))
                        chain(dve.scalar_tensor_tensor(out=comb[:, b, 0:EXPERTS], in0=hot[:, b, 1, :],
                                                       scalar=wts[:, b, 3:4], in1=comb[:, b, 0:EXPERTS],
                                                       op0=ALU.mult, op1=ALU.add))
                        chain(dve.tensor_copy(comb[:, b, EXPERTS:], comb[:, b, 0:EXPERTS]))
                    dve.wait_ge(rank_done, 1)
                    for b in range(NB):
                        chain(dve.scalar_tensor_tensor(out=rank[:, b, 0:EXPERTS],
                                                       in0=ps[:, 6, b * 8:(b + 1) * 8], scalar=1.0,
                                                       in1=sel[:, b, :], op0=ALU.add, op1=ALU.mult))
                        chain(dve.tensor_scalar(rank[:, b, 0:EXPERTS], rank[:, b, 0:EXPERTS], -1.0, None,
                                                ALU.add))
                        chain(dve.tensor_scalar(rank[:, b, EXPERTS:2 * EXPERTS], rank[:, b, 0:EXPERTS],
                                                -float(P), None, ALU.add))
                    chain(dve.memset(rank[:, :, 2 * EXPERTS:], -1.0))
                    chain(dve.tensor_copy(load[:, :], ps[:, 6, 16:24]))
                    chain(dve.tensor_reduce(most[:, 0:1], load[:, :], AX.X, ALU.max))
                    chain(dve.tensor_scalar(most[:, 1:2], most[:, 0:1], float(P), None, ALU.is_gt))
                    dve.tensor_copy(more_i[:, :], most[:, 1:2]).then_inc(routed, 1)
                    experts(1, t0 + T_FFN)
                    more = dve.value_load(more_i[0:1, 0:1], min_val=0, max_val=1)
                    with dve.If(more > 0):
                        experts(2, BODY_TILES)
                        dve.wait_ge(tile_used2, (EXPERTS + 1) * BODY_TILES)
                        dve.wait_ge(x_ffn[2], 1 + NB * (EXPERTS + 1))
                    dve.wait_ge(x_ffn[1], 1 + NB * (EXPERTS + 1))
                u = t0 + T_PLE[l]
                if l:
                    split_lo(u)
                    split_lo(u + 1)
                norm(3 * l + 2)
                split_lo(u + 2)
                turn_lo(4 * l + 3)
                for i in range(4):
                    if u + 3 + i < N_TILES:
                        split_lo(u + 3 + i)
                for b in range(NB):
                    dve.wait_ge(psig, NB * l + b + 1)
                    dve.wait_ge(proj_out, NB * l + b + 1)
                    if b:
                        dve.wait_ge(x_ple, NB * l + b)
                    chain(dve.tensor_tensor(halves(tmp[:, :]), sg[:, :, :], halves(M[:, b, :]), ALU.mult))
                    dve.tensor_tensor(X[:, b, :], X[:, b, :], tmp[:, :], ALU.add).then_inc(x_ple, 1)
                dve.wait_ge(x_ple, NB * (l + 1))
            norm(6)

        @block.tensor
        def _(pe):
            def product(dst, lh, rh, start, stop):
                pe.matmul(dst, lh[0], rh[0], start=start, stop=False)
                pe.matmul(dst, lh[0], rh[1], start=False, stop=False)
                return pe.matmul(dst, lh[1], rh[0], start=False, stop=stop)

            def pair(buf, *index):
                return [buf[(slice(None), s) + index] for s in range(2)]

            def tile_pair(t, n, k, cols):
                return [slot(t, s, n)[:, k, cols] for s in range(2)]

            def turn(n, src, half, ready):
                for b in range(NB):
                    pe.wait_ge(*ready(b))
                    for k in range(4):
                        ins = pe.transpose(ps[:, turn_bank(b, half), k * P:(k + 1) * P],
                                           src[:, b, (4 * half + k) * P:(4 * half + k + 1) * P], ident[:, :])
                    ins.then_inc(turned, 1)

            def tokens(b):
                return slice(b * P, (b + 1) * P)

            def wide(t, i, n_tiles, lhs, banks, done):
                pe.wait_ge(lo_ready, t + 1)
                for b in range(NB):
                    for nh in range(2):
                        for k in range(2):
                            ins = product(ps[:, banks[b] + nh, :], pair(lhs, 2 * i + k, tokens(b)),
                                          tile_pair(t, D, k, slice(nh * 512, (nh + 1) * 512)),
                                          i == 0 and k == 0, i == n_tiles - 1 and k == 1)
                    if b == 0 and i == n_tiles - 1:
                        ins.then_inc(done, 1)
                ins.then_inc(tile_used, 1)

            def att_scores(l, u):
                b = 0 if u < 2 else 1
                nh, n = (4, P) if u < 2 else (2, SEQ)
                h0 = 4 * u if u < 2 else 2 * (u - 2)
                if u == 0:
                    pe.wait_ge(qT_ready, 2 * l + 2)
                    pe.wait_ge(kT_ready, 2 * (l + 1))
                if u:
                    pe.wait_ge(masked, 6 * l + u)
                for i in range(nh):
                    h = h0 + i
                    ins = pe.matmul(ps[:, 6, i * n:(i + 1) * n], qT[:, h // 2, tokens(b)],
                                    kT[:, h // (HEADS // KV_HEADS), h % 2, 0:n], start=True, stop=True)
                ins.then_inc(s_done, 1)

            def att_turn(l, u):
                pe.wait_ge(probs, 6 * l + u + 1)
                if u:
                    pe.wait_ge(prT_ready, 6 * l + u)
                for i in range(4):
                    ins = pe.transpose(ps[:, 7, i * P:(i + 1) * P], sc[:, i * P:(i + 1) * P], ident[:, :])
                ins.then_inc(pr_turned, 1)

            def att_values(l, u):
                b = 0 if u < 2 else 1
                h0 = 4 * u if u < 2 else 2 * (u - 2)
                pe.wait_ge(prT_ready, 6 * l + u + 1)
                if u == 0:
                    pe.wait_ge(v_ready, NB * (l + 1))
                    pe.wait_ge(pool_lo, 2 * (l + 1))
                per = b + 1
                for i in range(4):
                    h = h0 + i // per
                    kv = h // (HEADS // KV_HEADS)
                    c = h // 2
                    rows = slice(h % 2 * HD, (h % 2 + 1) * HD)
                    ins = pe.matmul(ps[rows, 2 + c // 2, (c % 2) * SEQ + b * P:(c % 2) * SEQ + (b + 1) * P],
                                    v_sb[:, i % per, kv * HD:(kv + 1) * HD], prT[:, i, :],
                                    start=i % per == 0, stop=i % per == per - 1)
                if u == 5:
                    ins.then_inc(att_done, 1)

            def body(s, nb, moe, t0, i):
                stream = 2 if s == 2 else 1
                _, _, lo, used = STREAMS[stream]
                lhs = xe if moe else hT
                aT = aT_moe if moe else aT_dense
                j = 0
                for step, kind, f in body_schedule(moe):
                    if step == "tile":
                        t = t0 + j
                        pe.wait_ge(lo, t + 1 + i * BODY_TILES)
                        if kind in "ab":
                            k0 = 0 if kind == "a" else 4
                            if moe and kind == "a" and f == 0:
                                pe.wait_ge(xe_lo[s], 2 + i * 2)
                            for b in range(nb):
                                bank = 4 + (f % 2 if moe else b)
                                if kind == "a" and moe and f >= 2:
                                    pe.wait_ge(act_ready[s], f - 1 + i * BODY_F)
                                if kind == "a" and not moe and f >= 1:
                                    pe.wait_ge(act_ready[s], nb * (f - 1) + b + 1 + i * (nb * BODY_F))
                                for k in range(4):
                                    for m, (sl, sr) in enumerate(((0, 0), (0, 1), (1, 0))):
                                        ins = pe.matmul(ps[:, bank, :], lhs[:, sl, k0 + k, tokens(b)],
                                                        slot(t, sr, 512)[:, k, :],
                                                        start=kind == "a" and k + m == 0,
                                                        stop=kind == "b" and k == 3 and m == 2)
                                if kind == "b" and b < nb - 1:
                                    ins.then_inc(gu_done, 1)
                        else:
                            pe.wait_ge(aT_lo[s], f + 1 + i * BODY_F)
                            if f == 0 and not moe:
                                pe.wait_ge(x_ffn[s], 1 + i * nb)
                            for b in range(nb):
                                for nh in range(2):
                                    for k in range(2):
                                        for m, (sl, sr) in enumerate(((0, 0), (0, 1), (1, 0))):
                                            ins = pe.matmul(ps[:, 2 * b + nh, :],
                                                            aT[:, f % 2, sl, k, tokens(b)],
                                                            slot(t, sr, D)[:, k, nh * 512:(nh + 1) * 512],
                                                            start=f == 0 and k + m == 0,
                                                            stop=f == BODY_F - 1 and k == 1 and m == 2)
                                if f == BODY_F - 1 and b < nb - 1:
                                    ins.then_inc(down_done, 1)
                        ins.then_inc(used, 1)
                        j += 1
                    elif step == "turn":
                        pe.wait_ge(act_ready[s], nb * (f + 1) + i * (nb * BODY_F))
                        for k in range(2):
                            for b in range(nb):
                                ins = pe.transpose(ps[:, 6 + f % 2, (k * nb + b) * P:(k * nb + b + 1) * P],
                                                   tmp[:, b * 256 + k * P:b * 256 + (k + 1) * P], ident[:, :])
                        ins.then_inc(a_turned[s], 1)
                    elif step == "scatter":
                        if f == 0:
                            pe.wait_ge(ye_lo[s], 2 + i * 2)
                            pe.wait_ge(gT_ready[s], 1 + i)
                        scatter(s, f, NB * i + f)
                    elif step == "route":
                        pe.wait_ge(x_ffn[s], 1 + NB + i * NB)
                        for b in range(NB):
                            pe.transpose(ps[:, 2, tokens(b)], G[:, b, :].bitcast(F32), ident[:, :])
                        for b in range(NB):
                            ins = pe.matmul(ps[:, 2, SEQ:SEQ + 1], G[:, b, :].bitcast(F32),
                                            comb[:, b, bass.ds(i + (EXPERTS if s == 2 else 0), 1)],
                                            start=b == 0, stop=b == NB - 1)
                        ins.then_inc(route_done[s], 1)
                    elif step == "gather":
                        pe.wait_ge(g_ready[s], 2 + i)
                        pe.wait_ge(gT_ready[s], 2 + i)
                        gather(s)

            def scatter(s, b, n):
                pe.wait_ge(x_ffn[s], 1 + n)
                for nh in range(2):
                    for k in range(2):
                        ins = pe.matmul(ps[:, 2 + nh, :], GT[:, tokens(b)], ye[:, k, nh * 512:(nh + 1) * 512],
                                        start=k == 0, stop=k == 1)
                ins.then_inc(scattered[s], 1)

            def gather(s):
                for k in range(KD):
                    for m, (b, part) in enumerate(((0, 0), (0, 1), (1, 0), (1, 1))):
                        ins = pe.matmul(ps[:, 2 + k // 4, k % 4 * P:(k % 4 + 1) * P],
                                        yn[:, part, b, k * P:(k + 1) * P], G[:, b, :],
                                        start=m == 0, stop=m == 3)
                    if k % 4 == 3:
                        ins.then_inc(gathered[s], 1)

            def experts(s, t0):
                pe.wait_ge(g_ready[s], 1)
                if s == 1:
                    pe.wait_ge(yn_lo, 1)
                gather(s)
                with pe.Fori(0, EXPERTS) as e:
                    body(s, 1, True, t0, e)
                pe.wait_ge(ye_lo[s], 2 * (EXPERTS + 1))
                pe.wait_ge(gT_ready[s], EXPERTS + 1)
                pe.wait_ge(xe_lo[s], 2 * (EXPERTS + 1))
                for b in range(NB):
                    scatter(s, b, EXPERTS * NB + b)

            pe.wait_ge(consts, 9)
            for l in range(DEPTH):
                t0 = LAYER_T0[l]
                pe.wait_ge(p_in, 16 * (l + 1))
                for k in range(2):
                    for b in range(NB):
                        ins = pe.transpose(ps[:, 5, k * SEQ + b * P:k * SEQ + (b + 1) * P],
                                           tmp[:, b * PLE + k * P:b * PLE + (k + 1) * P], ident[:, :])
                ins.then_inc(p_turned, 1)
                for half in range(2):
                    turn(4 * l, Y, half, lambda b: (y_ready, NB * 3 * l + b + 1))
                pe.wait_ge(pT_lo, l + 1)
                for i in range(2):
                    t = t0 + i
                    pe.wait_ge(lo_ready, t + 1)
                    pe.wait_ge(hT_lo, 16 * l + 2 * i + 2)
                    for b in range(NB):
                        for k in range(4):
                            ins = product(ps[:, 4 + b, :], pair(hT, 4 * i + k, tokens(b)),
                                          tile_pair(t, 512, k, slice(0, 512)), i + k == 0, i == 1 and k == 3)
                        if i == 1 and b == 0:
                            ins.then_inc(q_done, 1)
                    ins.then_inc(tile_used, 1)
                t = t0 + 2
                pe.wait_ge(lo_ready, t + 1)
                for b in range(NB):
                    for k in range(KD):
                        ins = product(ps[:, b, 0:256], pair(hT, k, tokens(b)),
                                      tile_pair(t, 256, k, slice(0, 256)), k == 0, k == KD - 1)
                    if b == 0:
                        ins.then_inc(kv_done, 1)
                ins.then_inc(tile_used, 1)
                for j, bank in enumerate((2, 3, 6, 7, 2, 3, 4, 5)):
                    t = t0 + T_CHAN + j
                    pe.wait_ge(lo_ready, t + 1)
                    if j in (4, 5):
                        pe.wait_ge(c_copied, 2 * l + j - 3)
                    if j == 6:
                        pe.wait_ge(rot_ready, 4 * (l + 1))
                    for c in range(2):
                        for k in range(KD):
                            ins = product(ps[:, bank, c * SEQ:(c + 1) * SEQ],
                                          tile_pair(t, 256, k, slice(c * P, (c + 1) * P)),
                                          pair(hT, k, slice(0, SEQ)), k == 0, k == KD - 1)
                    ins.then_inc(tile_used, 1)
                    if j == 5:
                        pe.wait_ge(rot_ready, 4 * (l + 1))
                        pe.wait_ge(v_ready, NB * (l + 1))
                        pe.wait_ge(conv_y, 2 * l + 1)
                        for c in range(CH):
                            for b in range(NB):
                                ins = pe.transpose(
                                    ps[:, 6 + c // 2, c % 2 * SEQ + b * P:c % 2 * SEQ + (b + 1) * P],
                                    q_rot[:, b, c * P:(c + 1) * P], ident[:, :])
                            if c % 2:
                                ins.then_inc(qk_turned, 1)
                        for h in range(KV_HEADS):
                            for b in range(NB):
                                ins = pe.transpose(ps[:, 0, h * SEQ + b * P:h * SEQ + (b + 1) * P],
                                                   kdup[:, b, h].rearrange("p c d -> p (c d)"), ident[:, :])
                        ins.then_inc(qk_turned, 1)
                for c in range(6):
                    r, nh = c // 2, c % 2
                    for step in range(3):
                        t = t0 + T_GATE + 3 * c + step
                        at = 3 * c + step
                        pe.wait_ge(lo_ready, t + 1)
                        if step < 2:
                            for b in range(NB):
                                if c and step == 0:
                                    pe.wait_ge(sig_ready, 12 * l + NB * (c - 1) + b + 1)
                                if c == 0 and step == 0:
                                    pe.wait_ge(chan_out, 2 * l + 1 + b)
                                for k in range(4):
                                    ins = product(ps[:, 4 + b, :], pair(hT, 4 * step + k, tokens(b)),
                                                  tile_pair(t, 512, k, slice(0, 512)),
                                                  step + k == 0, step == 1 and k == 3)
                                if step and b == 0:
                                    ins.then_inc(gate_done, 1)
                        else:
                            ready = ((conv_lo, 2 * (l + 1)), (pool_lo, 2 * (l + 1)), (att_lo, 2 * (l + 1)))[r]
                            pe.wait_ge(*ready)
                            if c == 0:
                                pe.wait_ge(kT_ready, 2 * (l + 1))
                            for b in range(NB):
                                if c:
                                    pe.wait_ge(merged, 12 * l + NB * (c - 1) + b + 1)
                                for k in range(CH):
                                    lh = [brv[:, 2 * r + s, k, tokens(b)] for s in range(2)]
                                    ins = product(ps[:, b, :], lh, tile_pair(t, 512, k, slice(0, 512)),
                                                  k == 0, k == CH - 1)
                                if b == 0:
                                    ins.then_inc(branch_done, 1)
                        ins.then_inc(tile_used, 1)
                        if at == 0:
                            pe.wait_ge(pooled_ready, CH * (l + 1))
                            pe.wait_ge(small_in, 16 + 96 * (l + 1))
                            pe.wait_ge(conv_y, 2 * (l + 1))
                            for g in range(CH):
                                ins = pe.matmul(ps[:, 2 + g // 2, g % 2 * SEQ:(g % 2 + 1) * SEQ],
                                                poolw_sb[:, g, :], pooled[:, g, :], start=True, stop=True)
                            ins.then_inc(mixed_done, 1)
                        if 3 <= at <= 8:
                            att_values(l, at - 3)
                        if 2 <= at <= 7:
                            att_turn(l, at - 2)
                        if 1 <= at <= 6:
                            att_scores(l, at - 1)
                        if at == 15:
                            turn(4 * l + 1, M, 0, lambda b: (merged, 12 * l + 8 + b + 1))
                turn(4 * l + 1, M, 1, lambda b: (merged, 12 * l + 10 + b + 1))
                for i in range(4):
                    if i == 0:
                        pe.wait_ge(hT_lo, 16 * l + 8)
                    wide(t0 + T_OUT + i, i, 4, hT, (0, 2), out_done)
                for half in range(2):
                    turn(4 * l + 2, Y, half, lambda b: (y_ready, NB * (3 * l + 1) + b + 1))
                pe.wait_ge(hT_lo, 16 * l + 12)
                if l == 0:
                    with pe.Fori(0, FFN_BODIES[0]) as i:
                        body(0, NB, False, t0 + T_FFN, i)
                    pe.wait_ge(x_ffn[0], 1 + NB * FFN_BODIES[0])
                else:
                    for b in range(NB):
                        for k in range(KD):
                            for s in range(2):
                                ins = pe.matmul(ps[:, 4 + b, 0:EXPERTS], hT[:, s, k, tokens(b)].bitcast(F32),
                                                router_sb[:, k, :], start=k + s == 0, stop=k + s == KD)
                        ins.then_inc(logit_done, 1)
                    pe.wait_ge(sel_ready, NB)
                    pe.matmul(ps[:, 6, 0:8], below[:, :], sel[:, 0, :], start=True, stop=True)
                    pe.matmul(ps[:, 6, 8:16], ones[:, :], sel[:, 0, :], start=True, stop=False)
                    pe.matmul(ps[:, 6, 8:16], below[:, :], sel[:, 1, :], start=False, stop=True)
                    pe.matmul(ps[:, 6, 16:24], ones[:, :], sel[:, 0, :], start=True, stop=False)
                    pe.matmul(ps[:, 6, 16:24], ones[:, :], sel[:, 1, :], start=False, stop=True
                              ).then_inc(rank_done, 1)
                    experts(1, t0 + T_FFN)
                    more = pe.value_load(more_i[0:1, 0:1], min_val=0, max_val=1)
                    with pe.If(more > 0):
                        pe.wait_ge(x_ffn[1], 1 + NB * (EXPERTS + 1))
                        pe.sem_inc(tile_used2, BODY_TILES)
                        experts(2, BODY_TILES)
                        pe.wait_ge(x_ffn[2], 1 + NB * (EXPERTS + 1))
                    pe.wait_ge(x_ffn[1], 1 + NB * (EXPERTS + 1))
                u = t0 + T_PLE[l]
                wide(u, 0, 1, pT, (0, 4), proj_done)
                for half in range(2):
                    turn(4 * l + 3, Y, half, lambda b: (y_ready, NB * (3 * l + 2) + b + 1))
                pe.wait_ge(hT_lo, 16 * l + 16)
                pe.wait_ge(proj_out, NB * (l + 1))
                for i in range(4):
                    wide(u + 1 + i, i, 4, hT, (0, 2), pg_done)


_INS = ["x", "p", "positions", "norm_mix_g", "w_in", "conv_w", "pool_w", "pool_scale", "attn_sinks",
        "w_branch", "w_out", "norm_ffn_g", "ffn_w_gu", "ffn_w_down", "moe_router", "moe_w_gu",
        "moe_w_down", "norm_ple_g", "ple_w_proj", "ple_w_gate", "final_norm_g"]


def kernel(**inputs):
    import concourse.bacc as bacc
    from concourse.bass_utils import run_bass_kernel_spmd as run

    nc = bacc.Bacc("TRN2", target_bir_lowering=False, num_devices=1, dynamic_dma_scratch_size=4096)
    arrays = {name: np.ascontiguousarray(inputs[name]) for name in _INS}
    arrays["inv_freq"] = (np.float32(10000.0) ** (
        np.float32(-2.0) * np.arange(HALF, dtype=np.float32) / np.float32(HD))).astype(np.float32)[None, :]
    args = [nc.dram_tensor(f"{n}_dram", a.shape, mybir.dt.from_np(a.dtype), kind="ExternalInput").ap()
            for n, a in arrays.items()]
    out = nc.dram_tensor("out_dram", (1, SEQ, D), F32, kind="ExternalOutput").ap()
    trunk(nc, *args, out)
    r = run(nc, [{f"{n}_dram": a for n, a in arrays.items()}], core_ids=[0])
    return r.results[0]["out_dram"]
```

```python
from contextlib import ExitStack

import numpy as np

import concourse.bass as bass
from concourse import mybir

F32 = mybir.dt.float32
F32R = mybir.dt.float32r
I32 = mybir.dt.int32
U32 = mybir.dt.uint32
ALU = mybir.AluOpType
ACT = mybir.ActivationFunctionType
AX = mybir.AxisListType

P = 128
D = 1024
SEQ = 256
NB = SEQ // P
KD = D // P
DEPTH = 2
BW = 512
CH = BW // P
HEADS, KV_HEADS, HD = 8, 2, 64
HALF = HD // 2
D_FF = 3584
EXPERTS = 8
D_FFE = 1792
PLE = 256
EPS = 1e-6
NEG = -1e30
OFF_POOL, OFF_Q, OFF_K, OFF_GATE = 1536, 2048, 2560, 2816

RAW, SPLIT = 7, 3
TILE = 2048
BODY_F = 7
BODY_TILES = 3 * BODY_F

MIX, ATT, ATT_OUT = 2, 1, 11
PROJ_BANKS = [(0, 2), (4, 6)]

SCATTER_BANKS = (2, 0)

T_CHAN = 3
T_GATE = T_CHAN + 8
T_OUT = T_GATE + 18
T_FFN = T_OUT + 4
FFN_BODIES = [D_FF // (256 * BODY_F), EXPERTS]
T_PLE = [T_FFN + BODY_TILES * n for n in FFN_BODIES]
LAYER_T0 = [0, T_PLE[0] + 5]
N_TILES = LAYER_T0[1] + T_PLE[1] + 5


def swiglu_blocks(moe, kind, f):
    if moe:
        return (0,) if kind == "" else ()
    if f:
        return (0, 1) if kind == "" else ()
    return {"a": (), "b": (0,), "": (1,)}[kind]


def body_schedule(moe):
    s = []
    for f in range(BODY_F):
        s.append(("tile", "a", f))
        if moe and f == 0:
            s.append(("scatter", "", 0))
        if f:
            s.append(("turn", "", f - 1))
        s.append(("tile", "b", f))
        s.append(("swiglu", "", f))
        if moe and f == 0:
            s.append(("scatter", "", 1))
        if moe and f == 1:
            s.append(("route", "", 0))
        if f:
            s.append(("tile", "d", f - 1))
    s.append(("turn", "", BODY_F - 1))
    if moe:
        s.append(("gather", "", 0))
    s.append(("tile", "d", BODY_F - 1))
    s.append(("close", "", 0))
    return s


def turn_order(n):
    if n % 4 == 1:
        return [(b, half) for half in range(2) for b in range(NB)]
    return [(b, half) for b in range(NB) for half in range(2)]


def turn_bank(blk, half):
    return (6, 4)[half] + blk


def trunk(nc, x, p, positions, norm_mix_g, w_in, conv_w, pool_w, pool_scale, attn_sinks, w_branch,
          w_out, norm_ffn_g, ffn_w_gu, ffn_w_down, moe_router, moe_w_gu, moe_w_down, norm_ple_g,
          ple_w_proj, ple_w_gate, final_norm_g, inv_freq, out):
    ctx = ExitStack()
    with ctx:
        def sb(name, shape, dt=F32):
            return ctx.enter_context(nc.sbuf_tensor(name, shape, dt))

        def sem(name):
            return ctx.enter_context(nc.semaphore(name))

        raw = sb("raw", [P, RAW, TILE])
        split = sb("split", [P, SPLIT, 2, TILE], F32R)
        X = sb("X", [P, NB, D])
        Y = sb("Y", [P, NB, D])
        M = sb("M", [P, NB, D])
        g_row = sb("g_row", [P, D])
        hT = sb("hT", [P, 2, KD, SEQ], F32R)
        br = sb("br", [P, 6, CH * SEQ], F32R)
        pT = sb("pT", [P, 2, 2, SEQ], F32R)
        upool = sb("upool", [P, CH, 16 + SEQ])
        wsum = sb("wsum", [P, 2, 16 + SEQ])
        kdup = sb("kdup", [P, NB, KV_HEADS, 2, HD])
        v_sb = sb("v_sb", [P, NB, KV_HEADS * HD])
        qT = sb("qT", [P, CH, SEQ])
        kT = sb("kT", [P, KV_HEADS, 2, SEQ])
        sc = sb("sc", [P, 512])
        prT = sb("prT", [P, 4, P])
        sg = sb("sg", [P, NB, 512])
        tmp = sb("tmp", [P, D])
        poolw_sb = sb("poolw_sb", [P, CH, P])
        convw_sb = sb("convw_sb", [P, CH, 3])
        pscale_sb = sb("pscale_sb", [P, CH])
        sinks_sb = sb("sinks_sb", [P, HEADS])
        router_sb = sb("router_sb", [P, KD, EXPERTS])
        ident = sb("ident", [P, P])
        below = sb("below", [P, P])
        ones = sb("ones", [P, P])
        slot_row = sb("slot_row", [P, P])
        mask = sb("mask", [P, SEQ])
        rcount = sb("rcount", [P, 16])
        pos_i = sb("pos_i", [P, NB], I32)
        pos_f = sb("pos_f", [P, NB])
        freq = sb("freq", [P, HALF])
        ang = sb("ang", [P, 2, NB, HALF])
        turns = sb("turns", [P, 2, NB, HALF])
        sin2 = sb("sin2", [P, NB, 2, HALF])
        cos1 = sb("cos1", [P, NB, HALF])
        ms = sb("ms", [P, NB])
        rstd = sb("rstd", [P, 2])
        power = sb("power", [P, 1])
        mx = sb("mx", [P, 4])
        nmx = sb("nmx", [P, 2, 4])
        den = sb("den", [P, 2, 4])
        esk = sb("esk", [P, 2, 4])
        rden = sb("rden", [P, 4])
        logit = sb("logit", [P, NB, EXPERTS])
        top = sb("top", [P, NB, 8])
        topi = sb("topi", [P, NB, 8], U32)
        topf = sb("topf", [P, NB, 8])
        hot = sb("hot", [P, NB, 2, EXPERTS])
        wts = sb("wts", [P, NB, 4])
        comb = sb("comb", [P, NB, 2 * EXPERTS])
        sel = sb("sel", [P, NB, EXPERTS])
        rank = sb("rank", [P, NB, 2 * EXPERTS + 1])
        load = sb("load", [P, EXPERTS])
        most = sb("most", [P, 2])
        more_i = sb("more_i", [P, 1], I32)
        G = sb("G", [P, NB, P], F32R)
        GT = sb("GT", [P, SEQ], F32R)
        w_slot = sb("w_slot", [P, 1])

        q_rot = Y[:, 0, :].rearrange("p (b n) -> p b n", b=NB)
        p_sb = upool[:, 0:NB, 16:]
        c_sb = Y[:, 1, :].rearrange("p (c n) -> p c n", c=CH)
        pooled = c_sb
        vpad = M[:, 0:2, :].rearrange("p b n -> p (b n)")[:, 0:CH * (SEQ + 2)].rearrange(
            "p (c n) -> p c n", c=CH)
        cacc = M[:, 0:2, :].rearrange("p b n -> p (b n)")[:, 1536:2048].rearrange(
            "p (c n) -> p c n", c=2)
        ctmp = tmp[:, 0:512].rearrange("p (c n) -> p c n", c=2)
        brv = br[:, :, :].rearrange("p r (c n) -> p r c n", c=CH)
        yn = br[:, 0:4, :].rearrange("p (s b) n -> p s b n", s=2)
        xe = br[:, 4:6, :].rearrange("p s (k n) -> p s k n", k=KD)
        hTf = hT[:, :, :, :].rearrange("p s k n -> p (s k n)")
        ye = hTf[:, 0:2 * D].rearrange("p (s n) -> p s n", s=2)
        aT_moe = hTf[:, 2 * D:2 * D + 1024].rearrange("p (u s k n) -> p u s k n", u=2, s=2, k=2)
        brf = br[:, :, :].rearrange("p r n -> p (r n)")
        aT_dense = brf[:, 0:2048].rearrange("p (u s k n) -> p u s k n", u=2, s=2, k=2)

        ps = ctx.enter_context(nc.psum_tensor("ps", [P, 8, 512], F32))

        landed = [sem(f"landed{i}") for i in range(RAW)]
        hi_ready, lo_ready, tile_used = sem("hi_ready"), sem("lo_ready"), sem("tile_used")
        consts = sem("consts")
        cstep = sem("cstep")
        x_in = [sem(f"x_in{b}") for b in range(NB)]
        pos_in, small_in, g_in = sem("pos_in"), sem("small_in"), sem("g_in")
        g_first = sem("g_first")
        p_in = [sem(f"p_in{l}") for l in range(DEPTH)]
        dve_step = sem("dve_step")
        rope_ang, rope_ready = sem("rope_ang"), sem("rope_ready")
        ms_plus = sem("ms_plus")
        ms_ready, rstd_ready, y_ready = sem("ms_ready"), sem("rstd_ready"), sem("y_ready")
        turned, hT_hi, hT_lo = sem("turned"), sem("hT_hi"), sem("hT_lo")
        p_turned, pT_hi, pT_lo = sem("p_turned"), sem("pT_hi"), sem("pT_lo")
        q_done, kv_done, rot_ready, v_ready = sem("q_done"), sem("kv_done"), sem("rot_ready"), sem("v_ready")
        chan_out = sem("chan_out")
        c_copied = sem("c_copied")
        conv_y, conv_hi, conv_lo = sem("conv_y"), sem("conv_hi"), sem("conv_lo")
        conv_v, pool_step, rcount_ready = sem("conv_v"), sem("pool_step"), sem("rcount_ready")
        pooled_ready, mixed_done = sem("pooled_ready"), sem("mixed_done")
        pool_hi, pool_lo = sem("pool_hi"), sem("pool_lo")
        qk_turned, qT_ready, kT_ready = sem("qk_turned"), sem("qT_ready"), sem("kT_ready")
        s_done, masked, exped, probs, pr_turned, prT_ready = (
            sem("s_done"), sem("masked"), sem("exped"), sem("probs"), sem("pr_turned"), sem("prT_ready"))
        att_done, att_hi, att_lo = sem("att_done"), sem("att_hi"), sem("att_lo")
        gate_done, sig_ready, branch_done, merged = (
            sem("gate_done"), sem("sig_ready"), sem("branch_done"), sem("merged"))
        out_done, x_out = sem("out_done"), sem("x_out")
        proj_done, proj_out = sem("proj_done"), sem("proj_out")
        pg_done, psig, x_ple = sem("pg_done"), sem("psig"), sem("x_ple")
        gu_done, down_done = sem("gu_done"), sem("down_done")
        silu_ready = [sem(f"silu_ready{i}") for i in range(3)]
        act_ready = [sem(f"act_ready{i}") for i in range(3)]
        a_turned = [sem(f"a_turned{i}") for i in range(3)]
        aT_hi = [sem(f"aT_hi{i}") for i in range(3)]
        aT_lo = [sem(f"aT_lo{i}") for i in range(3)]
        x_ffn = [sem(f"x_ffn{i}") for i in range(3)]
        logit_done, route_step, sel_ready, rank_done = (
            sem("logit_done"), sem("route_step"), sem("sel_ready"), sem("rank_done"))
        routed, yn_hi, yn_lo = sem("routed"), sem("yn_hi"), sem("yn_lo")
        g_ready = [None] + [sem(f"g_ready{i}") for i in (1, 2)]
        route_done = [None] + [sem(f"route_done{i}") for i in (1, 2)]
        gT_ready = [None] + [sem(f"gT_ready{i}") for i in (1, 2)]
        ws_ready = [None] + [sem(f"ws_ready{i}") for i in (1, 2)]
        gathered = [None] + [sem(f"gathered{i}") for i in (1, 2)]
        xe_hi = [None] + [sem(f"xe_hi{i}") for i in (1, 2)]
        xe_lo = [None] + [sem(f"xe_lo{i}") for i in (1, 2)]
        ye_hi = [None] + [sem(f"ye_hi{i}") for i in (1, 2)]
        ye_lo = [None] + [sem(f"ye_lo{i}") for i in (1, 2)]
        scattered = [None] + [sem(f"scattered{i}") for i in (1, 2)]
        landed2 = [sem(f"landed2_{i}") for i in range(RAW)]
        hi_ready2, lo_ready2, tile_used2 = sem("hi_ready2"), sem("lo_ready2"), sem("tile_used2")
        stored = sem("stored")

        STREAMS = {1: (landed, hi_ready, lo_ready, tile_used),
                   2: (landed2, hi_ready2, lo_ready2, tile_used2)}

        def slot(t, s, n):
            return split[:, t % SPLIT, s, :].rearrange("p (k n) -> p k n", n=n)

        def raw_slot(t, n):
            return raw[:, t % RAW, :].rearrange("p (k n) -> p k n", n=n)

        def wait_product(eng, b, last, signal, n, t, i=0, per=0, stream=1):
            if b == last:
                eng.wait_ge(STREAMS[stream][3], t + 1 + i * per)
            else:
                eng.wait_ge(signal, n)

        def scores_of(u):
            return sc[:, :] if u % 3 == 2 else tmp[:, u % 3 * 512:(u % 3 + 1) * 512]

        def halves(a):
            return a.rearrange("p (h n) -> p h n", h=2)

        def two_banks(b0):
            return ps[:, b0:b0 + 2, :]

        block = ctx.enter_context(nc.Block())

        @block.sync
        def _(sp):
            def fetch(t, parts, i=0, per=0, stream=1):
                land, _, lo, _ = STREAMS[stream]
                if t >= RAW:
                    sp.wait_ge(lo, t - RAW + 1 + i * per)
                for dst, src in parts:
                    sp.dma_start(dst, src).then_inc(land[t % RAW], 32 // len(parts))

            def rows(w, k0, nk, c0, n):
                return w[k0 * P:(k0 + nk) * P, c0:c0 + n].rearrange("(k p) n -> p k n", p=P)

            def ffn(stream, t0, w_gu, w_down, d_ff, f0, i=0):
                j = 0
                for step, kind, f in body_schedule(False):
                    if step != "tile":
                        continue
                    t = t0 + j
                    if kind == "d":
                        src = w_down[bass.ds((f0 + f) * 256, 256), :].rearrange("(k p) n -> p k n", p=P)
                        fetch(t, [(raw_slot(t, D), src)], i, BODY_TILES, stream)
                    else:
                        k0 = 0 if kind == "a" else 4
                        parts = []
                        for s in range(2):
                            src = w_gu[k0 * P:(k0 + 4) * P, bass.ds(s * d_ff + (f0 + f) * 256, 256)]
                            parts.append((raw_slot(t, 512)[:, :, s * 256:(s + 1) * 256],
                                          src.rearrange("(k p) n -> p k n", p=P)))
                        fetch(t, parts, i, BODY_TILES, stream)
                    j += 1

            def experts(stream, t0):
                with sp.Fori(0, EXPERTS) as e:
                    gu = moe_w_gu[0, bass.ds(e, 1)].rearrange("e k n -> (e k) n")
                    dn = moe_w_down[0, bass.ds(e, 1)].rearrange("e k n -> (e k) n")
                    ffn(stream, t0, gu, dn, D_FFE, 0, e)

            for b in range(NB):
                sp.dma_start(X[:, b, :], x[0, b * P:(b + 1) * P, :]).then_inc(x_in[b], 16)
            for l in range(DEPTH):
                t = LAYER_T0[l]
                w = w_in[l]
                for i in range(2):
                    fetch(t + i, [(raw_slot(t + i, 512), rows(w, 4 * i, 4, OFF_Q, 512))])
                fetch(t + 2, [(raw_slot(t + 2, 256), rows(w, 0, KD, OFF_K, 256))])
                for j, c0 in enumerate((512, 768, 1024, 1280, 0, 256, OFF_POOL, OFF_POOL + 256)):
                    u = t + T_CHAN + j
                    fetch(u, [(raw_slot(u, 256), rows(w, 0, KD, c0, 256))])
                for r in range(3):
                    for nh in range(2):
                        u = t + T_GATE + 3 * (2 * r + nh)
                        for i in range(2):
                            fetch(u + i, [(raw_slot(u + i, 512),
                                           rows(w, 4 * i, 4, OFF_GATE + r * D + nh * 512, 512))])
                        fetch(u + 2, [(raw_slot(u + 2, 512), rows(w_branch[l, r], 0, CH, nh * 512, 512))])
                for i in range(4):
                    fetch(t + T_OUT + i, [(raw_slot(t + T_OUT + i, D), rows(w_out[l], 2 * i, 2, 0, D))])
                u = t + T_PLE[l]
                if l == 0:
                    with sp.Fori(0, FFN_BODIES[0]) as i:
                        ffn(1, t + T_FFN, ffn_w_gu[0], ffn_w_down[0], D_FF, i * BODY_F, i)
                    fetch(u, [(raw_slot(u, D), rows(ple_w_proj[l], 0, 2, 0, D))])
                else:
                    experts(1, t + T_FFN)
                    fetch(u, [(raw_slot(u, D), rows(ple_w_proj[l], 0, 2, 0, D))])
                    sp.wait_ge(routed, 1)
                    more = sp.value_load(more_i[0:1, 0:1], min_val=0, max_val=1)
                    with sp.If(more > 0):
                        sp.wait_ge(lo_ready, u + 1)
                        for land in landed2:
                            sp.sem_inc(land, 32 * (BODY_TILES // RAW))
                        experts(2, BODY_TILES)
                        sp.wait_ge(lo_ready2, (EXPERTS + 1) * BODY_TILES)
                for i in range(4):
                    fetch(u + 1 + i, [(raw_slot(u + 1 + i, D), rows(ple_w_gate[l], 2 * i, 2, 0, D))])
            for b in range(NB):
                sp.wait_ge(y_ready, 6 * NB + b + 1)
                sp.dma_start(out[0, b * P:(b + 1) * P, :], Y[:, b, :]).then_inc(stored, 16)
            sp.wait_ge(stored, 16 * NB)

        gains = [norm_mix_g[0:1, :], norm_ffn_g[0:1, :], norm_ple_g[0:1, :],
                 norm_mix_g[1:2, :], norm_ffn_g[1:2, :], norm_ple_g[1:2, :],
                 final_norm_g.rearrange("(a n) -> a n", a=1)]

        def on_all(row):
            return row.broadcast_to([P, row.shape[-1]])

        @block.gpsimd
        def _(pool):
            pool.memset(power[:, :], -0.5).then_inc(consts, 1)
            pool.memset(ident[:, :], 0.0).then_inc(cstep, 1)
            pool.memset(below[:, :], 1.0).then_inc(cstep, 1)
            pool.memset(mask[:, :], 0.0).then_inc(cstep, 1)
            pool.memset(ones[:, :], 1.0).then_inc(consts, 1)
            pool.memset(upool[:, :, 0:16], 0.0).then_inc(consts, 1)
            pool.memset(wsum[:, :, 0:16], 0.0).then_inc(consts, 1)
            pool.memset(kT[:, :, :, :], 0.0).then_inc(consts, 1)
            pool.iota(slot_row[:, :], pattern=[[1, P]], base=0, channel_multiplier=0,
                      allow_small_or_imprecise_dtypes=True).then_inc(consts, 1)
            pool.wait_ge(cstep, 3)
            pool.affine_select(out=ident[:, :], in_=ident[:, :], compare_op=ALU.not_equal, fill=1.0,
                               base=0, pattern=[[-1, P]], channel_multiplier=1).then_inc(consts, 1)
            pool.affine_select(out=below[:, :], in_=below[:, :], compare_op=ALU.is_gt, fill=0.0,
                               base=0, pattern=[[1, P]], channel_multiplier=-1).then_inc(consts, 1)
            pool.affine_select(out=mask[:, :], in_=mask[:, :], compare_op=ALU.is_gt, fill=NEG,
                               base=0, pattern=[[1, SEQ]], channel_multiplier=-1).then_inc(cstep, 1)
            pool.wait_ge(cstep, 4)
            pool.affine_select(out=mask[:, :], in_=mask[:, :], compare_op=ALU.is_ge, fill=NEG,
                               base=P, pattern=[[-1, SEQ]], channel_multiplier=1).then_inc(consts, 1)
            pool.wait_ge(consts, 9)

            def layer_loads(l):
                if l:
                    pool.wait_ge(mixed_done, l)
                    pool.wait_ge(pool_lo, 2 * l)
                    pool.wait_ge(conv_lo, 2 * l)
                    pool.wait_ge(probs, 6 * l)
                pool.dma_start(poolw_sb[:, :, :], pool_w[l].rearrange("g c d -> c g d")).then_inc(small_in, 16)
                for k in range(3):
                    pool.dma_start(convw_sb[:, :, k], conv_w[l, k].rearrange("(c p) -> p c", p=P),
                                   allow_slow_non_contiguous=True
                                   ).then_inc(small_in, 16)
                pool.dma_start(pscale_sb[:, :], pool_scale[l].rearrange("(c p) -> p c", p=P),
                               allow_slow_non_contiguous=True
                               ).then_inc(small_in, 16)
                pool.dma_start(sinks_sb[:, :], on_all(attn_sinks[l:l + 1, :])).then_inc(small_in, 16)

            def rms(n):
                for b in range(NB):
                    pool.wait_ge(ms_ready, NB * n + b + 1)
                    pool.tensor_scalar(rstd[:, b:b + 1], ms[:, b:b + 1], EPS, None, ALU.add
                                       ).then_inc(ms_plus, 1)
                    pool.wait_ge(ms_plus, NB * n + b + 1)
                    pool.tensor_tensor(rstd[:, b:b + 1], rstd[:, b:b + 1], power[:, :], ALU.pow
                                       ).then_inc(rstd_ready, 1)
                if n + 1 < len(gains):
                    pool.wait_ge(y_ready, NB * (n + 1))
                    pool.dma_start(g_row[:, :], on_all(gains[n + 1])).then_inc(g_in, 16)

            def pooling(l):
                step = CH * (CH + 1) // 2 + 2 * CH
                n = l * step

                def chain(ins, n):
                    ins.then_inc(pool_step, 1)
                    pool.wait_ge(pool_step, n)

                pool.wait_ge(conv_v, 2 * (l + 1))
                for g in range(CH):
                    pool.wait_ge(chan_out, 2 * l + g // 2 + 1)
                    if g:
                        pool.wait_ge(pooled_ready, CH * l + g)
                    src, w = upool[:, g, :], 1
                    for k in range(g + 1):
                        dst = wsum[:, k % 2, :]
                        n += 1
                        chain(pool.tensor_tensor(dst[:, 16:], src[:, 16:], src[:, 16 - w:16 - w + SEQ], ALU.add), n)
                        src, w = dst, 2 * w
                    n += 1
                    chain(pool.tensor_scalar(wsum[:, (g + 1) % 2, 16:], src[:, 16:], 1.0 / w, None, ALU.mult), n)
                    n += 1
                    mean = wsum[:, (g + 1) % 2, :]
                    chain(pool.tensor_tensor(mean[:, 16:15 + w], src[:, 16:15 + w], rcount[:, 0:w - 1],
                                             ALU.mult), n)
                    pool.tensor_tensor(pooled[:, g, :], mean[:, 16:], upool[:, g, 16:], ALU.subtract
                                       ).then_inc(pooled_ready, 1)

            layer_loads(0)
            pool.wait_ge(rcount_ready, 1)
            pool.dma_start(router_sb[:, :, :],
                           moe_router[0].rearrange("(k p) e -> p k e", p=P)).then_inc(small_in, 16)
            for l in range(DEPTH):
                for n in range(3):
                    if n == 1:
                        pooling(l)
                    rms(3 * l + n)
                    if l == 0 and n == 1:
                        layer_loads(1)
                        pool.wait_ge(pooled_ready, CH)
                        pool.dma_start(p_sb, p[1, 0].rearrange("(b p) n -> p b n", p=P)).then_inc(p_in[1], 16)
            rms(6)

        @block.scalar
        def _(act):
            def split_hi(t, i=0, per=0, stream=1):
                land, hi, _, used = STREAMS[stream]
                visits = BODY_TILES // RAW if per else 0
                act.wait_ge(land[t % RAW], 32 * (t // RAW + 1) + i * (32 * visits))
                if t >= SPLIT:
                    act.wait_ge(used, t - SPLIT + 1 + i * per)
                act.activation(split[:, t % SPLIT, 0, :], raw[:, t % RAW, :], ACT.Copy).then_inc(hi, 1)

            def turn_hi(n, places=None):
                for at, (b, half) in enumerate(turn_order(n)):
                    if places is None or at in places:
                        act.wait_ge(turned, 4 * n + at + 1)
                        act.activation(hT[:, 0, 4 * half:4 * half + 4, b * P:(b + 1) * P],
                                       ps[:, turn_bank(b, half), :].rearrange("p (k n) -> p k n", k=4),
                                       ACT.Copy).then_inc(hT_hi, 1)

            def mean_square(b, ready, count):
                act.wait_ge(ready, count)
                act.activation(Y[:, b, :], X[:, b, :], ACT.Square, scale=D ** -0.5,
                               accum_out=ms[:, b:b + 1]).then_inc(ms_ready, 1)

            def p_hi(l, bank):
                act.wait_ge(p_turned, l + 1)
                act.activation(pT[:, 0], ps[:, bank, :].rearrange("p (k n) -> p k n", k=2), ACT.Copy
                               ).then_inc(pT_hi, 1)

            def softmax_exp(l, u):
                nh, n = (4, P) if u < 2 else (2, SEQ)
                h0 = 4 * u if u < 2 else 2 * (u - 2)
                act.wait_ge(masked, 6 * l + u + 1)
                for h in range(nh):
                    s = scores_of(u)[:, h * n:(h + 1) * n]
                    act.activation(s, s, ACT.Exp, bias=nmx[:, u % 2, h:h + 1],
                                   accum_out=den[:, u % 2, h:h + 1])
                act.activation(esk[:, u % 2, 0:nh], esk[:, u % 2, 0:nh], ACT.Exp).then_inc(exped, 1)

            def body(s, nb, moe, t0, i, last_split):
                stream = 2 if s == 2 else 1
                aT = aT_moe if moe else aT_dense
                j = 0
                for step, kind, f in body_schedule(moe):
                    if step == "swiglu" or (step == "tile" and kind == "b"):
                        for b in swiglu_blocks(moe, kind, f):
                            wait_product(act, b, nb - 1, gu_done, f + 1 + i * BODY_F,
                                         t0 + (3 * f if f else 1), i, BODY_TILES, stream)
                            bank = 4 + (f % 2 if moe else b)
                            act.activation(sg[:, b, 0:256], ps[:, bank, 0:256], ACT.Silu
                                           ).then_inc(silu_ready[s], 1)
                    if step == "tile":
                        if j + 2 < BODY_TILES + last_split:
                            split_hi(t0 + j + 2, i, BODY_TILES, stream)
                        j += 1
                    elif step == "turn":
                        act.wait_ge(a_turned[s], f + 1 + i * BODY_F)
                        act.activation(aT[:, f % 2, 0], ps[:, 6 + f % 2, 0:nb * SEQ].rearrange(
                            "p (k n) -> p k n", k=2), ACT.Copy).then_inc(aT_hi[s], 1)
                    elif step == "route":
                        act.wait_ge(route_done[s], 1 + i)
                        act.activation(GT[:, :], ps[:, 2, 0:SEQ], ACT.Copy).then_inc(gT_ready[s], 1)
                    elif step == "gather":
                        gather_hi(s, 2 + i * 2)
                    elif step == "close" and moe:
                        act.wait_ge(STREAMS[stream][3], t0 + BODY_TILES + i * BODY_TILES)
                        act.wait_ge(ws_ready[s], 1 + i)
                        for nh in range(2):
                            act.activation(ye[:, 0, nh * 512:(nh + 1) * 512], ps[:, nh, :], ACT.Copy,
                                           scale=w_slot[:, 0:1]).then_inc(ye_hi[s], 1)

            def gather_hi(s, n):
                for half in range(2):
                    act.wait_ge(gathered[s], n + half + 1)
                    act.activation(xe[:, 0, 4 * half:4 * half + 4, :],
                                   ps[:, 2 + half, :].rearrange("p (k n) -> p k n", k=4), ACT.Copy
                                   ).then_inc(xe_hi[s], 1)

            def experts(s, t0):
                gather_hi(s, 0)
                if s == 2:
                    act.wait_ge(tile_used, LAYER_T0[1] + T_PLE[1] + 1)
                    act.sem_inc(hi_ready2, BODY_TILES)
                    for t in range(2):
                        split_hi(BODY_TILES + t, stream=2)
                with act.Fori(0, EXPERTS - 1) as e:
                    body(s, 1, True, t0, e, 2)
                body(s, 1, True, t0, EXPERTS - 1, 1 if s == 1 else 0)

            act.dma_start(pos_i[:, :], positions[0].rearrange("(b p) -> p b", p=P),
                          allow_slow_non_contiguous=True).then_inc(pos_in, 16)
            act.dma_start(freq[:, :], on_all(inv_freq)).then_inc(pos_in, 16)
            act.dma_start(g_row[:, :], on_all(gains[0])).then_inc(g_first, 16)
            act.dma_start(p_sb, p[0, 0].rearrange("(b p) n -> p b n", p=P)).then_inc(p_in[0], 16)
            for b in range(NB):
                mean_square(b, x_in[b], 16)
            p_hi(0, 0)
            turn_hi(0)
            split_hi(0)
            act.wait_ge(rope_ang, 1)
            act.activation(sin2[:, :, 1, :], ang[:, 0], ACT.Sin).then_inc(rope_ready, 1)
            act.activation(sin2[:, :, 0, :], ang[:, 0], ACT.Sin, scale=-1.0).then_inc(rope_ready, 1)
            act.activation(cos1[:, :, :], ang[:, 1], ACT.Sin).then_inc(rope_ready, 1)
            split_hi(1)
            for l in range(DEPTH):
                t0 = LAYER_T0[l]
                for j in range(T_CHAN):
                    split_hi(t0 + j + 2)
                for b in range(NB):
                    wait_product(act, b, NB - 1, kv_done, l + 1, t0 + 2)
                    act.activation(v_sb[:, b, :], ps[:, b, P:2 * P], ACT.Copy).then_inc(v_ready, 1)
                for j in range(8):
                    split_hi(t0 + T_CHAN + j + 2)
                    if j < 2:
                        act.wait_ge(tile_used, t0 + T_CHAN + j + 1)
                        act.activation(c_sb[:, 2 * j:2 * j + 2, :],
                                       ps[:, 2 + j, :].rearrange("p (c n) -> p c n", c=2), ACT.Copy
                                       ).then_inc(c_copied, 1)
                    if j in (4, 5):
                        act.wait_ge(conv_y, 2 * l + j - 3)
                        act.activation(brv[:, 0, 2 * (j - 4):2 * (j - 4) + 2, :], ctmp, ACT.Copy
                                       ).then_inc(conv_hi, 1)
                    if j == 5:
                        act.wait_ge(qk_turned, 3 * l + 3)
                        for c in range(2):
                            act.activation(qT[:, 2 * c:2 * c + 2, :],
                                           ps[:, 6 + c, :].rearrange("p (c n) -> p c n", c=2), ACT.Copy
                                           ).then_inc(qT_ready, 1)
                    if j in (6, 7):
                        act.wait_ge(tile_used, t0 + T_CHAN + j + 1)
                        act.activation(upool[:, 2 * (j - 6):2 * (j - 6) + 2, 16:],
                                       ps[:, j - 2, :].rearrange("p (c n) -> p c n", c=2), ACT.Copy
                                       ).then_inc(chan_out, 1)
                for c in range(6):
                    for step in range(3):
                        split_hi(t0 + T_GATE + 3 * c + step + 2)
                        at = 3 * c + step
                        if 0 <= at - ATT - 2 < 6:
                            softmax_exp(l, at - ATT - 2)
                        if at == MIX + 1:
                            act.wait_ge(mixed_done, l + 1)
                            for g in range(CH):
                                ins = act.activation(
                                    brv[:, 2, g, :], ps[:, 2 + g // 2, g % 2 * SEQ:(g % 2 + 1) * SEQ],
                                    ACT.Copy, scale=pscale_sb[:, g:g + 1])
                            ins.then_inc(pool_hi, 1)
                        if step == 1:
                            for b in range(NB):
                                wait_product(act, b, NB - 1, gate_done, 6 * l + c + 1,
                                             t0 + T_GATE + 3 * c + 1)
                                if NB * c + b >= NB:
                                    act.wait_ge(merged, 12 * l + NB * (c - 1) + b + 1)
                                act.activation(sg[:, b, :], ps[:, 4 + b, :], ACT.Sigmoid
                                               ).then_inc(sig_ready, 1)
                        if at == ATT_OUT:
                            act.wait_ge(att_done, l + 1)
                            for h in range(2):
                                act.activation(brv[:, 4, 2 * h:2 * h + 2, :],
                                               ps[:, 2 + h, :].rearrange("p (c n) -> p c n", c=2), ACT.Copy
                                               ).then_inc(att_hi, 1)
                turn_hi(4 * l + 1)
                for i in range(3):
                    split_hi(t0 + T_OUT + i + 2)
                mean_square(0, x_out, NB * l + 1)
                turn_hi(4 * l + 2, (0, 1))
                split_hi(t0 + T_OUT + 5)
                mean_square(1, x_out, NB * l + 2)
                turn_hi(4 * l + 2, (2, 3))
                if l == 0:
                    with act.Fori(0, FFN_BODIES[0]) as i:
                        body(0, NB, False, t0 + T_FFN, i, 2)
                    added, seen = x_ffn[0], 1 + NB * (FFN_BODIES[0] - 1)
                else:
                    act.wait_ge(y_ready, NB * 5)
                    act.activation(yn[:, 0], Y[:, :, :], ACT.Copy).then_inc(yn_hi, 1)
                    act.wait_ge(sel_ready, 2)
                    act.activation(wts[:, :, 1:2], wts[:, :, 0:1], ACT.Exp).then_inc(route_step, 1)
                    experts(1, t0 + T_FFN)
                    added, seen = x_ffn[1], 1 + NB * EXPERTS
                u = t0 + T_PLE[l]

                def proj_out_of(b):
                    wait_product(act, b, NB - 1, proj_done, l + 1, u)
                    act.activation(halves(M[:, b, :]), two_banks(PROJ_BANKS[l][b]), ACT.Copy
                                   ).then_inc(proj_out, 1)

                if l:
                    proj_out_of(0)
                    proj_out_of(1)
                    act.wait_ge(routed, 1)
                    more = act.value_load(more_i[0:1, 0:1], min_val=0, max_val=1)
                    with act.If(more > 0):
                        experts(2, BODY_TILES)
                        act.wait_ge(tile_used2, (EXPERTS + 1) * BODY_TILES)
                        act.wait_ge(x_ffn[2], 1 + NB * (EXPERTS + 1))
                mean_square(0, added, seen + 1)
                if l:
                    split_hi(u + 1)
                split_hi(u + 2)
                mean_square(1, added, seen + 2)
                if l == 0:
                    proj_out_of(0)
                turn_hi(4 * l + 3, (0, 1))
                if l == 0:
                    proj_out_of(1)
                turn_hi(4 * l + 3, (2, 3))
                split_hi(u + 3)
                split_hi(u + 4)
                if l == 0:
                    p_hi(1, 6)
                    split_hi(u + 5)
                for b in range(NB):
                    wait_product(act, b, NB - 1, pg_done, l + 1, u + 4)
                    if b:
                        act.wait_ge(x_ple, NB * l + b)
                    act.activation(sg[:, :, :], two_banks(2 * b), ACT.Sigmoid).then_inc(psig, 1)
                    mean_square(b, x_ple, NB * l + b + 1)
                    if l == 0:
                        turn_hi(4, (2 * b, 2 * b + 1))
                        if b == 0:
                            split_hi(u + 6)

        @block.vector
        def _(dve):
            done = [0]

            def chain(ins):
                done[0] += 1
                ins.then_inc(dve_step, 1)
                dve.wait_ge(dve_step, done[0])

            def split_lo(t, i=0, per=0, stream=1):
                _, hi, lo, _ = STREAMS[stream]
                dve.wait_ge(hi, t + 1 + i * per)
                dve.tensor_tensor(split[:, t % SPLIT, 1, :], raw[:, t % RAW, :],
                                  split[:, t % SPLIT, 0, :].bitcast(F32), ALU.subtract).then_inc(lo, 1)

            def norm(n, b):
                if n:
                    dve.wait_ge(g_in, 16 * n)
                else:
                    dve.wait_ge(g_first, 16)
                dve.wait_ge(rstd_ready, NB * n + b + 1)
                dve.scalar_tensor_tensor(out=Y[:, b, :], in0=X[:, b, :], scalar=rstd[:, b:b + 1],
                                         in1=g_row[:, :], op0=ALU.mult, op1=ALU.mult).then_inc(y_ready, 1)

            def turn_lo(n, places=None):
                for at, (b, half) in enumerate(turn_order(n)):
                    if places is None or at in places:
                        dve.wait_ge(hT_hi, 4 * n + at + 1)
                        ks = slice(4 * half, 4 * half + 4)
                        dve.tensor_tensor(hT[:, 1, ks, b * P:(b + 1) * P],
                                          ps[:, turn_bank(b, half), :].rearrange("p (k n) -> p k n", k=4),
                                          hT[:, 0, ks, b * P:(b + 1) * P].bitcast(F32), ALU.subtract
                                          ).then_inc(hT_lo, 1)

            def p_lo(l, bank):
                dve.wait_ge(pT_hi, l + 1)
                dve.tensor_tensor(pT[:, 1], ps[:, bank, :].rearrange("p (k n) -> p k n", k=2),
                                  pT[:, 0].bitcast(F32), ALU.subtract).then_inc(pT_lo, 1)

            def add_to_x(b, b0, signal):
                dve.tensor_tensor(halves(X[:, b, :]), two_banks(b0), halves(X[:, b, :]), ALU.add
                                  ).then_inc(signal, 1)

            def rotate(src, dst, nh, b, nth):
                if nth:
                    dve.wait_ge(rot_ready, nth)
                s4 = src.rearrange("p (h s d) -> p h s d", h=nh, s=2)
                n = nh * HD
                t1 = tmp[:, 0:n].rearrange("p (h s d) -> p h s d", h=nh, s=2)
                t2 = tmp[:, 512:512 + n].rearrange("p (h s d) -> p h s d", h=nh, s=2)
                for s in range(2):
                    cosb = cos1[:, b, :].unsqueeze(1).broadcast_to([P, nh, HALF])
                    sinb = sin2[:, b, s, :].unsqueeze(1).broadcast_to([P, nh, HALF])
                    dve.tensor_tensor(t1[:, :, s, :], s4[:, :, s, :], cosb, ALU.mult)
                    ins = dve.tensor_tensor(t2[:, :, s, :], s4[:, :, 1 - s, :], sinb, ALU.mult)
                chain(ins)
                for d in dst:
                    ins = dve.tensor_tensor(d, t1.rearrange("p h s d -> p h (s d)"),
                                            t2.rearrange("p h s d -> p h (s d)"), ALU.add)
                ins.then_inc(rot_ready, 1)

            def take_probs(l, u):
                dve.wait_ge(pr_turned, 6 * l + u + 1)
                dve.tensor_copy(prT[:, :, :], ps[:, 7, :].rearrange("p (c n) -> p c n", c=4)
                                ).then_inc(prT_ready, 1)

            def mask_scores(l, u):
                nh, n = (4, P) if u < 2 else (2, SEQ)
                h0 = 4 * u if u < 2 else 2 * (u - 2)
                dve.wait_ge(s_done, 6 * l + u + 1)
                if u > 2:
                    dve.wait_ge(pr_turned, 6 * l + u - 2)
                s3 = scores_of(u).rearrange("p (h n) -> p h n", h=nh)
                for h in range(nh):
                    ins = dve.scalar_tensor_tensor(out=s3[:, h, :], in0=ps[:, 6, h * n:(h + 1) * n],
                                                   scalar=HD ** -0.5, in1=mask[:, SEQ - n:SEQ],
                                                   op0=ALU.mult, op1=ALU.add)
                chain(ins)
                chain(dve.tensor_reduce(mx[:, 0:nh], s3, AX.X, ALU.max))
                chain(dve.tensor_tensor(mx[:, 0:nh], mx[:, 0:nh], sinks_sb[:, h0:h0 + nh], ALU.max))
                dve.tensor_scalar(nmx[:, u % 2, 0:nh], mx[:, 0:nh], -1.0, None, ALU.mult)
                dve.tensor_tensor(esk[:, u % 2, 0:nh], sinks_sb[:, h0:h0 + nh], mx[:, 0:nh], ALU.subtract
                                  ).then_inc(masked, 1)

            def scale_probs(l, u):
                nh = 4 if u < 2 else 2
                dve.wait_ge(exped, 6 * l + u + 1)
                chain(dve.tensor_tensor(rden[:, 0:nh], den[:, u % 2, 0:nh], esk[:, u % 2, 0:nh], ALU.add))
                chain(dve.reciprocal(rden[:, 0:nh], rden[:, 0:nh]))
                s3 = scores_of(u).rearrange("p (h n) -> p h n", h=nh)
                for h in range(nh):
                    ins = dve.tensor_scalar(s3[:, h, :], s3[:, h, :], rden[:, h:h + 1], None, ALU.mult)
                ins.then_inc(probs, 1)

            def build_g(s, col, signal):
                for b in range(NB):
                    ins = dve.tensor_scalar(G[:, b, :], slot_row[:, :], rank[:, b, bass.ds(col, 1)], None,
                                            ALU.is_equal)
                ins.then_inc(signal, 1)

            def gather_lo(s, n):
                for half in range(2):
                    dve.wait_ge(xe_hi[s], n + half + 1)
                    ks = slice(4 * half, 4 * half + 4)
                    dve.tensor_tensor(xe[:, 1, ks, :], ps[:, 2 + half, :].rearrange("p (k n) -> p k n", k=4),
                                      xe[:, 0, ks, :].bitcast(F32), ALU.subtract).then_inc(xe_lo[s], 1)

            def body(s, nb, moe, t0, i, last_split):
                stream = 2 if s == 2 else 1
                aT = aT_moe if moe else aT_dense
                j = 0
                for step, kind, f in body_schedule(moe):
                    if step == "swiglu" or (step == "tile" and kind == "b"):
                        for b in swiglu_blocks(moe, kind, f):
                            dve.wait_ge(silu_ready[s], nb * f + b + 1 + i * (nb * BODY_F))
                            bank = 4 + (f % 2 if moe else b)
                            dve.tensor_tensor(tmp[:, b * 256:(b + 1) * 256], ps[:, bank, 256:512],
                                              sg[:, b, 0:256], ALU.mult).then_inc(act_ready[s], 1)
                    if step == "tile":
                        if j + 2 < BODY_TILES + last_split:
                            split_lo(t0 + j + 2, i, BODY_TILES, stream)
                        j += 1
                    elif step == "turn":
                        dve.wait_ge(aT_hi[s], f + 1 + i * BODY_F)
                        dve.tensor_tensor(aT[:, f % 2, 1], ps[:, 6 + f % 2, 0:nb * SEQ].rearrange(
                            "p (k n) -> p k n", k=2), aT[:, f % 2, 0].bitcast(F32), ALU.subtract
                            ).then_inc(aT_lo[s], 1)
                    elif step == "scatter":
                        dve.wait_ge(scattered[s], f + 1 + i * NB)
                        add_to_x(f, SCATTER_BANKS[f], x_ffn[s])
                    elif step == "route":
                        dve.wait_ge(gT_ready[s], 2 + i)
                        dve.tensor_copy(w_slot[:, :], ps[:, 2, SEQ:SEQ + 1]).then_inc(ws_ready[s], 1)
                        build_g(s, i + 1 + (EXPERTS if s == 2 else 0), g_ready[s])
                    elif step == "gather":
                        gather_lo(s, 2 + i * 2)
                    elif step == "close" and moe:
                        for nh in range(2):
                            dve.wait_ge(ye_hi[s], nh + 1 + i * 2)
                            cols = slice(nh * 512, (nh + 1) * 512)
                            dve.scalar_tensor_tensor(out=ye[:, 1, cols], in0=ps[:, nh, :],
                                                     scalar=w_slot[:, 0:1], in1=ye[:, 0, cols].bitcast(F32),
                                                     op0=ALU.mult, op1=ALU.subtract).then_inc(ye_lo[s], 1)
                    elif step == "close":
                        for b in range(nb):
                            wait_product(dve, b, nb - 1, down_done, 1 + i, t0 + BODY_TILES - 1, i, BODY_TILES)
                            add_to_x(b, 2 * b, x_ffn[s])

            def experts(s, t0):
                dve.sem_inc(x_ffn[s], 1)
                dve.memset(ye[:, :, :].bitcast(U32), 0).then_inc(ye_lo[s], 2)
                dve.memset(GT[:, :].bitcast(U32), 0).then_inc(gT_ready[s], 1)
                if s == 2:
                    build_g(s, EXPERTS, g_ready[s])
                gather_lo(s, 0)
                if s == 2:
                    dve.sem_inc(lo_ready2, BODY_TILES)
                    for t in range(2):
                        split_lo(BODY_TILES + t, stream=2)
                with dve.Fori(0, EXPERTS - 1) as e:
                    body(s, 1, True, t0, e, 2)
                body(s, 1, True, t0, EXPERTS - 1, 1 if s == 1 else 0)
                for b in range(NB):
                    dve.wait_ge(scattered[s], EXPERTS * NB + b + 1)
                    add_to_x(b, SCATTER_BANKS[b], x_ffn[s])

            PI = float(np.pi)

            def parts(value, bits, count):
                got = []
                for _ in range(count):
                    e = int(np.floor(np.log2(abs(value))))
                    q = 2.0 ** (e - bits + 1)
                    got.append(float(np.floor(value / q) * q))
                    value -= got[-1]
                return got

            dve.wait_ge(pos_in, 32)
            chain(dve.tensor_copy(pos_f[:, :], pos_i[:, :]))
            for b in range(NB):
                ins = dve.tensor_scalar(ang[:, 0, b, :], freq[:, :], pos_f[:, b:b + 1], None, ALU.mult)
            chain(ins)
            for period, bits, count in ((4096 * 2 * PI, 7, 6), (2 * PI, 11, 4)):
                chain(dve.tensor_scalar(turns[:, 0], ang[:, 0], 1.0 / period, 12582912.0, ALU.mult, ALU.add))
                chain(dve.tensor_scalar(turns[:, 0], turns[:, 0], -12582912.0, None, ALU.add))
                for part in parts(period, bits, count):
                    chain(dve.scalar_tensor_tensor(out=ang[:, 0], in0=turns[:, 0], scalar=-part, in1=ang[:, 0],
                                                   op0=ALU.mult, op1=ALU.add))
            chain(dve.tensor_scalar(ang[:, 1], ang[:, 0], PI / 2, None, ALU.add))
            chain(dve.tensor_scalar(turns[:, 1], ang[:, 1], PI, -2 * PI, ALU.is_gt, ALU.mult))
            chain(dve.tensor_tensor(ang[:, 1], ang[:, 1], turns[:, 1], ALU.add))
            dve.tensor_scalar(ang[:, :, :, :], ang[:, :, :, :], 3.1415925, -3.1415925, ALU.min, ALU.max
                              ).then_inc(rope_ang, 1)
            dve.wait_ge(consts, 9)
            chain(dve.tensor_scalar(rcount[:, :], slot_row[:, 0:16], 1.0, None, ALU.add))
            dve.reciprocal(rcount[:, :], rcount[:, :]).then_inc(rcount_ready, 1)
            for b in range(NB):
                norm(0, b)
            p_lo(0, 0)
            turn_lo(0)
            split_lo(0)
            split_lo(1)
            for l in range(DEPTH):
                t0 = LAYER_T0[l]
                for j in range(2):
                    split_lo(t0 + j + 2)
                if l == 0:
                    dve.wait_ge(rope_ready, 3)
                for b in range(NB):
                    wait_product(dve, b, NB - 1, q_done, l + 1, t0 + 1)
                    rotate(ps[:, 4 + b, :], [q_rot[:, b, :].rearrange("p (h d) -> p h d", h=HEADS)], HEADS, b, 4 * l + b)
                split_lo(t0 + 4)
                for b in range(NB):
                    wait_product(dve, b, NB - 1, kv_done, l + 1, t0 + 2)
                    dve.wait_ge(v_ready, NB * l + b + 1)
                    rotate(ps[:, b, 0:P], [kdup[:, b, :, c, :] for c in range(2)], KV_HEADS, b,
                           4 * l + NB + b)
                chain(dve.memset(vpad[:, :, 0:2], 0.0))
                for j in range(8):
                    split_lo(t0 + T_CHAN + j + 2)
                    cs = slice(2 * (j % 2), 2 * (j % 2) + 2)
                    if j in (2, 3):
                        dve.wait_ge(tile_used, t0 + T_CHAN + j + 1)
                        dve.wait_ge(c_copied, 2 * l + j - 1)
                        dve.tensor_tensor(vpad[:, cs, 2:], ps[:, 4 + j, :].rearrange(
                            "p (c n) -> p c n", c=2), c_sb[:, cs, :], ALU.mult).then_inc(conv_v, 1)
                    if j in (4, 5):
                        dve.wait_ge(small_in, 16 + 96 * (l + 1))
                        dve.wait_ge(conv_v, 2 * l + j - 3)
                        for c in range(2):
                            ch = 2 * (j - 4) + c
                            chain(dve.tensor_scalar(cacc[:, c, :], vpad[:, ch, 0:SEQ], convw_sb[:, ch, 0:1],
                                                    None, ALU.mult))
                            for k in (1, 2):
                                chain(dve.scalar_tensor_tensor(
                                    out=cacc[:, c, :], in0=vpad[:, ch, k:k + SEQ],
                                    scalar=convw_sb[:, ch, k:k + 1], in1=cacc[:, c, :],
                                    op0=ALU.mult, op1=ALU.add))
                        dve.wait_ge(tile_used, t0 + T_CHAN + j + 1)
                        dve.tensor_tensor(ctmp, ps[:, j - 2, :].rearrange("p (c n) -> p c n", c=2), cacc,
                                          ALU.mult).then_inc(conv_y, 1)
                        dve.wait_ge(conv_hi, 2 * l + j - 3)
                        dve.tensor_tensor(brv[:, 1, cs, :], ctmp, brv[:, 0, cs, :].bitcast(F32),
                                          ALU.subtract).then_inc(conv_lo, 1)
                    if j == 5:
                        dve.wait_ge(qk_turned, 3 * l + 3)
                        for s in range(2):
                            half = slice(s * HD, (s + 1) * HD)
                            dve.tensor_copy(kT[half, :, s, :], ps[half, 0, :].rearrange(
                                "p (c n) -> p c n", c=2)).then_inc(kT_ready, 1)
                for c in range(6):
                    for step in range(3):
                        split_lo(t0 + T_GATE + 3 * c + step + 2)
                        at = 3 * c + step
                        for stage, late in ((take_probs, 4), (scale_probs, 3), (mask_scores, 1)):
                            if 0 <= at - ATT - late < 6:
                                stage(l, at - ATT - late)
                        if at == MIX + 1:
                            dve.wait_ge(pool_hi, l + 1)
                            for g in range(CH):
                                ins = dve.scalar_tensor_tensor(
                                    out=brv[:, 3, g, :], in0=ps[:, 2 + g // 2, g % 2 * SEQ:(g % 2 + 1) * SEQ],
                                    scalar=pscale_sb[:, g:g + 1], in1=brv[:, 2, g, :].bitcast(F32),
                                    op0=ALU.mult, op1=ALU.subtract)
                            ins.then_inc(pool_lo, 2)
                        if step == 2:
                            r, nh = c // 2, c % 2
                            for b in range(NB):
                                dve.wait_ge(sig_ready, 12 * l + NB * c + b + 1)
                                wait_product(dve, b, NB - 1, branch_done, 6 * l + c + 1,
                                             t0 + T_GATE + 3 * c + 2)
                                m = M[:, b, nh * 512:(nh + 1) * 512]
                                if c == 2:
                                    dve.wait_ge(pr_turned, 6 * l + 4 + b)
                                if r == 0:
                                    dve.tensor_tensor(m, ps[:, b, :], sg[:, b, :], ALU.mult
                                                      ).then_inc(merged, 1)
                                else:
                                    dve.wait_ge(merged, 12 * l + NB * (c - 1) + b + 1)
                                    chain(dve.tensor_tensor(tmp[:, b * 512:(b + 1) * 512], ps[:, b, :],
                                                            sg[:, b, :], ALU.mult))
                                    dve.tensor_tensor(m, m, tmp[:, b * 512:(b + 1) * 512], ALU.add
                                                      ).then_inc(merged, 1)
                        if at == ATT_OUT:
                            for h in range(2):
                                dve.wait_ge(att_hi, 2 * l + h + 1)
                                dve.tensor_tensor(brv[:, 5, 2 * h:2 * h + 2, :],
                                                  ps[:, 2 + h, :].rearrange("p (c n) -> p c n", c=2),
                                                  brv[:, 4, 2 * h:2 * h + 2, :].bitcast(F32), ALU.subtract
                                                  ).then_inc(att_lo, 1)
                turn_lo(4 * l + 1)
                for i in range(3):
                    split_lo(t0 + T_OUT + i + 2)
                dve.wait_ge(out_done, l + 1)
                add_to_x(0, 0, x_out)
                norm(3 * l + 1, 0)
                turn_lo(4 * l + 2, (0, 1))
                dve.wait_ge(tile_used, t0 + T_OUT + 4)
                add_to_x(1, 2, x_out)
                split_lo(t0 + T_OUT + 5)
                norm(3 * l + 1, 1)
                turn_lo(4 * l + 2, (2, 3))
                if l == 0:
                    dve.sem_inc(x_ffn[0], 1)
                    with dve.Fori(0, FFN_BODIES[0]) as i:
                        body(0, NB, False, t0 + T_FFN, i, 2)
                    dve.wait_ge(x_ffn[0], 1 + NB * FFN_BODIES[0])
                else:
                    dve.wait_ge(yn_hi, 1)
                    dve.tensor_tensor(yn[:, 1], Y[:, :, :], yn[:, 0].bitcast(F32), ALU.subtract
                                      ).then_inc(yn_lo, 1)
                    dve.wait_ge(logit_done, NB)
                    chain(dve.tensor_copy(logit[:, :, :], ps[:, 0:NB, 0:EXPERTS]))
                    for b in range(NB):
                        ins = dve.max(top[:, b, :], logit[:, b, :])
                    chain(ins)
                    for b in range(NB):
                        ins = dve.max_index(topi[:, b, :], top[:, b, :], logit[:, b, :])
                    chain(ins)
                    chain(dve.tensor_copy(topf[:, :, :], topi[:, :, :]))
                    for b in range(NB):
                        for k in range(2):
                            ins = dve.tensor_scalar(hot[:, b, k, :], slot_row[:, 0:EXPERTS],
                                                    topf[:, b, k:k + 1], None, ALU.is_equal)
                    chain(ins)
                    dve.tensor_tensor(sel[:, :, :], hot[:, :, 0, :], hot[:, :, 1, :], ALU.add
                                      ).then_inc(sel_ready, 1)
                    dve.tensor_tensor(wts[:, :, 0:1], top[:, :, 1:2], top[:, :, 0:1], ALU.subtract
                                      ).then_inc(sel_ready, 1)
                    dve.memset(rank[:, :, 2 * EXPERTS:], -1.0)
                    dve.wait_ge(rank_done, 1)
                    chain(dve.scalar_tensor_tensor(out=rank[:, :, 0:EXPERTS],
                                                   in0=ps[:, 6, 0:16].rearrange("p (b e) -> p b e", b=NB),
                                                   scalar=1.0, in1=sel[:, :, :], op0=ALU.add, op1=ALU.mult))
                    chain(dve.tensor_scalar(rank[:, :, 0:EXPERTS], rank[:, :, 0:EXPERTS], -1.0, None, ALU.add))
                    build_g(1, 0, g_ready[1])
                    chain(dve.tensor_scalar(rank[:, :, EXPERTS:2 * EXPERTS], rank[:, :, 0:EXPERTS],
                                            -float(P), None, ALU.add))
                    chain(dve.tensor_copy(load[:, :], ps[:, 6, 16:24]))
                    chain(dve.tensor_reduce(most[:, 0:1], load[:, :], AX.X, ALU.max))
                    chain(dve.tensor_scalar(most[:, 1:2], most[:, 0:1], float(P), None, ALU.is_gt))
                    dve.tensor_copy(more_i[:, :], most[:, 1:2]).then_inc(routed, 1)
                    dve.wait_ge(route_step, 1)
                    chain(dve.tensor_scalar(wts[:, :, 2:3], wts[:, :, 1:2], 1.0, None, ALU.add))
                    chain(dve.reciprocal(wts[:, :, 2:3], wts[:, :, 2:3]))
                    chain(dve.tensor_tensor(wts[:, :, 3:4], wts[:, :, 1:2], wts[:, :, 2:3], ALU.mult))
                    for b in range(NB):
                        chain(dve.tensor_scalar(comb[:, b, 0:EXPERTS], hot[:, b, 0, :], wts[:, b, 2:3], None,
                                                ALU.mult))
                        chain(dve.scalar_tensor_tensor(out=comb[:, b, 0:EXPERTS], in0=hot[:, b, 1, :],
                                                       scalar=wts[:, b, 3:4], in1=comb[:, b, 0:EXPERTS],
                                                       op0=ALU.mult, op1=ALU.add))
                    chain(dve.tensor_copy(comb[:, :, EXPERTS:], comb[:, :, 0:EXPERTS]))
                    experts(1, t0 + T_FFN)
                    more = dve.value_load(more_i[0:1, 0:1], min_val=0, max_val=1)
                    with dve.If(more > 0):
                        experts(2, BODY_TILES)
                        dve.wait_ge(tile_used2, (EXPERTS + 1) * BODY_TILES)
                        dve.wait_ge(x_ffn[2], 1 + NB * (EXPERTS + 1))
                    dve.wait_ge(x_ffn[1], 1 + NB * (EXPERTS + 1))
                u = t0 + T_PLE[l]
                norm(3 * l + 2, 0)
                if l:
                    split_lo(u + 1)
                split_lo(u + 2)
                norm(3 * l + 2, 1)
                turn_lo(4 * l + 3)
                split_lo(u + 3)
                split_lo(u + 4)
                if l == 0:
                    p_lo(1, 6)
                    split_lo(u + 5)
                for b in range(NB):
                    dve.wait_ge(psig, NB * l + b + 1)
                    dve.wait_ge(proj_out, NB * l + b + 1)
                    if b:
                        dve.wait_ge(x_ple, NB * l + b)
                    chain(dve.tensor_tensor(halves(tmp[:, :]), sg[:, :, :], halves(M[:, b, :]), ALU.mult))
                    dve.tensor_tensor(X[:, b, :], X[:, b, :], tmp[:, :], ALU.add).then_inc(x_ple, 1)
                    norm(3 * (l + 1), b)
                    if l == 0:
                        turn_lo(4, (2 * b, 2 * b + 1))
                        if b == 0:
                            split_lo(u + 6)

        @block.tensor
        def _(pe):
            def product(dst, lh, rh, start, stop):
                pe.matmul(dst, lh[0], rh[0], start=start, stop=False)
                pe.matmul(dst, lh[0], rh[1], start=False, stop=False)
                return pe.matmul(dst, lh[1], rh[0], start=False, stop=stop)

            def pair(buf, *index):
                return [buf[(slice(None), s) + index] for s in range(2)]

            def tile_pair(t, n, k, cols):
                return [slot(t, s, n)[:, k, cols] for s in range(2)]

            def turn(n, src, ready, places=None):
                for at, (b, half) in enumerate(turn_order(n)):
                    if places is None or at in places:
                        pe.wait_ge(*ready(b))
                        for k in range(4):
                            ins = pe.transpose(ps[:, turn_bank(b, half), k * P:(k + 1) * P],
                                               src[:, b, (4 * half + k) * P:(4 * half + k + 1) * P],
                                               ident[:, :])
                        ins.then_inc(turned, 1)

            def turn_p(l, bank):
                pe.wait_ge(p_in[l], 16)
                for k in range(2):
                    for b in range(NB):
                        ins = pe.transpose(ps[:, bank, k * SEQ + b * P:k * SEQ + (b + 1) * P],
                                           p_sb[:, b, k * P:(k + 1) * P], ident[:, :])
                ins.then_inc(p_turned, 1)

            def tokens(b):
                return slice(b * P, (b + 1) * P)

            def wide(t, tiles, n_tiles, lhs, banks, ready, done=None, between=None, blocks=range(NB)):
                for b in blocks:
                    for condition in ready(b):
                        pe.wait_ge(*condition)
                    for i in tiles:
                        if b == 0:
                            pe.wait_ge(lo_ready, t + i + 1)
                        for nh in range(2):
                            for k in range(2):
                                ins = product(ps[:, banks[b] + nh, :], pair(lhs, 2 * i + k, tokens(b)),
                                              tile_pair(t + i, D, k, slice(nh * 512, (nh + 1) * 512)),
                                              i == 0 and k == 0, i == n_tiles - 1 and k == 1)
                                if between and b == NB - 1 and i == tiles[-1] and nh == 1 and k == 0:
                                    between()
                        if b == NB - 1:
                            ins.then_inc(tile_used, 1)
                    if b == 0 and done is not None:
                        ins.then_inc(done, 1)

            def att_scores(l, u):
                b = 0 if u < 2 else 1
                nh, n = (4, P) if u < 2 else (2, SEQ)
                h0 = 4 * u if u < 2 else 2 * (u - 2)
                if u == 0:
                    pe.wait_ge(qT_ready, 2 * l + 2)
                    pe.wait_ge(kT_ready, 2 * (l + 1))
                if u:
                    pe.wait_ge(masked, 6 * l + u)
                for i in range(nh):
                    h = h0 + i
                    ins = pe.matmul(ps[:, 6, i * n:(i + 1) * n], qT[:, h // 2, tokens(b)],
                                    kT[:, h // (HEADS // KV_HEADS), h % 2, 0:n], start=True, stop=True)
                ins.then_inc(s_done, 1)

            def att_turn(l, u):
                pe.wait_ge(probs, 6 * l + u + 1)
                if u:
                    pe.wait_ge(prT_ready, 6 * l + u)
                for i in range(4):
                    ins = pe.transpose(ps[:, 7, i * P:(i + 1) * P], scores_of(u)[:, i * P:(i + 1) * P],
                                       ident[:, :])
                ins.then_inc(pr_turned, 1)

            def att_values(l, u):
                b = 0 if u < 2 else 1
                h0 = 4 * u if u < 2 else 2 * (u - 2)
                pe.wait_ge(prT_ready, 6 * l + u + 1)
                if u == 0:
                    pe.wait_ge(v_ready, NB * (l + 1))
                    pe.wait_ge(pool_lo, 2 * (l + 1))
                per = b + 1
                for i in range(4):
                    h = h0 + i // per
                    kv = h // (HEADS // KV_HEADS)
                    c = h // 2
                    rows = slice(h % 2 * HD, (h % 2 + 1) * HD)
                    ins = pe.matmul(ps[rows, 2 + c // 2, (c % 2) * SEQ + b * P:(c % 2) * SEQ + (b + 1) * P],
                                    v_sb[:, i % per, kv * HD:(kv + 1) * HD], prT[:, i, :],
                                    start=i % per == 0, stop=i % per == per - 1)
                if u == 5:
                    ins.then_inc(att_done, 1)

            def first_chunk(t0, i):
                for b in range(NB):
                    pe.wait_ge(hT_lo, 8 + 2 * (b + 1))
                    for half in range(2):
                        if b == 0:
                            pe.wait_ge(lo_ready, t0 + half + 1 + i * BODY_TILES)
                        for k in range(4):
                            ins = product(ps[:, 4 + b, :], pair(hT, 4 * half + k, tokens(b)),
                                          tile_pair(t0 + half, 512, k, slice(0, 512)),
                                          half + k == 0, half == 1 and k == 3)
                            if b == 0 and half == 1 and k == 2:
                                with pe.If(i < 1):
                                    turn(2, Y, lambda b: (y_ready, NB + b + 1), (2, 3))
                        if b == NB - 1:
                            ins.then_inc(tile_used, 1)
                    if b == 0:
                        ins.then_inc(gu_done, 1)

            def turn_chunk(s, nb, f, i):
                pe.wait_ge(act_ready[s], nb * (f + 1) + i * (nb * BODY_F))
                for k in range(2):
                    for b in range(nb):
                        ins = pe.transpose(ps[:, 6 + f % 2, (k * nb + b) * P:(k * nb + b + 1) * P],
                                           tmp[:, b * 256 + k * P:b * 256 + (k + 1) * P], ident[:, :])
                ins.then_inc(a_turned[s], 1)

            def body(s, nb, moe, t0, i):
                stream = 2 if s == 2 else 1
                _, _, lo, used = STREAMS[stream]
                lhs = xe if moe else hT
                aT = aT_moe if moe else aT_dense
                j = 0
                for step, kind, f in body_schedule(moe):
                    if step == "tile" and not moe and f == 0 and kind in "ab":
                        if kind == "b":
                            first_chunk(t0, i)
                        j += 1
                    elif step == "tile":
                        t = t0 + j
                        pe.wait_ge(lo, t + 1 + i * BODY_TILES)
                        if kind in "ab":
                            k0 = 0 if kind == "a" else 4
                            if moe and kind == "a" and f == 0:
                                pe.wait_ge(xe_lo[s], 2 + i * 2)
                            for b in range(nb):
                                bank = 4 + (f % 2 if moe else b)
                                if kind == "a" and moe and f >= 2:
                                    pe.wait_ge(act_ready[s], f - 1 + i * BODY_F)
                                if kind == "a" and not moe and f >= 1:
                                    pe.wait_ge(act_ready[s], nb * (f - 1) + b + 1 + i * (nb * BODY_F))
                                for k in range(4):
                                    for m, (sl, sr) in enumerate(((0, 0), (0, 1), (1, 0))):
                                        ins = pe.matmul(ps[:, bank, :], lhs[:, sl, k0 + k, tokens(b)],
                                                        slot(t, sr, 512)[:, k, :],
                                                        start=kind == "a" and k + m == 0,
                                                        stop=kind == "b" and k == 3 and m == 2)
                                if kind == "b" and b < nb - 1:
                                    ins.then_inc(gu_done, 1)
                        else:
                            pe.wait_ge(aT_lo[s], f + 1 + i * BODY_F)
                            if f == 0:
                                pe.wait_ge(x_ffn[s], 1 + NB + i * NB if moe else 1 + i * NB)
                            for b in range(nb):
                                for nh in range(2):
                                    for k in range(2):
                                        for m, (sl, sr) in enumerate(((0, 0), (0, 1), (1, 0))):
                                            ins = pe.matmul(ps[:, 2 * b + nh, :],
                                                            aT[:, f % 2, sl, k, tokens(b)],
                                                            slot(t, sr, D)[:, k, nh * 512:(nh + 1) * 512],
                                                            start=f == 0 and k + m == 0,
                                                            stop=f == BODY_F - 1 and k == 1 and m == 2)
                                if f == BODY_F - 1 and b < nb - 1:
                                    ins.then_inc(down_done, 1)
                                if f == BODY_F - 2 and b < nb - 1:
                                    turn_chunk(s, nb, f + 1, i)
                        ins.then_inc(used, 1)
                        j += 1
                    elif step == "turn":
                        if f < BODY_F - 1 or moe:
                            turn_chunk(s, nb, f, i)
                    elif step == "scatter":
                        if f == 0:
                            pe.wait_ge(ye_lo[s], 2 + i * 2)
                            pe.wait_ge(gT_ready[s], 1 + i)
                        scatter(s, f, NB * i + f)
                    elif step == "route":
                        pe.wait_ge(x_ffn[s], 1 + NB + i * NB)
                        for b in range(NB):
                            pe.transpose(ps[:, 2, tokens(b)], G[:, b, :].bitcast(F32), ident[:, :])
                        for b in range(NB):
                            ins = pe.matmul(ps[:, 2, SEQ:SEQ + 1], G[:, b, :].bitcast(F32),
                                            comb[:, b, bass.ds(i + (EXPERTS if s == 2 else 0), 1)],
                                            start=b == 0, stop=b == NB - 1)
                        ins.then_inc(route_done[s], 1)
                    elif step == "gather":
                        pe.wait_ge(g_ready[s], 2 + i)
                        pe.wait_ge(gT_ready[s], 2 + i)
                        gather(s)

            def scatter(s, b, n):
                bank = SCATTER_BANKS[b]
                for nh in range(2):
                    for k in range(2):
                        ins = pe.matmul(ps[:, bank + nh, :], GT[:, tokens(b)], ye[:, k, nh * 512:(nh + 1) * 512],
                                        start=k == 0, stop=k == 1)
                ins.then_inc(scattered[s], 1)

            def gather(s):
                for k in range(KD):
                    for m, (b, part) in enumerate(((0, 0), (0, 1), (1, 0), (1, 1))):
                        ins = pe.matmul(ps[:, 2 + k // 4, k % 4 * P:(k % 4 + 1) * P],
                                        yn[:, part, b, k * P:(k + 1) * P], G[:, b, :],
                                        start=m == 0, stop=m == 3)
                    if k % 4 == 3:
                        ins.then_inc(gathered[s], 1)

            def logits(b):
                pe.wait_ge(hT_lo, 24 + 2 * (b + 1))
                for k in range(KD):
                    for s in range(2):
                        ins = pe.matmul(ps[:, b, 0:EXPERTS], hT[:, s, k, tokens(b)].bitcast(F32),
                                        router_sb[:, k, :], start=k + s == 0, stop=k + s == KD)
                ins.then_inc(logit_done, 1)

            def experts(s, t0):
                pe.wait_ge(g_ready[s], 1)
                if s == 1:
                    pe.wait_ge(yn_lo, 1)
                gather(s)
                with pe.Fori(0, EXPERTS) as e:
                    body(s, 1, True, t0, e)
                if s == 1:
                    proj(1, (0,))
                pe.wait_ge(ye_lo[s], 2 * (EXPERTS + 1))
                pe.wait_ge(gT_ready[s], EXPERTS + 1)
                pe.wait_ge(xe_lo[s], 2 * (EXPERTS + 1))
                for b in range(NB):
                    scatter(s, b, EXPERTS * NB + b)
                if s == 1:
                    proj(1, (1,))

            def proj(l, blocks):
                wide(LAYER_T0[l] + T_PLE[l], (0,), 1, pT, PROJ_BANKS[l],
                     lambda b: [(x_ffn[0], 1 + NB * (FFN_BODIES[0] - 1) + b + 1)] if l == 0 else [],
                     proj_done, blocks=blocks)

            pe.wait_ge(consts, 9)
            turn_p(0, 0)
            turn(0, Y, lambda b: (y_ready, b + 1))
            pe.wait_ge(pT_lo, 1)
            for l in range(DEPTH):
                t0 = LAYER_T0[l]
                for b in range(NB):
                    if l and b:
                        turn(4 * l, Y, lambda b: (y_ready, NB * 3 * l + b + 1), (2, 3))
                    pe.wait_ge(hT_lo, 16 * l + 2 * (b + 1))
                    for i in range(2):
                        t = t0 + i
                        if b == 0:
                            pe.wait_ge(lo_ready, t + 1)
                        for k in range(4):
                            ins = product(ps[:, 4 + b, :], pair(hT, 4 * i + k, tokens(b)),
                                          tile_pair(t, 512, k, slice(0, 512)), i + k == 0, i == 1 and k == 3)
                        if b == NB - 1:
                            ins.then_inc(tile_used, 1)
                    if b == 0:
                        ins.then_inc(q_done, 1)
                t = t0 + 2
                pe.wait_ge(lo_ready, t + 1)
                for b in range(NB):
                    for k in range(KD):
                        ins = product(ps[:, b, 0:256], pair(hT, k, tokens(b)),
                                      tile_pair(t, 256, k, slice(0, 256)), k == 0, k == KD - 1)
                    if b == 0:
                        ins.then_inc(kv_done, 1)
                ins.then_inc(tile_used, 1)
                for j, bank in enumerate((2, 3, 6, 7, 2, 3, 4, 5)):
                    t = t0 + T_CHAN + j
                    pe.wait_ge(lo_ready, t + 1)
                    if j in (4, 5):
                        pe.wait_ge(c_copied, 2 * l + j - 3)
                    if j == 6:
                        pe.wait_ge(rot_ready, 4 * (l + 1))
                    for c in range(2):
                        for k in range(KD):
                            ins = product(ps[:, bank, c * SEQ:(c + 1) * SEQ],
                                          tile_pair(t, 256, k, slice(c * P, (c + 1) * P)),
                                          pair(hT, k, slice(0, SEQ)), k == 0, k == KD - 1)
                    ins.then_inc(tile_used, 1)
                    if j == 5:
                        pe.wait_ge(rot_ready, 4 * (l + 1))
                        pe.wait_ge(v_ready, NB * (l + 1))
                        pe.wait_ge(conv_y, 2 * l + 1)
                        for c in range(CH):
                            for b in range(NB):
                                ins = pe.transpose(
                                    ps[:, 6 + c // 2, c % 2 * SEQ + b * P:c % 2 * SEQ + (b + 1) * P],
                                    q_rot[:, b, c * P:(c + 1) * P], ident[:, :])
                            if c % 2:
                                ins.then_inc(qk_turned, 1)
                        for h in range(KV_HEADS):
                            for b in range(NB):
                                ins = pe.transpose(ps[:, 0, h * SEQ + b * P:h * SEQ + (b + 1) * P],
                                                   kdup[:, b, h].rearrange("p c d -> p (c d)"), ident[:, :])
                        ins.then_inc(qk_turned, 1)
                for c in range(6):
                    r, nh = c // 2, c % 2
                    for step in range(3):
                        t = t0 + T_GATE + 3 * c + step
                        at = 3 * c + step
                        pe.wait_ge(lo_ready, t + 1)
                        if step < 2:
                            for b in range(NB):
                                if c and step == 0:
                                    pe.wait_ge(sig_ready, 12 * l + NB * (c - 1) + b + 1)
                                if c == 0 and step == 0:
                                    pe.wait_ge(chan_out, 2 * l + 1 + b)
                                for k in range(4):
                                    ins = product(ps[:, 4 + b, :], pair(hT, 4 * step + k, tokens(b)),
                                                  tile_pair(t, 512, k, slice(0, 512)),
                                                  step + k == 0, step == 1 and k == 3)
                                if step and b == 0:
                                    ins.then_inc(gate_done, 1)
                        else:
                            ready = ((conv_lo, 2 * (l + 1)), (pool_lo, 2 * (l + 1)), (att_lo, 2 * (l + 1)))[r]
                            pe.wait_ge(*ready)
                            if c == 0:
                                pe.wait_ge(kT_ready, 2 * (l + 1))
                            for b in range(NB):
                                if c:
                                    pe.wait_ge(merged, 12 * l + NB * (c - 1) + b + 1)
                                for k in range(CH):
                                    lh = [brv[:, 2 * r + s, k, tokens(b)] for s in range(2)]
                                    ins = product(ps[:, b, :], lh, tile_pair(t, 512, k, slice(0, 512)),
                                                  k == 0, k == CH - 1)
                                if b == 0:
                                    ins.then_inc(branch_done, 1)
                        ins.then_inc(tile_used, 1)
                        if at == MIX:
                            pe.wait_ge(pooled_ready, CH * (l + 1))
                            pe.wait_ge(small_in, 16 + 96 * (l + 1))
                            pe.wait_ge(conv_y, 2 * (l + 1))
                            for g in range(CH):
                                ins = pe.matmul(ps[:, 2 + g // 2, g % 2 * SEQ:(g % 2 + 1) * SEQ],
                                                poolw_sb[:, g, :], pooled[:, g, :], start=True, stop=True)
                            ins.then_inc(mixed_done, 1)
                        for stage, late in ((att_values, 4), (att_turn, 3), (att_scores, 0)):
                            if 0 <= at - ATT - late < 6:
                                stage(l, at - ATT - late)
                        if at == 15:
                            turn(4 * l + 1, M, lambda b: (merged, 12 * l + 8 + b + 1), (0, 1))
                turn(4 * l + 1, M, lambda b: (merged, 12 * l + 10 + b + 1), (2, 3))
                wide(t0 + T_OUT, (0, 1), 4, hT, (0, 2), lambda b: [(hT_lo, 16 * l + 6)])
                wide(t0 + T_OUT, (2, 3), 4, hT, (0, 2), lambda b: [(hT_lo, 16 * l + 8)], out_done,
                     lambda: turn(4 * l + 2, Y, lambda b: (y_ready, NB * (3 * l + 1) + 1), (0, 1)))
                if l == 1:
                    logits(0)
                if l == 1:
                    turn(6, Y, lambda b: (y_ready, NB * 4 + b + 1), (2, 3))
                    logits(1)
                if l == 0:
                    with pe.Fori(0, FFN_BODIES[0]) as i:
                        body(0, NB, False, t0 + T_FFN, i)
                else:
                    pe.wait_ge(sel_ready, 1)
                    pe.matmul(ps[:, 6, 0:8], below[:, :], sel[:, 0, :], start=True, stop=True)
                    pe.matmul(ps[:, 6, 8:16], ones[:, :], sel[:, 0, :], start=True, stop=False)
                    pe.matmul(ps[:, 6, 8:16], below[:, :], sel[:, 1, :], start=False, stop=True)
                    pe.matmul(ps[:, 6, 16:24], ones[:, :], sel[:, 0, :], start=True, stop=False)
                    pe.matmul(ps[:, 6, 16:24], ones[:, :], sel[:, 1, :], start=False, stop=True
                              ).then_inc(rank_done, 1)
                    experts(1, t0 + T_FFN)
                    more = pe.value_load(more_i[0:1, 0:1], min_val=0, max_val=1)
                    with pe.If(more > 0):
                        pe.wait_ge(x_ffn[1], 1 + NB * (EXPERTS + 1))
                        pe.wait_ge(proj_out, 2 * NB)
                        pe.sem_inc(tile_used2, BODY_TILES)
                        experts(2, BODY_TILES)
                        pe.wait_ge(x_ffn[2], 1 + NB * (EXPERTS + 1))
                u = t0 + T_PLE[l]
                if l == 0:
                    proj(0, range(NB))
                else:
                    pe.wait_ge(proj_out, 2 * NB)
                turn(4 * l + 3, Y, lambda b: (y_ready, NB * (3 * l + 2) + b + 1))
                wide(u + 1, (0, 1), 4, hT, (0, 2),
                     lambda b: [(hT_lo, 16 * l + 12 + 2 * (b + 1)), (proj_out, NB * l + b + 1)])
                if l == 0:
                    turn_p(1, 6)
                wide(u + 1, (2, 3), 4, hT, (0, 2), lambda b: [], pg_done)
                if l == 0:
                    pe.wait_ge(pT_lo, 2)
                    turn(4, Y, lambda b: (y_ready, NB * 3 + b + 1), (0, 1))


_INS = ["x", "p", "positions", "norm_mix_g", "w_in", "conv_w", "pool_w", "pool_scale", "attn_sinks",
        "w_branch", "w_out", "norm_ffn_g", "ffn_w_gu", "ffn_w_down", "moe_router", "moe_w_gu",
        "moe_w_down", "norm_ple_g", "ple_w_proj", "ple_w_gate", "final_norm_g"]


def kernel(**inputs):
    import concourse.bacc as bacc
    from concourse.bass_utils import run_bass_kernel_spmd as run

    nc = bacc.Bacc("TRN2", target_bir_lowering=False, num_devices=1, dynamic_dma_scratch_size=4096)
    arrays = {name: np.ascontiguousarray(inputs[name]) for name in _INS}
    arrays["inv_freq"] = (np.float32(10000.0) ** (
        np.float32(-2.0) * np.arange(HALF, dtype=np.float32) / np.float32(HD))).astype(np.float32)[None, :]
    args = [nc.dram_tensor(f"{n}_dram", a.shape, mybir.dt.from_np(a.dtype), kind="ExternalInput").ap()
            for n, a in arrays.items()]
    out = nc.dram_tensor("out_dram", (1, SEQ, D), F32, kind="ExternalOutput").ap()
    trunk(nc, *args, out)
    r = run(nc, [{f"{n}_dram": a for n, a in arrays.items()}], core_ids=[0])
    return r.results[0]["out_dram"]
```

```python
from contextlib import ExitStack

import numpy as np

import concourse.bass as bass
from concourse import mybir

F32 = mybir.dt.float32
F32R = mybir.dt.float32r
I32 = mybir.dt.int32
U32 = mybir.dt.uint32
ALU = mybir.AluOpType
ACT = mybir.ActivationFunctionType
AX = mybir.AxisListType

P = 128
D = 1024
SEQ = 256
NB = SEQ // P
KD = D // P
DEPTH = 2
BW = 512
CH = BW // P
HEADS, KV_HEADS, HD = 8, 2, 64
HALF = HD // 2
D_FF = 3584
EXPERTS = 8
D_FFE = 1792
PLE = 256
EPS = 1e-6
NEG = -1e30
OFF_POOL, OFF_Q, OFF_K, OFF_GATE = 1536, 2048, 2560, 2816

RAW, SPLIT = 7, 3
TILE = 2048
BODY_F = 7
BODY_TILES = 3 * BODY_F

MIX, ATT, ATT_OUT = 2, 1, 11
OUT_BANKS = (2, 0)
PROJ_BANKS = [(0, 2), (2, 0)]
SCATTER_BANKS = (0, 2)

T_CHAN = 3
T_GATE = T_CHAN + 8
T_OUT = T_GATE + 18
FFN_BODIES = [D_FF // (256 * BODY_F), EXPERTS]
T_FFN = [T_OUT + 4, T_OUT + 5]
T_PROJ = [T_FFN[0] + BODY_TILES * FFN_BODIES[0], T_OUT + 4]
T_PLE = [T_PROJ[0] + 1, T_FFN[1] + BODY_TILES * FFN_BODIES[1]]
LAYER_T0 = [0, T_PLE[0] + 4]
N_TILES = LAYER_T0[1] + T_PLE[1] + 4


def swiglu_blocks(moe, kind, f):
    if moe:
        return (0,) if kind == "" else ()
    if f:
        return (0, 1) if kind == "" else ()
    return {"a": (), "b": (0,), "": (1,)}[kind]


def body_schedule(moe):
    s = []
    for f in range(BODY_F):
        s.append(("tile", "a", f))
        if f:
            s.append(("turn", "", f - 1))
        if moe and f == 1:
            s.append(("scatter", "", 1))
        s.append(("tile", "b", f))
        s.append(("swiglu", "", f))
        if moe and f == 0:
            s.append(("scatter", "", 0))
        if moe and f == BODY_F - 1:
            s.append(("gather", "", 0))
            s.append(("turn", "", f))
        if f:
            s.append(("tile", "d", f - 1))
        if moe and f == 1:
            s.append(("route", "", 0))
    if not moe:
        s.append(("turn", "", BODY_F - 1))
    s.append(("tile", "d", BODY_F - 1))
    s.append(("close", "", 0))
    return s


def turn_order(n):
    if n % 4 == 1:
        return [(b, half) for half in range(2) for b in range(NB)]
    return [(b, half) for b in range(NB) for half in range(2)]


def turn_bank(n, blk, half):
    return (6 + blk, OUT_BANKS[blk])[half] if n == 2 else (6, 4)[half] + blk


def trunk(nc, x, p, positions, norm_mix_g, w_in, conv_w, pool_w, pool_scale, attn_sinks, w_branch,
          w_out, norm_ffn_g, ffn_w_gu, ffn_w_down, moe_router, moe_w_gu, moe_w_down, norm_ple_g,
          ple_w_proj, ple_w_gate, final_norm_g, inv_freq, out):
    ctx = ExitStack()
    with ctx:
        def sb(name, shape, dt=F32):
            return ctx.enter_context(nc.sbuf_tensor(name, shape, dt))

        def sem(name):
            return ctx.enter_context(nc.semaphore(name))

        raw = sb("raw", [P, RAW, TILE])
        split = sb("split", [P, SPLIT, 2, TILE], F32R)
        X = sb("X", [P, NB, D])
        Y = sb("Y", [P, NB, D])
        M = sb("M", [P, NB, D])
        g_row = sb("g_row", [P, D])
        hT = sb("hT", [P, 2, KD, SEQ], F32R)
        br = sb("br", [P, 6, CH * SEQ], F32R)
        pT = sb("pT", [P, 2, 2, SEQ], F32R)
        upool = sb("upool", [P, CH, 16 + SEQ])
        wsum = sb("wsum", [P, 2, 16 + SEQ])
        kdup = sb("kdup", [P, NB, KV_HEADS, 2, HD])
        v_sb = sb("v_sb", [P, NB, KV_HEADS * HD])
        qT = sb("qT", [P, CH, SEQ])
        kT = sb("kT", [P, KV_HEADS, 2, SEQ])
        sc = sb("sc", [P, 512])
        prT = sb("prT", [P, 4, P])
        sg = sb("sg", [P, NB, 512])
        tmp = sb("tmp", [P, D])
        poolw_sb = sb("poolw_sb", [P, CH, P])
        convw_sb = sb("convw_sb", [P, CH, 3])
        pscale_sb = sb("pscale_sb", [P, CH])
        sinks_sb = sb("sinks_sb", [P, HEADS])
        router_sb = sb("router_sb", [P, KD, EXPERTS])
        router_split = sb("router_split", [P, KD, 2, EXPERTS], F32R)
        ident = sb("ident", [P, P])
        below = sb("below", [P, P])
        ones = sb("ones", [P, P])
        slot_row = sb("slot_row", [P, P])
        mask = sb("mask", [P, SEQ])
        rcount = sb("rcount", [P, 16])
        pos_i = sb("pos_i", [P, NB], I32)
        pos_f = sb("pos_f", [P, NB])
        freq = sb("freq", [P, HALF])
        ang = sb("ang", [P, 2, NB, HALF])
        turns = sb("turns", [P, 2, NB, HALF])
        sin2 = sb("sin2", [P, NB, 2, HALF])
        cos1 = sb("cos1", [P, NB, HALF])
        ms = sb("ms", [P, NB, 2])
        rstd = sb("rstd", [P, 2])
        power = sb("power", [P, 1])
        mx = sb("mx", [P, 4])
        nmx = sb("nmx", [P, 2, 4])
        den = sb("den", [P, 2, 4])
        esk = sb("esk", [P, 2, 4])
        rden = sb("rden", [P, 4])
        logit = sb("logit", [P, NB, EXPERTS])
        top = sb("top", [P, NB, 8])
        topi = sb("topi", [P, NB, 8], U32)
        topf = sb("topf", [P, NB, 8])
        hot = sb("hot", [P, NB, 2, EXPERTS])
        wts = sb("wts", [P, NB, 4])
        comb = sb("comb", [P, NB, 2 * EXPERTS])
        sel = sb("sel", [P, NB, EXPERTS])
        rank = sb("rank", [P, NB, 2 * EXPERTS + 1])
        load = sb("load", [P, EXPERTS])
        most = sb("most", [P, 2])
        more_i = sb("more_i", [P, 1], I32)
        G = sb("G", [P, NB, P], F32R)
        GT = sb("GT", [P, SEQ], F32R)
        w_slot = sb("w_slot", [P, 1])

        q_rot = Y[:, 0, :].rearrange("p (b n) -> p b n", b=NB)
        p_sb = upool[:, 0:NB, 16:]
        c_sb = Y[:, 1, :].rearrange("p (c n) -> p c n", c=CH)
        pooled = c_sb
        vpad = M[:, 0:2, :].rearrange("p b n -> p (b n)")[:, 0:CH * (SEQ + 2)].rearrange(
            "p (c n) -> p c n", c=CH)
        cacc = M[:, 0:2, :].rearrange("p b n -> p (b n)")[:, 1536:2048].rearrange(
            "p (c n) -> p c n", c=2)
        ctmp = tmp[:, 0:512].rearrange("p (c n) -> p c n", c=2)
        brv = br[:, :, :].rearrange("p r (c n) -> p r c n", c=CH)
        yn = br[:, 0:4, :].rearrange("p (s b) n -> p s b n", s=2)
        xe = br[:, 4:6, :].rearrange("p s (k n) -> p s k n", k=KD)
        hTf = hT[:, :, :, :].rearrange("p s k n -> p (s k n)")
        ye = hTf[:, 0:2 * D].rearrange("p (s n) -> p s n", s=2)
        aT_moe = hTf[:, 2 * D:2 * D + 1024].rearrange("p (u s k n) -> p u s k n", u=2, s=2, k=2)
        brf = br[:, :, :].rearrange("p r n -> p (r n)")
        aT_dense = brf[:, 0:2048].rearrange("p (u s k n) -> p u s k n", u=2, s=2, k=2)

        ps = ctx.enter_context(nc.psum_tensor("ps", [P, 8, 512], F32))

        landed = [sem(f"landed{i}") for i in range(RAW)]
        hi_ready, lo_ready, tile_used = sem("hi_ready"), sem("lo_ready"), sem("tile_used")
        consts = sem("consts")
        cstep = sem("cstep")
        x_in = [sem(f"x_in{b}") for b in range(NB)]
        pos_in, small_in, g_in = sem("pos_in"), sem("small_in"), sem("g_in")
        g_first = sem("g_first")
        p_in = [sem(f"p_in{l}") for l in range(DEPTH)]
        dve_step = sem("dve_step")
        rope_ang, rope_ready = sem("rope_ang"), sem("rope_ready")
        ms_plus = sem("ms_plus")
        ms_ready, rstd_ready, y_ready = sem("ms_ready"), sem("rstd_ready"), sem("y_ready")
        turned, hT_hi, hT_lo = sem("turned"), sem("hT_hi"), sem("hT_lo")
        p_turned, pT_hi, pT_lo = sem("p_turned"), sem("pT_hi"), sem("pT_lo")
        q_done, kv_done, rot_ready, v_ready = sem("q_done"), sem("kv_done"), sem("rot_ready"), sem("v_ready")
        chan_out = sem("chan_out")
        c_copied = sem("c_copied")
        conv_y, conv_hi, conv_lo = sem("conv_y"), sem("conv_hi"), sem("conv_lo")
        conv_v, pool_step, rcount_ready = sem("conv_v"), sem("pool_step"), sem("rcount_ready")
        pooled_ready, mixed_done = sem("pooled_ready"), sem("mixed_done")
        pool_hi, pool_lo = sem("pool_hi"), sem("pool_lo")
        qk_turned, qT_ready, kT_ready = sem("qk_turned"), sem("qT_ready"), sem("kT_ready")
        s_done, masked, exped, probs, pr_turned, prT_ready = (
            sem("s_done"), sem("masked"), sem("exped"), sem("probs"), sem("pr_turned"), sem("prT_ready"))
        att_done, att_hi, att_lo = sem("att_done"), sem("att_hi"), sem("att_lo")
        gate_done, sig_ready, branch_done, merged = (
            sem("gate_done"), sem("sig_ready"), sem("branch_done"), sem("merged"))
        out_done, x_out = sem("out_done"), sem("x_out")
        proj_done, proj_out = sem("proj_done"), sem("proj_out")
        pg_done, psig, x_ple = sem("pg_done"), sem("psig"), sem("x_ple")
        gu_done, down_done = sem("gu_done"), sem("down_done")
        silu_ready = [sem(f"silu_ready{i}") for i in range(3)]
        act_ready = [sem(f"act_ready{i}") for i in range(3)]
        a_turned = [sem(f"a_turned{i}") for i in range(3)]
        aT_hi = [sem(f"aT_hi{i}") for i in range(3)]
        aT_lo = [sem(f"aT_lo{i}") for i in range(3)]
        x_ffn = [sem(f"x_ffn{i}") for i in range(3)]
        logit_done, route_step, sel_ready, rank_done = (
            sem("logit_done"), sem("route_step"), sem("sel_ready"), sem("rank_done"))
        router_hi, router_lo = sem("router_hi"), sem("router_lo")
        routed, yn_hi, yn_lo = sem("routed"), sem("yn_hi"), sem("yn_lo")
        g_ready = [None] + [sem(f"g_ready{i}") for i in (1, 2)]
        route_done = [None] + [sem(f"route_done{i}") for i in (1, 2)]
        gT_ready = [None] + [sem(f"gT_ready{i}") for i in (1, 2)]
        ws_ready = [None] + [sem(f"ws_ready{i}") for i in (1, 2)]
        gathered = [None] + [sem(f"gathered{i}") for i in (1, 2)]
        xe_hi = [None] + [sem(f"xe_hi{i}") for i in (1, 2)]
        xe_lo = [None] + [sem(f"xe_lo{i}") for i in (1, 2)]
        ye_hi = [None] + [sem(f"ye_hi{i}") for i in (1, 2)]
        ye_lo = [None] + [sem(f"ye_lo{i}") for i in (1, 2)]
        half_down = [None] + [sem(f"half_down{i}") for i in (1, 2)]
        scattered = [None] + [sem(f"scattered{i}") for i in (1, 2)]
        landed2 = [sem(f"landed2_{i}") for i in range(RAW)]
        hi_ready2, lo_ready2, tile_used2 = sem("hi_ready2"), sem("lo_ready2"), sem("tile_used2")
        stored = sem("stored")

        STREAMS = {1: (landed, hi_ready, lo_ready, tile_used),
                   2: (landed2, hi_ready2, lo_ready2, tile_used2)}

        def slot(t, s, n):
            return split[:, t % SPLIT, s, :].rearrange("p (k n) -> p k n", n=n)

        def raw_slot(t, n):
            return raw[:, t % RAW, :].rearrange("p (k n) -> p k n", n=n)

        def wait_product(eng, b, last, signal, n, t, i=0, per=0, stream=1):
            if b == last:
                eng.wait_ge(STREAMS[stream][3], t + 1 + i * per)
            else:
                eng.wait_ge(signal, n)

        def wait_half(eng, b, nh, signal, n0, t, i=0, per=0):
            if (b, nh) == (NB - 1, 1):
                eng.wait_ge(tile_used, t + 1 + i * per)
            else:
                eng.wait_ge(signal, n0 + 2 * b + nh + 1)

        def cols(nh):
            return slice(nh * 512, (nh + 1) * 512)

        def scores_of(u):
            return sc[:, :] if u % 3 == 2 else tmp[:, u % 3 * 512:(u % 3 + 1) * 512]

        def halves(a):
            return a.rearrange("p (h n) -> p h n", h=2)

        def two_banks(b0):
            return ps[:, b0:b0 + 2, :]

        block = ctx.enter_context(nc.Block())

        @block.sync
        def _(sp):
            def fetch(t, parts, i=0, per=0, stream=1):
                land, _, lo, _ = STREAMS[stream]
                if t >= RAW:
                    sp.wait_ge(lo, t - RAW + 1 + i * per)
                for dst, src in parts:
                    sp.dma_start(dst, src).then_inc(land[t % RAW], 32 // len(parts))

            def rows(w, k0, nk, c0, n):
                return w[k0 * P:(k0 + nk) * P, c0:c0 + n].rearrange("(k p) n -> p k n", p=P)

            def ffn(stream, t0, w_gu, w_down, d_ff, f0, i=0):
                j = 0
                for step, kind, f in body_schedule(False):
                    if step != "tile":
                        continue
                    t = t0 + j
                    if kind == "d":
                        src = w_down[bass.ds((f0 + f) * 256, 256), :].rearrange("(k p) n -> p k n", p=P)
                        fetch(t, [(raw_slot(t, D), src)], i, BODY_TILES, stream)
                    else:
                        k0 = 0 if kind == "a" else 4
                        parts = []
                        for s in range(2):
                            src = w_gu[k0 * P:(k0 + 4) * P, bass.ds(s * d_ff + (f0 + f) * 256, 256)]
                            parts.append((raw_slot(t, 512)[:, :, s * 256:(s + 1) * 256],
                                          src.rearrange("(k p) n -> p k n", p=P)))
                        fetch(t, parts, i, BODY_TILES, stream)
                    j += 1

            def experts(stream, t0):
                with sp.Fori(0, EXPERTS) as e:
                    gu = moe_w_gu[0, bass.ds(e, 1)].rearrange("e k n -> (e k) n")
                    dn = moe_w_down[0, bass.ds(e, 1)].rearrange("e k n -> (e k) n")
                    ffn(stream, t0, gu, dn, D_FFE, 0, e)

            for b in range(NB):
                sp.dma_start(X[:, b, :], x[0, b * P:(b + 1) * P, :]).then_inc(x_in[b], 16)
            for l in range(DEPTH):
                t = LAYER_T0[l]
                w = w_in[l]
                for i in range(2):
                    fetch(t + i, [(raw_slot(t + i, 512), rows(w, 4 * i, 4, OFF_Q, 512))])
                fetch(t + 2, [(raw_slot(t + 2, 256), rows(w, 0, KD, OFF_K, 256))])
                for j, c0 in enumerate((512, 768, 1024, 1280, 0, 256, OFF_POOL, OFF_POOL + 256)):
                    u = t + T_CHAN + j
                    fetch(u, [(raw_slot(u, 256), rows(w, 0, KD, c0, 256))])
                for r in range(3):
                    for nh in range(2):
                        u = t + T_GATE + 3 * (2 * r + nh)
                        for i in range(2):
                            fetch(u + i, [(raw_slot(u + i, 512),
                                           rows(w, 4 * i, 4, OFF_GATE + r * D + nh * 512, 512))])
                        fetch(u + 2, [(raw_slot(u + 2, 512), rows(w_branch[l, r], 0, CH, nh * 512, 512))])
                for i in range(4):
                    fetch(t + T_OUT + i, [(raw_slot(t + T_OUT + i, D), rows(w_out[l], 2 * i, 2, 0, D))])
                u = t + T_PLE[l]
                if l == 0:
                    with sp.Fori(0, FFN_BODIES[0]) as i:
                        ffn(1, t + T_FFN[0], ffn_w_gu[0], ffn_w_down[0], D_FF, i * BODY_F, i)
                v = t + T_PROJ[l]
                fetch(v, [(raw_slot(v, D), rows(ple_w_proj[l], 0, 2, 0, D))])
                if l:
                    experts(1, t + T_FFN[1])
                    sp.wait_ge(routed, 1)
                    more = sp.value_load(more_i[0:1, 0:1], min_val=0, max_val=1)
                    with sp.If(more > 0):
                        sp.wait_ge(lo_ready, u)
                        for land in landed2:
                            sp.sem_inc(land, 32 * (BODY_TILES // RAW))
                        experts(2, BODY_TILES)
                        sp.wait_ge(lo_ready2, (EXPERTS + 1) * BODY_TILES)
                for i in range(4):
                    fetch(u + i, [(raw_slot(u + i, D), rows(ple_w_gate[l], 2 * i, 2, 0, D))])
            for b in range(NB):
                for nh in range(2):
                    sp.wait_ge(y_ready, 2 * (6 * NB + b) + nh + 1)
                    sp.dma_start(out[0, b * P:(b + 1) * P, cols(nh)], Y[:, b, cols(nh)]).then_inc(stored, 16)
            sp.wait_ge(stored, 2 * 16 * NB)

        gains = [norm_mix_g[0:1, :], norm_ffn_g[0:1, :], norm_ple_g[0:1, :],
                 norm_mix_g[1:2, :], norm_ffn_g[1:2, :], norm_ple_g[1:2, :],
                 final_norm_g.rearrange("(a n) -> a n", a=1)]

        def on_all(row):
            return row.broadcast_to([P, row.shape[-1]])

        @block.gpsimd
        def _(pool):
            pool.memset(power[:, :], -0.5).then_inc(consts, 1)
            pool.memset(ident[:, :], 0.0).then_inc(cstep, 1)
            pool.memset(below[:, :], 1.0).then_inc(cstep, 1)
            pool.memset(mask[:, :], 0.0).then_inc(cstep, 1)
            pool.memset(ones[:, :], 1.0).then_inc(consts, 1)
            pool.memset(upool[:, :, 0:16], 0.0).then_inc(consts, 1)
            pool.memset(wsum[:, :, 0:16], 0.0).then_inc(consts, 1)
            pool.memset(kT[:, :, :, :], 0.0).then_inc(consts, 1)
            pool.iota(slot_row[:, :], pattern=[[1, P]], base=0, channel_multiplier=0,
                      allow_small_or_imprecise_dtypes=True).then_inc(consts, 1)
            pool.wait_ge(cstep, 3)
            pool.affine_select(out=ident[:, :], in_=ident[:, :], compare_op=ALU.not_equal, fill=1.0,
                               base=0, pattern=[[-1, P]], channel_multiplier=1).then_inc(consts, 1)
            pool.affine_select(out=below[:, :], in_=below[:, :], compare_op=ALU.is_gt, fill=0.0,
                               base=0, pattern=[[1, P]], channel_multiplier=-1).then_inc(consts, 1)
            pool.affine_select(out=mask[:, :], in_=mask[:, :], compare_op=ALU.is_gt, fill=NEG,
                               base=0, pattern=[[1, SEQ]], channel_multiplier=-1).then_inc(cstep, 1)
            pool.wait_ge(cstep, 4)
            pool.affine_select(out=mask[:, :], in_=mask[:, :], compare_op=ALU.is_ge, fill=NEG,
                               base=P, pattern=[[-1, SEQ]], channel_multiplier=1).then_inc(consts, 1)
            pool.wait_ge(consts, 9)

            def layer_loads(l):
                if l:
                    pool.wait_ge(mixed_done, l)
                    pool.wait_ge(pool_lo, 2 * l)
                    pool.wait_ge(conv_lo, 2 * l)
                    pool.wait_ge(probs, 6 * l)
                pool.dma_start(poolw_sb[:, :, :], pool_w[l].rearrange("g c d -> c g d")).then_inc(small_in, 16)
                for k in range(3):
                    pool.dma_start(convw_sb[:, :, k], conv_w[l, k].rearrange("(c p) -> p c", p=P),
                                   allow_slow_non_contiguous=True
                                   ).then_inc(small_in, 16)
                pool.dma_start(pscale_sb[:, :], pool_scale[l].rearrange("(c p) -> p c", p=P),
                               allow_slow_non_contiguous=True
                               ).then_inc(small_in, 16)
                pool.dma_start(sinks_sb[:, :], on_all(attn_sinks[l:l + 1, :])).then_inc(small_in, 16)

            def rms(n):
                for b in range(NB):
                    pool.wait_ge(ms_ready, 2 * (NB * n + b + 1))
                    pool.tensor_scalar(rstd[:, b:b + 1], ms[:, b, 0:1], ms[:, b, 1:2], EPS, ALU.add, ALU.add
                                       ).then_inc(ms_plus, 1)
                    pool.wait_ge(ms_plus, NB * n + b + 1)
                    pool.tensor_tensor(rstd[:, b:b + 1], rstd[:, b:b + 1], power[:, :], ALU.pow
                                       ).then_inc(rstd_ready, 1)
                if n == 0:
                    layer_loads(0)
                    pool.dma_start(router_sb[:, :, :],
                                   moe_router[0].rearrange("(k p) e -> p k e", p=P)).then_inc(small_in, 16)
                if n + 1 < len(gains):
                    pool.wait_ge(y_ready, 2 * NB * (n + 1))
                    pool.dma_start(g_row[:, :], on_all(gains[n + 1])).then_inc(g_in, 16)

            done = [0]

            def chain(ins):
                done[0] += 1
                ins.then_inc(pool_step, 1)
                pool.wait_ge(pool_step, done[0])

            def pooling(l):
                pool.wait_ge(rcount_ready, 1)
                pool.wait_ge(conv_v, 2 * (l + 1))
                for g in range(CH):
                    pool.wait_ge(chan_out, 2 * l + g // 2 + 1)
                    if g:
                        pool.wait_ge(pooled_ready, CH * l + g)
                    src, w = upool[:, g, :], 1
                    for k in range(g + 1):
                        dst = wsum[:, k % 2, :]
                        chain(pool.tensor_tensor(dst[:, 16:], src[:, 16:], src[:, 16 - w:16 - w + SEQ],
                                                 ALU.add))
                        src, w = dst, 2 * w
                    mean = wsum[:, (g + 1) % 2, :]
                    chain(pool.tensor_scalar(mean[:, 16:], src[:, 16:], 1.0 / w, None, ALU.mult))
                    chain(pool.tensor_tensor(mean[:, 16:15 + w], src[:, 16:15 + w], rcount[:, 0:w - 1],
                                             ALU.mult))
                    pool.tensor_tensor(pooled[:, g, :], mean[:, 16:], upool[:, g, 16:], ALU.subtract
                                       ).then_inc(pooled_ready, 1)

            for l in range(DEPTH):
                for n in range(3):
                    if l and n == 2:
                        pool.wait_ge(logit_done, NB)
                        pool.memset(ye[:, :, :].bitcast(U32), 0).then_inc(ye_lo[1], 2)
                        pool.memset(GT[:, :].bitcast(U32), 0).then_inc(gT_ready[1], 1)
                    if n == 1:
                        pooling(l)
                    rms(3 * l + n)
                    if l == 0 and n == 1:
                        layer_loads(1)
                        pool.wait_ge(pooled_ready, CH)
                        pool.dma_start(p_sb, p[1, 0].rearrange("(b p) n -> p b n", p=P)).then_inc(p_in[1], 16)
            rms(6)

        @block.scalar
        def _(act):
            def split_hi(t, i=0, per=0, stream=1):
                land, hi, _, used = STREAMS[stream]
                visits = BODY_TILES // RAW if per else 0
                act.wait_ge(land[t % RAW], 32 * (t // RAW + 1) + i * (32 * visits))
                if t >= SPLIT:
                    act.wait_ge(used, t - SPLIT + 1 + i * per)
                act.activation(split[:, t % SPLIT, 0, :], raw[:, t % RAW, :], ACT.Copy).then_inc(hi, 1)

            def turn_hi(n, places=None):
                for at, (b, half) in enumerate(turn_order(n)):
                    if places is None or at in places:
                        act.wait_ge(turned, 4 * n + at + 1)
                        act.activation(hT[:, 0, 4 * half:4 * half + 4, b * P:(b + 1) * P],
                                       ps[:, turn_bank(n, b, half), :].rearrange("p (k n) -> p k n", k=4),
                                       ACT.Copy).then_inc(hT_hi, 1)

            def mean_square(b, nh, ready, count):
                act.wait_ge(ready, count)
                act.activation(Y[:, b, cols(nh)], X[:, b, cols(nh)], ACT.Square, scale=D ** -0.5,
                               accum_out=ms[:, b, nh:nh + 1]).then_inc(ms_ready, 1)

            def yn_hi_of(b):
                act.wait_ge(y_ready, 2 * (NB * 4 + b + 1))
                act.activation(yn[:, 0, b], Y[:, b, :], ACT.Copy).then_inc(yn_hi, 1)

            def proj_out_of(l, b):
                wait_half(act, b, 1, proj_done, 3 * l, LAYER_T0[l] + T_PROJ[l])
                act.activation(halves(M[:, b, :]), two_banks(PROJ_BANKS[l][b]), ACT.Copy
                               ).then_inc(proj_out, 1)

            def p_hi(l, bank):
                act.wait_ge(p_turned, l + 1)
                act.activation(pT[:, 0], ps[:, bank, :].rearrange("p (k n) -> p k n", k=2), ACT.Copy
                               ).then_inc(pT_hi, 1)

            def softmax_exp(l, u):
                nh, n = (4, P) if u < 2 else (2, SEQ)
                h0 = 4 * u if u < 2 else 2 * (u - 2)
                act.wait_ge(masked, 6 * l + u + 1)
                for h in range(nh):
                    s = scores_of(u)[:, h * n:(h + 1) * n]
                    act.activation(s, s, ACT.Exp, bias=nmx[:, u % 2, h:h + 1],
                                   accum_out=den[:, u % 2, h:h + 1])
                act.activation(esk[:, u % 2, 0:nh], esk[:, u % 2, 0:nh], ACT.Exp).then_inc(exped, 1)

            def body(s, nb, moe, t0, i, last_split):
                stream = 2 if s == 2 else 1
                aT = aT_moe if moe else aT_dense
                j = 0
                for step, kind, f in body_schedule(moe):
                    if step == "swiglu" or (step == "tile" and kind == "b"):
                        for b in swiglu_blocks(moe, kind, f):
                            wait_product(act, b, nb - 1, gu_done, f + 1 + i * BODY_F,
                                         t0 + (3 * f if f else 1), i, BODY_TILES, stream)
                            bank = 4 + (f % 2 if moe else b)
                            act.activation(sg[:, b, 0:256], ps[:, bank, 0:256], ACT.Silu
                                           ).then_inc(silu_ready[s], 1)
                    if step == "tile":
                        if j + 2 < BODY_TILES + last_split:
                            split_hi(t0 + j + 2, i, BODY_TILES, stream)
                        j += 1
                    elif step == "turn":
                        act.wait_ge(a_turned[s], f + 1 + i * BODY_F)
                        act.activation(aT[:, f % 2, 0], ps[:, 6 + f % 2, 0:nb * SEQ].rearrange(
                            "p (k n) -> p k n", k=2), ACT.Copy).then_inc(aT_hi[s], 1)
                    elif step == "route":
                        act.wait_ge(route_done[s], 1 + i)
                        act.activation(GT[:, :], ps[:, 2, 0:SEQ], ACT.Copy).then_inc(gT_ready[s], 1)
                    elif step == "gather":
                        gather_hi(s, 2 + i * 2)
                    elif step == "close" and moe:
                        act.wait_ge(ws_ready[s], 1 + i)
                        for nh in range(2):
                            if nh:
                                act.wait_ge(STREAMS[stream][3], t0 + BODY_TILES + i * BODY_TILES)
                            else:
                                act.wait_ge(half_down[s], 1 + i)
                            act.activation(ye[:, 0, nh * 512:(nh + 1) * 512], ps[:, nh, :], ACT.Copy,
                                           scale=w_slot[:, 0:1]).then_inc(ye_hi[s], 1)

            def gather_hi(s, n):
                for half in range(2):
                    act.wait_ge(gathered[s], n + half + 1)
                    act.activation(xe[:, 0, 4 * half:4 * half + 4, :],
                                   ps[:, 2 + half, :].rearrange("p (k n) -> p k n", k=4), ACT.Copy
                                   ).then_inc(xe_hi[s], 1)

            def experts(s, t0):
                gather_hi(s, 0)
                if s == 2:
                    act.wait_ge(tile_used, LAYER_T0[1] + T_PLE[1])
                    act.sem_inc(hi_ready2, BODY_TILES)
                    for t in range(2):
                        split_hi(BODY_TILES + t, stream=2)
                with act.Fori(0, EXPERTS - 1) as e:
                    body(s, 1, True, t0, e, 2)
                body(s, 1, True, t0, EXPERTS - 1, 0)

            act.dma_start(pos_i[:, :], positions[0].rearrange("(b p) -> p b", p=P),
                          allow_slow_non_contiguous=True).then_inc(pos_in, 16)
            act.dma_start(freq[:, :], on_all(inv_freq)).then_inc(pos_in, 16)
            act.dma_start(g_row[:, :], on_all(gains[0])).then_inc(g_first, 16)
            act.dma_start(p_sb, p[0, 0].rearrange("(b p) n -> p b n", p=P)).then_inc(p_in[0], 16)
            for b in range(NB):
                for nh in range(2):
                    mean_square(b, nh, x_in[b], 16)
            split_hi(0)
            turn_hi(0)
            split_hi(1)
            act.wait_ge(rope_ang, 1)
            act.activation(sin2[:, :, 1, :], ang[:, 0], ACT.Sin).then_inc(rope_ready, 1)
            act.activation(sin2[:, :, 0, :], ang[:, 0], ACT.Sin, scale=-1.0).then_inc(rope_ready, 1)
            act.activation(cos1[:, :, :], ang[:, 1], ACT.Sin).then_inc(rope_ready, 1)
            for l in range(DEPTH):
                t0 = LAYER_T0[l]
                for j in range(T_CHAN):
                    split_hi(t0 + j + 2)
                    if l == 0 and j == 0:
                        p_hi(0, 4)
                for b in range(NB):
                    wait_product(act, b, NB - 1, kv_done, l + 1, t0 + 2)
                    act.activation(v_sb[:, b, :], ps[:, 2 + b, P:2 * P], ACT.Copy).then_inc(v_ready, 1)
                for j in range(8):
                    split_hi(t0 + T_CHAN + j + 2)
                    if j < 2:
                        act.wait_ge(tile_used, t0 + T_CHAN + j + 1)
                        act.activation(c_sb[:, 2 * j:2 * j + 2, :],
                                       ps[:, 4 + j, :].rearrange("p (c n) -> p c n", c=2), ACT.Copy
                                       ).then_inc(c_copied, 1)
                    if j in (4, 5):
                        act.wait_ge(conv_y, 2 * l + j - 3)
                        act.activation(brv[:, 0, 2 * (j - 4):2 * (j - 4) + 2, :], ctmp, ACT.Copy
                                       ).then_inc(conv_hi, 1)
                    if j == 5:
                        act.wait_ge(qk_turned, 3 * l + 3)
                        for c in range(2):
                            act.activation(qT[:, 2 * c:2 * c + 2, :],
                                           ps[:, 6 + c, :].rearrange("p (c n) -> p c n", c=2), ACT.Copy
                                           ).then_inc(qT_ready, 1)
                    if j in (6, 7):
                        act.wait_ge(tile_used, t0 + T_CHAN + j + 1)
                        act.activation(upool[:, 2 * (j - 6):2 * (j - 6) + 2, 16:],
                                       ps[:, j - 2, :].rearrange("p (c n) -> p c n", c=2), ACT.Copy
                                       ).then_inc(chan_out, 1)
                for c in range(6):
                    for step in range(3):
                        split_hi(t0 + T_GATE + 3 * c + step + 2)
                        at = 3 * c + step
                        if 0 <= at - ATT - 2 < 6:
                            softmax_exp(l, at - ATT - 2)
                        if at == MIX + 1:
                            act.wait_ge(mixed_done, l + 1)
                            for g in range(CH):
                                ins = act.activation(
                                    brv[:, 2, g, :], ps[:, 2 + g // 2, g % 2 * SEQ:(g % 2 + 1) * SEQ],
                                    ACT.Copy, scale=pscale_sb[:, g:g + 1])
                            ins.then_inc(pool_hi, 1)
                        if at == 17:
                            turn_hi(4 * l + 1, (0, 1))
                        if step == 1:
                            for b in range(NB):
                                wait_product(act, b, NB - 1, gate_done, 6 * l + c + 1,
                                             t0 + T_GATE + 3 * c + 1)
                                if NB * c + b >= NB:
                                    act.wait_ge(merged, 12 * l + NB * (c - 1) + b + 1)
                                act.activation(sg[:, b, :], ps[:, 4 + b, :], ACT.Sigmoid
                                               ).then_inc(sig_ready, 1)
                        if at == ATT_OUT:
                            act.wait_ge(att_done, l + 1)
                            for h in range(2):
                                act.activation(brv[:, 4, 2 * h:2 * h + 2, :],
                                               ps[:, 2 + h, :].rearrange("p (c n) -> p c n", c=2), ACT.Copy
                                               ).then_inc(att_hi, 1)
                if l == 0:
                    act.activation(router_split[:, :, 0], router_sb[:, :, :], ACT.Copy).then_inc(router_hi, 1)
                split_hi(t0 + T_OUT + 2)
                turn_hi(4 * l + 1, (2, 3))
                for i in range(1, 3):
                    split_hi(t0 + T_OUT + i + 2)
                for nh in range(2):
                    mean_square(0, nh, x_out, 4 * l + nh + 1)
                turn_hi(4 * l + 2, (0, 1))
                split_hi(t0 + T_OUT + 5)
                if l:
                    yn_hi_of(0)
                for nh in range(2):
                    mean_square(1, nh, x_out, 4 * l + nh + 3)
                turn_hi(4 * l + 2, (2, 3))
                if l == 0:
                    with act.Fori(0, FFN_BODIES[0]) as i:
                        body(0, NB, False, t0 + T_FFN[0], i, 2)
                else:
                    yn_hi_of(1)
                    proj_out_of(1, 0)
                    proj_out_of(1, 1)
                    act.wait_ge(sel_ready, 2)
                    act.activation(wts[:, :, 1:2], wts[:, :, 0:1], ACT.Exp).then_inc(route_step, 1)
                    split_hi(t0 + T_OUT + 6)
                    experts(1, t0 + T_FFN[1])
                u = t0 + T_PLE[l]
                if l:
                    act.wait_ge(routed, 1)
                    more = act.value_load(more_i[0:1, 0:1], min_val=0, max_val=1)
                    with act.If(more > 0):
                        experts(2, BODY_TILES)
                        act.wait_ge(tile_used2, (EXPERTS + 1) * BODY_TILES)
                        act.wait_ge(x_ffn[2], 1 + NB * EXPERTS + 4)
                if l == 0:
                    for nh in range(2):
                        mean_square(0, nh, x_ffn[0], 1 + 4 * (FFN_BODIES[0] - 1) + nh + 1)
                    split_hi(u + 1)
                    for nh in range(2):
                        mean_square(1, nh, x_ffn[0], 1 + 4 * (FFN_BODIES[0] - 1) + nh + 3)
                else:
                    split_hi(u)
                    for b in range(NB):
                        for nh in range(2):
                            mean_square(b, nh, x_ffn[1], 1 + NB * EXPERTS + 2 * nh + b + 1)
                    split_hi(u + 1)
                if l == 0:
                    proj_out_of(0, 0)
                turn_hi(4 * l + 3, (0, 1))
                if l == 0:
                    proj_out_of(0, 1)
                turn_hi(4 * l + 3, (2, 3))
                split_hi(u + 2)
                split_hi(u + 3)
                if l == 0:
                    p_hi(1, 6)
                    split_hi(u + 4)
                for b in range(NB):
                    for nh in range(2):
                        wait_half(act, b, nh, pg_done, 3 * l, u + 3)
                        if b:
                            act.wait_ge(x_ple, 4 * l + nh + 1)
                        act.activation(sg[:, nh, :], ps[:, 2 * b + nh, :], ACT.Sigmoid).then_inc(psig, 1)
                    for nh in range(2):
                        mean_square(b, nh, x_ple, 4 * l + 2 * b + nh + 1)
                    if l == 0:
                        if b == 0:
                            split_hi(u + 5)
                        turn_hi(4, (2 * b, 2 * b + 1))

        @block.vector
        def _(dve):
            done = [0]

            def chain(ins):
                done[0] += 1
                ins.then_inc(dve_step, 1)
                dve.wait_ge(dve_step, done[0])

            def split_lo(t, i=0, per=0, stream=1):
                _, hi, lo, _ = STREAMS[stream]
                dve.wait_ge(hi, t + 1 + i * per)
                dve.tensor_tensor(split[:, t % SPLIT, 1, :], raw[:, t % RAW, :],
                                  split[:, t % SPLIT, 0, :].bitcast(F32), ALU.subtract).then_inc(lo, 1)

            def norm(n, b):
                if n:
                    dve.wait_ge(g_in, 16 * n)
                else:
                    dve.wait_ge(g_first, 16)
                dve.wait_ge(rstd_ready, NB * n + b + 1)
                for nh in range(2):
                    dve.scalar_tensor_tensor(out=Y[:, b, cols(nh)], in0=X[:, b, cols(nh)],
                                             scalar=rstd[:, b:b + 1], in1=g_row[:, cols(nh)],
                                             op0=ALU.mult, op1=ALU.mult).then_inc(y_ready, 1)

            def turn_lo(n, places=None):
                for at, (b, half) in enumerate(turn_order(n)):
                    if places is None or at in places:
                        dve.wait_ge(hT_hi, 4 * n + at + 1)
                        ks = slice(4 * half, 4 * half + 4)
                        dve.tensor_tensor(hT[:, 1, ks, b * P:(b + 1) * P],
                                          ps[:, turn_bank(n, b, half), :].rearrange("p (k n) -> p k n", k=4),
                                          hT[:, 0, ks, b * P:(b + 1) * P].bitcast(F32), ALU.subtract
                                          ).then_inc(hT_lo, 1)

            def yn_lo_of(b):
                dve.wait_ge(yn_hi, b + 1)
                dve.tensor_tensor(yn[:, 1, b], Y[:, b, :], yn[:, 0, b].bitcast(F32), ALU.subtract
                                  ).then_inc(yn_lo, 1)

            def p_lo(l, bank):
                dve.wait_ge(pT_hi, l + 1)
                dve.tensor_tensor(pT[:, 1], ps[:, bank, :].rearrange("p (k n) -> p k n", k=2),
                                  pT[:, 0].bitcast(F32), ALU.subtract).then_inc(pT_lo, 1)

            def add_half_to_x(b, nh, bank, signal):
                dve.tensor_tensor(X[:, b, cols(nh)], ps[:, bank, :], X[:, b, cols(nh)], ALU.add
                                  ).then_inc(signal, 1)

            def add_to_x(b, b0, signal):
                dve.tensor_tensor(halves(X[:, b, :]), two_banks(b0), halves(X[:, b, :]), ALU.add
                                  ).then_inc(signal, 1)

            def rotate(src, dst, nh, b, nth):
                if nth:
                    dve.wait_ge(rot_ready, nth)
                s4 = src.rearrange("p (h s d) -> p h s d", h=nh, s=2)
                n = nh * HD
                t1 = tmp[:, 0:n].rearrange("p (h s d) -> p h s d", h=nh, s=2)
                t2 = tmp[:, 512:512 + n].rearrange("p (h s d) -> p h s d", h=nh, s=2)
                for s in range(2):
                    cosb = cos1[:, b, :].unsqueeze(1).broadcast_to([P, nh, HALF])
                    sinb = sin2[:, b, s, :].unsqueeze(1).broadcast_to([P, nh, HALF])
                    dve.tensor_tensor(t1[:, :, s, :], s4[:, :, s, :], cosb, ALU.mult)
                    ins = dve.tensor_tensor(t2[:, :, s, :], s4[:, :, 1 - s, :], sinb, ALU.mult)
                chain(ins)
                for d in dst:
                    ins = dve.tensor_tensor(d, t1.rearrange("p h s d -> p h (s d)"),
                                            t2.rearrange("p h s d -> p h (s d)"), ALU.add)
                ins.then_inc(rot_ready, 1)

            def take_probs(l, u):
                dve.wait_ge(pr_turned, 6 * l + u + 1)
                dve.tensor_copy(prT[:, :, :], ps[:, 7, :].rearrange("p (c n) -> p c n", c=4)
                                ).then_inc(prT_ready, 1)

            def mask_scores(l, u):
                nh, n = (4, P) if u < 2 else (2, SEQ)
                h0 = 4 * u if u < 2 else 2 * (u - 2)
                dve.wait_ge(s_done, 6 * l + u + 1)
                if u > 2:
                    dve.wait_ge(pr_turned, 6 * l + u - 2)
                s3 = scores_of(u).rearrange("p (h n) -> p h n", h=nh)
                for h in range(nh):
                    ins = dve.scalar_tensor_tensor(out=s3[:, h, :], in0=ps[:, 6, h * n:(h + 1) * n],
                                                   scalar=HD ** -0.5, in1=mask[:, SEQ - n:SEQ],
                                                   op0=ALU.mult, op1=ALU.add)
                chain(ins)
                chain(dve.tensor_reduce(mx[:, 0:nh], s3, AX.X, ALU.max))
                chain(dve.tensor_tensor(mx[:, 0:nh], mx[:, 0:nh], sinks_sb[:, h0:h0 + nh], ALU.max))
                dve.tensor_scalar(nmx[:, u % 2, 0:nh], mx[:, 0:nh], -1.0, None, ALU.mult)
                dve.tensor_tensor(esk[:, u % 2, 0:nh], sinks_sb[:, h0:h0 + nh], mx[:, 0:nh], ALU.subtract
                                  ).then_inc(masked, 1)

            def scale_probs(l, u):
                nh = 4 if u < 2 else 2
                dve.wait_ge(exped, 6 * l + u + 1)
                chain(dve.tensor_tensor(rden[:, 0:nh], den[:, u % 2, 0:nh], esk[:, u % 2, 0:nh], ALU.add))
                chain(dve.reciprocal(rden[:, 0:nh], rden[:, 0:nh]))
                s3 = scores_of(u).rearrange("p (h n) -> p h n", h=nh)
                for h in range(nh):
                    ins = dve.tensor_scalar(s3[:, h, :], s3[:, h, :], rden[:, h:h + 1], None, ALU.mult)
                ins.then_inc(probs, 1)

            def build_g(s, col, signal):
                for b in range(NB):
                    ins = dve.tensor_scalar(G[:, b, :], slot_row[:, :], rank[:, b, bass.ds(col, 1)], None,
                                            ALU.is_equal)
                ins.then_inc(signal, 1)

            def gather_lo(s, n):
                for half in range(2):
                    dve.wait_ge(xe_hi[s], n + half + 1)
                    ks = slice(4 * half, 4 * half + 4)
                    dve.tensor_tensor(xe[:, 1, ks, :], ps[:, 2 + half, :].rearrange("p (k n) -> p k n", k=4),
                                      xe[:, 0, ks, :].bitcast(F32), ALU.subtract).then_inc(xe_lo[s], 1)

            def body(s, nb, moe, t0, i, last_split):
                stream = 2 if s == 2 else 1
                aT = aT_moe if moe else aT_dense
                j = 0
                for step, kind, f in body_schedule(moe):
                    if step == "swiglu" or (step == "tile" and kind == "b"):
                        for b in swiglu_blocks(moe, kind, f):
                            dve.wait_ge(silu_ready[s], nb * f + b + 1 + i * (nb * BODY_F))
                            bank = 4 + (f % 2 if moe else b)
                            dve.tensor_tensor(tmp[:, b * 256:(b + 1) * 256], ps[:, bank, 256:512],
                                              sg[:, b, 0:256], ALU.mult).then_inc(act_ready[s], 1)
                    if step == "tile":
                        if j + 2 < BODY_TILES + last_split:
                            split_lo(t0 + j + 2, i, BODY_TILES, stream)
                        j += 1
                    elif step == "turn":
                        dve.wait_ge(aT_hi[s], f + 1 + i * BODY_F)
                        dve.tensor_tensor(aT[:, f % 2, 1], ps[:, 6 + f % 2, 0:nb * SEQ].rearrange(
                            "p (k n) -> p k n", k=2), aT[:, f % 2, 0].bitcast(F32), ALU.subtract
                            ).then_inc(aT_lo[s], 1)
                    elif step == "scatter":
                        dve.wait_ge(scattered[s], f + 1 + i * NB)
                        add_to_x(f, SCATTER_BANKS[f], x_ffn[s])
                    elif step == "route":
                        dve.wait_ge(gT_ready[s], 2 + i)
                        dve.tensor_copy(w_slot[:, :], ps[:, 2, SEQ:SEQ + 1]).then_inc(ws_ready[s], 1)
                        build_g(s, i + 1 + (EXPERTS if s == 2 else 0), g_ready[s])
                    elif step == "gather":
                        gather_lo(s, 2 + i * 2)
                    elif step == "close" and moe:
                        for nh in range(2):
                            dve.wait_ge(ye_hi[s], nh + 1 + i * 2)
                            cols = slice(nh * 512, (nh + 1) * 512)
                            dve.scalar_tensor_tensor(out=ye[:, 1, cols], in0=ps[:, nh, :],
                                                     scalar=w_slot[:, 0:1], in1=ye[:, 0, cols].bitcast(F32),
                                                     op0=ALU.mult, op1=ALU.subtract).then_inc(ye_lo[s], 1)
                    elif step == "close":
                        for b in range(nb):
                            for nh in range(2):
                                wait_half(dve, b, nh, down_done, 3 * i, t0 + BODY_TILES - 1, i, BODY_TILES)
                                add_half_to_x(b, nh, 2 * b + nh, x_ffn[s])

            def experts(s, t0):
                dve.sem_inc(x_ffn[s], 1)
                if s == 2:
                    dve.memset(ye[:, :, :].bitcast(U32), 0).then_inc(ye_lo[s], 2)
                    dve.memset(GT[:, :].bitcast(U32), 0).then_inc(gT_ready[s], 1)
                    build_g(s, EXPERTS, g_ready[s])
                    gather_lo(s, 0)
                    dve.sem_inc(lo_ready2, BODY_TILES)
                    for t in range(2):
                        split_lo(BODY_TILES + t, stream=2)
                with dve.Fori(0, EXPERTS - 1) as e:
                    body(s, 1, True, t0, e, 2)
                body(s, 1, True, t0, EXPERTS - 1, 0)
                for nh in range(2):
                    for b in range(NB):
                        dve.wait_ge(scattered[s], EXPERTS * NB + 2 * nh + b + 1)
                        add_half_to_x(b, nh, SCATTER_BANKS[b] + nh, x_ffn[s])

            PI = float(np.pi)

            def parts(value, bits, count):
                got = []
                for _ in range(count):
                    e = int(np.floor(np.log2(abs(value))))
                    q = 2.0 ** (e - bits + 1)
                    got.append(float(np.floor(value / q) * q))
                    value -= got[-1]
                return got

            dve.wait_ge(pos_in, 32)
            chain(dve.tensor_copy(pos_f[:, :], pos_i[:, :]))
            for b in range(NB):
                ins = dve.tensor_scalar(ang[:, 0, b, :], freq[:, :], pos_f[:, b:b + 1], None, ALU.mult)
            chain(ins)

            def take_off(period, bits, count):
                chain(dve.tensor_scalar(turns[:, 0], ang[:, 0], 1.0 / period, 12582912.0, ALU.mult, ALU.add))
                chain(dve.tensor_scalar(turns[:, 0], turns[:, 0], -12582912.0, None, ALU.add))
                for part in parts(period, bits, count):
                    chain(dve.scalar_tensor_tensor(out=ang[:, 0], in0=turns[:, 0], scalar=-part, in1=ang[:, 0],
                                                   op0=ALU.mult, op1=ALU.add))
            take_off(4096 * 2 * PI, 7, 6)
            for b in range(NB):
                norm(0, b)
            turn_lo(0, (0, 1))
            split_lo(0)
            turn_lo(0, (2, 3))
            take_off(2 * PI, 11, 4)
            chain(dve.tensor_scalar(ang[:, 1], ang[:, 0], PI / 2, None, ALU.add))
            chain(dve.tensor_scalar(turns[:, 1], ang[:, 1], PI, -2 * PI, ALU.is_gt, ALU.mult))
            chain(dve.tensor_tensor(ang[:, 1], ang[:, 1], turns[:, 1], ALU.add))
            dve.tensor_scalar(ang[:, :, :, :], ang[:, :, :, :], 3.1415925, -3.1415925, ALU.min, ALU.max
                              ).then_inc(rope_ang, 1)
            dve.wait_ge(consts, 9)
            chain(dve.tensor_scalar(rcount[:, :], slot_row[:, 0:16], 1.0, None, ALU.add))
            dve.reciprocal(rcount[:, :], rcount[:, :]).then_inc(rcount_ready, 1)
            split_lo(1)
            for l in range(DEPTH):
                t0 = LAYER_T0[l]
                split_lo(t0 + 2)
                if l == 0:
                    p_lo(0, 4)
                split_lo(t0 + 3)
                if l == 0:
                    dve.wait_ge(rope_ready, 3)
                for b in range(NB):
                    wait_product(dve, b, NB - 1, q_done, l + 1, t0 + 1)
                    rotate(ps[:, b, :], [q_rot[:, b, :].rearrange("p (h d) -> p h d", h=HEADS)], HEADS, b,
                           4 * l + b)
                split_lo(t0 + 4)
                for b in range(NB):
                    wait_product(dve, b, NB - 1, kv_done, l + 1, t0 + 2)
                    dve.wait_ge(v_ready, NB * l + b + 1)
                    rotate(ps[:, 2 + b, 0:P], [kdup[:, b, :, c, :] for c in range(2)], KV_HEADS, b,
                           4 * l + NB + b)
                chain(dve.memset(vpad[:, :, 0:2], 0.0))
                for j in range(8):
                    split_lo(t0 + T_CHAN + j + 2)
                    cs = slice(2 * (j % 2), 2 * (j % 2) + 2)
                    if j in (2, 3):
                        dve.wait_ge(tile_used, t0 + T_CHAN + j + 1)
                        dve.wait_ge(c_copied, 2 * l + j - 1)
                        dve.tensor_tensor(vpad[:, cs, 2:], ps[:, 4 + j, :].rearrange(
                            "p (c n) -> p c n", c=2), c_sb[:, cs, :], ALU.mult).then_inc(conv_v, 1)
                    if j in (4, 5):
                        dve.wait_ge(small_in, 16 + 96 * (l + 1))
                        dve.wait_ge(conv_v, 2 * l + j - 3)
                        for c in range(2):
                            ch = 2 * (j - 4) + c
                            chain(dve.tensor_scalar(cacc[:, c, :], vpad[:, ch, 0:SEQ], convw_sb[:, ch, 0:1],
                                                    None, ALU.mult))
                            for k in (1, 2):
                                chain(dve.scalar_tensor_tensor(
                                    out=cacc[:, c, :], in0=vpad[:, ch, k:k + SEQ],
                                    scalar=convw_sb[:, ch, k:k + 1], in1=cacc[:, c, :],
                                    op0=ALU.mult, op1=ALU.add))
                        dve.wait_ge(tile_used, t0 + T_CHAN + j + 1)
                        dve.tensor_tensor(ctmp, ps[:, j - 2, :].rearrange("p (c n) -> p c n", c=2), cacc,
                                          ALU.mult).then_inc(conv_y, 1)
                        dve.wait_ge(conv_hi, 2 * l + j - 3)
                        dve.tensor_tensor(brv[:, 1, cs, :], ctmp, brv[:, 0, cs, :].bitcast(F32),
                                          ALU.subtract).then_inc(conv_lo, 1)
                    if j == 5:
                        dve.wait_ge(qk_turned, 3 * l + 3)
                        for s in range(2):
                            half = slice(s * HD, (s + 1) * HD)
                            dve.tensor_copy(kT[half, :, s, :], ps[half, 0, :].rearrange(
                                "p (c n) -> p c n", c=2)).then_inc(kT_ready, 1)
                for c in range(6):
                    for step in range(3):
                        split_lo(t0 + T_GATE + 3 * c + step + 2)
                        at = 3 * c + step
                        for stage, late in ((take_probs, 4), (scale_probs, 3), (mask_scores, 1)):
                            if 0 <= at - ATT - late < 6:
                                stage(l, at - ATT - late)
                        if at == MIX + 1:
                            dve.wait_ge(pool_hi, l + 1)
                            for g in range(CH):
                                ins = dve.scalar_tensor_tensor(
                                    out=brv[:, 3, g, :], in0=ps[:, 2 + g // 2, g % 2 * SEQ:(g % 2 + 1) * SEQ],
                                    scalar=pscale_sb[:, g:g + 1], in1=brv[:, 2, g, :].bitcast(F32),
                                    op0=ALU.mult, op1=ALU.subtract)
                            ins.then_inc(pool_lo, 2)
                        if at == 17:
                            turn_lo(4 * l + 1, (0, 1))
                        if step == 2:
                            r, nh = c // 2, c % 2
                            for b in range(NB):
                                dve.wait_ge(sig_ready, 12 * l + NB * c + b + 1)
                                wait_product(dve, b, NB - 1, branch_done, 6 * l + c + 1,
                                             t0 + T_GATE + 3 * c + 2)
                                m = M[:, b, nh * 512:(nh + 1) * 512]
                                if c == 2:
                                    dve.wait_ge(pr_turned, 6 * l + 4 + b)
                                if r == 0:
                                    dve.tensor_tensor(m, ps[:, b, :], sg[:, b, :], ALU.mult
                                                      ).then_inc(merged, 1)
                                else:
                                    dve.wait_ge(merged, 12 * l + NB * (c - 1) + b + 1)
                                    chain(dve.tensor_tensor(tmp[:, b * 512:(b + 1) * 512], ps[:, b, :],
                                                            sg[:, b, :], ALU.mult))
                                    dve.tensor_tensor(m, m, tmp[:, b * 512:(b + 1) * 512], ALU.add
                                                      ).then_inc(merged, 1)
                        if at == ATT_OUT:
                            for h in range(2):
                                dve.wait_ge(att_hi, 2 * l + h + 1)
                                dve.tensor_tensor(brv[:, 5, 2 * h:2 * h + 2, :],
                                                  ps[:, 2 + h, :].rearrange("p (c n) -> p c n", c=2),
                                                  brv[:, 4, 2 * h:2 * h + 2, :].bitcast(F32), ALU.subtract
                                                  ).then_inc(att_lo, 1)
                if l == 0:
                    dve.wait_ge(router_hi, 1)
                    dve.tensor_tensor(router_split[:, :, 1], router_sb[:, :, :],
                                      router_split[:, :, 0].bitcast(F32), ALU.subtract).then_inc(router_lo, 1)
                split_lo(t0 + T_OUT + 2)
                turn_lo(4 * l + 1, (2, 3))
                for i in range(1, 3):
                    split_lo(t0 + T_OUT + i + 2)
                for nh in range(2):
                    wait_half(dve, 0, nh, out_done, 3 * l, t0 + T_OUT + 3)
                    add_half_to_x(0, nh, OUT_BANKS[0] + nh, x_out)
                norm(3 * l + 1, 0)
                turn_lo(4 * l + 2, (0, 1))
                for nh in range(2):
                    wait_half(dve, 1, nh, out_done, 3 * l, t0 + T_OUT + 3)
                    add_half_to_x(1, nh, OUT_BANKS[1] + nh, x_out)
                split_lo(t0 + T_OUT + 5)
                norm(3 * l + 1, 1)
                if l:
                    yn_lo_of(0)
                turn_lo(4 * l + 2, (2, 3))
                if l == 0:
                    dve.sem_inc(x_ffn[0], 1)
                    with dve.Fori(0, FFN_BODIES[0]) as i:
                        body(0, NB, False, t0 + T_FFN[0], i, 2)
                    dve.wait_ge(x_ffn[0], 1 + 4 * FFN_BODIES[0])
                else:
                    dve.wait_ge(logit_done, NB)
                    logits2 = ps[:, 6, 0:4 * EXPERTS].rearrange("p (b s e) -> p b s e", b=NB, s=2)
                    chain(dve.tensor_copy(logit[:, :, :], logits2[:, :, 1, :]))
                    chain(dve.tensor_tensor(logit[:, :, :], logits2[:, :, 0, :], logit[:, :, :], ALU.add))
                    for b in range(NB):
                        ins = dve.max(top[:, b, :], logit[:, b, :])
                    chain(ins)
                    for b in range(NB):
                        ins = dve.max_index(topi[:, b, :], top[:, b, :], logit[:, b, :])
                    chain(ins)
                    chain(dve.tensor_copy(topf[:, :, :], topi[:, :, :]))
                    for b in range(NB):
                        for k in range(2):
                            ins = dve.tensor_scalar(hot[:, b, k, :], slot_row[:, 0:EXPERTS],
                                                    topf[:, b, k:k + 1], None, ALU.is_equal)
                    chain(ins)
                    dve.tensor_tensor(sel[:, :, :], hot[:, :, 0, :], hot[:, :, 1, :], ALU.add
                                      ).then_inc(sel_ready, 1)
                    dve.tensor_tensor(wts[:, :, 0:1], top[:, :, 1:2], top[:, :, 0:1], ALU.subtract
                                      ).then_inc(sel_ready, 1)
                    dve.memset(rank[:, :, 2 * EXPERTS:], -1.0)
                    yn_lo_of(1)
                    dve.wait_ge(rank_done, 1)
                    chain(dve.scalar_tensor_tensor(out=rank[:, :, 0:EXPERTS],
                                                   in0=ps[:, 6, 64:80].rearrange("p (b e) -> p b e", b=NB),
                                                   scalar=1.0, in1=sel[:, :, :], op0=ALU.add, op1=ALU.mult))
                    chain(dve.tensor_scalar(rank[:, :, 0:EXPERTS], rank[:, :, 0:EXPERTS], -1.0, None, ALU.add))
                    build_g(1, 0, g_ready[1])
                    chain(dve.tensor_scalar(rank[:, :, EXPERTS:2 * EXPERTS], rank[:, :, 0:EXPERTS],
                                            -float(P), None, ALU.add))
                    chain(dve.tensor_copy(load[:, :], ps[:, 6, 80:88]))
                    chain(dve.tensor_reduce(most[:, 0:1], load[:, :], AX.X, ALU.max))
                    chain(dve.tensor_scalar(most[:, 1:2], most[:, 0:1], float(P), None, ALU.is_gt))
                    dve.tensor_copy(more_i[:, :], most[:, 1:2]).then_inc(routed, 1)
                    split_lo(t0 + T_OUT + 6)
                    gather_lo(1, 0)
                    dve.wait_ge(route_step, 1)
                    chain(dve.tensor_scalar(wts[:, :, 2:3], wts[:, :, 1:2], 1.0, None, ALU.add))
                    chain(dve.reciprocal(wts[:, :, 2:3], wts[:, :, 2:3]))
                    chain(dve.tensor_tensor(wts[:, :, 3:4], wts[:, :, 1:2], wts[:, :, 2:3], ALU.mult))
                    for b in range(NB):
                        chain(dve.tensor_scalar(comb[:, b, 0:EXPERTS], hot[:, b, 0, :], wts[:, b, 2:3], None,
                                                ALU.mult))
                        chain(dve.scalar_tensor_tensor(out=comb[:, b, 0:EXPERTS], in0=hot[:, b, 1, :],
                                                       scalar=wts[:, b, 3:4], in1=comb[:, b, 0:EXPERTS],
                                                       op0=ALU.mult, op1=ALU.add))
                    chain(dve.tensor_copy(comb[:, :, EXPERTS:], comb[:, :, 0:EXPERTS]))
                    experts(1, t0 + T_FFN[1])
                    more = dve.value_load(more_i[0:1, 0:1], min_val=0, max_val=1)
                    with dve.If(more > 0):
                        experts(2, BODY_TILES)
                        dve.wait_ge(tile_used2, (EXPERTS + 1) * BODY_TILES)
                        dve.wait_ge(x_ffn[2], 1 + NB * EXPERTS + 4)
                    dve.wait_ge(x_ffn[1], 1 + NB * EXPERTS + 4)
                u = t0 + T_PLE[l]
                if l:
                    split_lo(u)
                norm(3 * l + 2, 0)
                if l == 0:
                    split_lo(u + 1)
                norm(3 * l + 2, 1)
                turn_lo(4 * l + 3, (0, 1))
                if l:
                    split_lo(u + 1)
                turn_lo(4 * l + 3, (2, 3))
                split_lo(u + 2)
                split_lo(u + 3)
                if l == 0:
                    p_lo(1, 6)
                    split_lo(u + 4)
                for b in range(NB):
                    dve.wait_ge(proj_out, NB * l + b + 1)
                    for nh in range(2):
                        dve.wait_ge(psig, 4 * l + 2 * b + nh + 1)
                        if b:
                            dve.wait_ge(x_ple, 4 * l + nh + 1)
                        chain(dve.tensor_tensor(tmp[:, cols(nh)], sg[:, nh, :], M[:, b, cols(nh)], ALU.mult))
                        dve.tensor_tensor(X[:, b, cols(nh)], X[:, b, cols(nh)], tmp[:, cols(nh)], ALU.add
                                          ).then_inc(x_ple, 1)
                    norm(3 * (l + 1), b)
                    if l == 0:
                        turn_lo(4, (2 * b, 2 * b + 1))
                        if b == 0:
                            split_lo(u + 5)

        @block.tensor
        def _(pe):
            def product(dst, lh, rh, start, stop):
                pe.matmul(dst, lh[0], rh[0], start=start, stop=False)
                pe.matmul(dst, lh[0], rh[1], start=False, stop=False)
                return pe.matmul(dst, lh[1], rh[0], start=False, stop=stop)

            def pair(buf, *index):
                return [buf[(slice(None), s) + index] for s in range(2)]

            def tile_pair(t, n, k, cols):
                return [slot(t, s, n)[:, k, cols] for s in range(2)]

            def turn(n, src, ready, places=None):
                for at, (b, half) in enumerate(turn_order(n)):
                    if places is None or at in places:
                        pe.wait_ge(*ready(b, half))
                        for k in range(4):
                            ins = pe.transpose(ps[:, turn_bank(n, b, half), k * P:(k + 1) * P],
                                               src[:, b, (4 * half + k) * P:(4 * half + k + 1) * P],
                                               ident[:, :])
                        ins.then_inc(turned, 1)

            def y_of(n):
                return lambda b, half: (y_ready, 2 * (NB * n + b) + half + 1)

            def turn_p(l, bank):
                pe.wait_ge(p_in[l], 16)
                for k in range(2):
                    for b in range(NB):
                        ins = pe.transpose(ps[:, bank, k * SEQ + b * P:k * SEQ + (b + 1) * P],
                                           p_sb[:, b, k * P:(k + 1) * P], ident[:, :])
                ins.then_inc(p_turned, 1)

            def tokens(b):
                return slice(b * P, (b + 1) * P)

            def wide(t, tiles, n_tiles, lhs, banks, ready, done=None, between=None):
                for b in range(NB):
                    for condition in ready(b):
                        pe.wait_ge(*condition)
                    for i in tiles:
                        if b == 0:
                            pe.wait_ge(lo_ready, t + i + 1)
                        for nh in range(2):
                            for k in range(2):
                                ins = product(ps[:, banks[b] + nh, :], pair(lhs, 2 * i + k, tokens(b)),
                                              tile_pair(t + i, D, k, slice(nh * 512, (nh + 1) * 512)),
                                              i == 0 and k == 0, i == n_tiles - 1 and k == 1)
                                if between and (b, i, nh, k) == between[0]:
                                    between[1]()
                            if done is not None and i == tiles[-1] and (b, nh) != (NB - 1, 1):
                                ins.then_inc(done, 1)
                        if b == NB - 1:
                            ins.then_inc(tile_used, 1)

            def att_scores(l, u):
                b = 0 if u < 2 else 1
                nh, n = (4, P) if u < 2 else (2, SEQ)
                h0 = 4 * u if u < 2 else 2 * (u - 2)
                if u == 0:
                    pe.wait_ge(qT_ready, 2 * l + 2)
                    pe.wait_ge(kT_ready, 2 * (l + 1))
                if u:
                    pe.wait_ge(masked, 6 * l + u)
                for i in range(nh):
                    h = h0 + i
                    ins = pe.matmul(ps[:, 6, i * n:(i + 1) * n], qT[:, h // 2, tokens(b)],
                                    kT[:, h // (HEADS // KV_HEADS), h % 2, 0:n], start=True, stop=True)
                ins.then_inc(s_done, 1)

            def att_turn(l, u):
                pe.wait_ge(probs, 6 * l + u + 1)
                if u:
                    pe.wait_ge(prT_ready, 6 * l + u)
                for i in range(4):
                    ins = pe.transpose(ps[:, 7, i * P:(i + 1) * P], scores_of(u)[:, i * P:(i + 1) * P],
                                       ident[:, :])
                ins.then_inc(pr_turned, 1)

            def att_values(l, u):
                b = 0 if u < 2 else 1
                h0 = 4 * u if u < 2 else 2 * (u - 2)
                pe.wait_ge(prT_ready, 6 * l + u + 1)
                if u == 0:
                    pe.wait_ge(v_ready, NB * (l + 1))
                    pe.wait_ge(pool_lo, 2 * (l + 1))
                per = b + 1
                for i in range(4):
                    h = h0 + i // per
                    kv = h // (HEADS // KV_HEADS)
                    c = h // 2
                    rows = slice(h % 2 * HD, (h % 2 + 1) * HD)
                    ins = pe.matmul(ps[rows, 2 + c // 2, (c % 2) * SEQ + b * P:(c % 2) * SEQ + (b + 1) * P],
                                    v_sb[:, i % per, kv * HD:(kv + 1) * HD], prT[:, i, :],
                                    start=i % per == 0, stop=i % per == per - 1)
                if u == 5:
                    ins.then_inc(att_done, 1)

            def first_chunk(t0, i):
                for b in range(NB):
                    for half in range(2):
                        pe.wait_ge(hT_lo, 8 + 2 * b + half + 1)
                        if b == 0:
                            pe.wait_ge(lo_ready, t0 + half + 1 + i * BODY_TILES)
                        for k in range(4):
                            ins = product(ps[:, 4 + b, :], pair(hT, 4 * half + k, tokens(b)),
                                          tile_pair(t0 + half, 512, k, slice(0, 512)),
                                          half + k == 0, half == 1 and k == 3)
                            if b == 0 and half == 1 and k == 2:
                                with pe.If(i < 1):
                                    turn(2, Y, y_of(1), (2, 3))
                        if b == NB - 1:
                            ins.then_inc(tile_used, 1)
                    if b == 0:
                        ins.then_inc(gu_done, 1)

            def turn_chunk(s, nb, f, i):
                pe.wait_ge(act_ready[s], nb * (f + 1) + i * (nb * BODY_F))
                for k in range(2):
                    for b in range(nb):
                        ins = pe.transpose(ps[:, 6 + f % 2, (k * nb + b) * P:(k * nb + b + 1) * P],
                                           tmp[:, b * 256 + k * P:b * 256 + (k + 1) * P], ident[:, :])
                ins.then_inc(a_turned[s], 1)

            def body(s, nb, moe, t0, i):
                stream = 2 if s == 2 else 1
                _, _, lo, used = STREAMS[stream]
                lhs = xe if moe else hT
                aT = aT_moe if moe else aT_dense
                j = 0
                for step, kind, f in body_schedule(moe):
                    if step == "tile" and not moe and f == 0 and kind in "ab":
                        if kind == "b":
                            first_chunk(t0, i)
                        j += 1
                    elif step == "tile":
                        t = t0 + j
                        pe.wait_ge(lo, t + 1 + i * BODY_TILES)
                        if kind in "ab":
                            k0 = 0 if kind == "a" else 4
                            if moe and f == 0:
                                pe.wait_ge(xe_lo[s], (1 if kind == "a" else 2) + i * 2)
                            for b in range(nb):
                                bank = 4 + (f % 2 if moe else b)
                                if kind == "a" and moe and f >= 2:
                                    pe.wait_ge(act_ready[s], f - 1 + i * BODY_F)
                                if kind == "a" and not moe and f >= 1:
                                    pe.wait_ge(act_ready[s], nb * (f - 1) + b + 1 + i * (nb * BODY_F))
                                for k in range(4):
                                    for m, (sl, sr) in enumerate(((0, 0), (0, 1), (1, 0))):
                                        ins = pe.matmul(ps[:, bank, :], lhs[:, sl, k0 + k, tokens(b)],
                                                        slot(t, sr, 512)[:, k, :],
                                                        start=kind == "a" and k + m == 0,
                                                        stop=kind == "b" and k == 3 and m == 2)
                                if kind == "b" and b < nb - 1:
                                    ins.then_inc(gu_done, 1)
                        else:
                            pe.wait_ge(aT_lo[s], f + 1 + i * BODY_F)
                            if f == 0:
                                pe.wait_ge(x_ffn[s], 2 + i * NB if moe else 1 + i * 4)
                            for b in range(nb):
                                for nh in range(2):
                                    for k in range(2):
                                        for m, (sl, sr) in enumerate(((0, 0), (0, 1), (1, 0))):
                                            ins = pe.matmul(ps[:, 2 * b + nh, :],
                                                            aT[:, f % 2, sl, k, tokens(b)],
                                                            slot(t, sr, D)[:, k, nh * 512:(nh + 1) * 512],
                                                            start=f == 0 and k + m == 0,
                                                            stop=f == BODY_F - 1 and k == 1 and m == 2)
                                    if f == BODY_F - 1 and not moe and (b, nh) != (nb - 1, 1):
                                        ins.then_inc(down_done, 1)
                                    if f == BODY_F - 1 and moe and nh == 0:
                                        ins.then_inc(half_down[s], 1)
                                    if f == BODY_F - 2 and not moe and (b, nh) == (0, 1):
                                        turn_chunk(s, nb, f + 1, i)
                        ins.then_inc(used, 1)
                        j += 1
                    elif step == "turn":
                        if moe or f < BODY_F - 1:
                            turn_chunk(s, nb, f, i)
                    elif step == "scatter":
                        if f == 0:
                            pe.wait_ge(ye_lo[s], 2 + i * 2)
                            pe.wait_ge(xe_lo[s], 2 + i * 2)
                            pe.wait_ge(gT_ready[s], 1 + i)
                        scatter(s, f)
                    elif step == "route":
                        pe.wait_ge(x_ffn[s], 1 + NB + i * NB)
                        for b in range(NB):
                            pe.transpose(ps[:, 2, tokens(b)], G[:, b, :].bitcast(F32), ident[:, :])
                        for b in range(NB):
                            ins = pe.matmul(ps[:, 2, SEQ:SEQ + 1], G[:, b, :].bitcast(F32),
                                            comb[:, b, bass.ds(i + (EXPERTS if s == 2 else 0), 1)],
                                            start=b == 0, stop=b == NB - 1)
                        ins.then_inc(route_done[s], 1)
                    elif step == "gather":
                        pe.wait_ge(g_ready[s], 2 + i)
                        pe.wait_ge(gT_ready[s], 2 + i)
                        gather(s)

            def scatter(s, b, halves=(0, 1)):
                bank = SCATTER_BANKS[b]
                for nh in halves:
                    for k in range(2):
                        ins = pe.matmul(ps[:, bank + nh, :], GT[:, tokens(b)], ye[:, k, nh * 512:(nh + 1) * 512],
                                        start=k == 0, stop=k == 1)
                ins.then_inc(scattered[s], 1)

            def gather(s):
                for k in range(KD):
                    for m, (b, part) in enumerate(((0, 0), (0, 1), (1, 0), (1, 1))):
                        ins = pe.matmul(ps[:, 2 + k // 4, k % 4 * P:(k % 4 + 1) * P],
                                        yn[:, part, b, k * P:(k + 1) * P], G[:, b, :],
                                        start=m == 0, stop=m == 3)
                    if k % 4 == 3:
                        ins.then_inc(gathered[s], 1)

            def logits(b):
                pe.wait_ge(hT_lo, 24 + 2 * (b + 1))
                for k in range(KD):
                    for s in range(2):
                        ins = pe.matmul(ps[:, 6, b * 2 * EXPERTS:(b + 1) * 2 * EXPERTS],
                                        hT[:, s, k, tokens(b)],
                                        router_split[:, k].rearrange("p s e -> p (s e)"),
                                        start=k + s == 0, stop=k + s == KD)
                ins.then_inc(logit_done, 1)

            def experts(s, t0):
                pe.wait_ge(g_ready[s], 1)
                if s == 1:
                    pe.wait_ge(yn_lo, NB)
                gather(s)
                with pe.Fori(0, EXPERTS) as e:
                    body(s, 1, True, t0, e)
                pe.wait_ge(gT_ready[s], EXPERTS + 1)
                pe.wait_ge(xe_lo[s], 2 * (EXPERTS + 1))
                for nh in range(2):
                    pe.wait_ge(ye_lo[s], 2 * EXPERTS + nh + 1)
                    for b in range(NB):
                        scatter(s, b, (nh,))

            def proj_part(b, nh):
                t = LAYER_T0[1] + T_PROJ[1]
                if b + nh == 0:
                    pe.wait_ge(lo_ready, t + 1)
                if nh == 0:
                    pe.wait_ge(x_out, 4 + 2 * (b + 1))
                for k in range(2):
                    ins = product(ps[:, PROJ_BANKS[1][b] + nh, :], pair(pT, k, tokens(b)),
                                  tile_pair(t, D, k, slice(nh * 512, (nh + 1) * 512)), k == 0, k == 1)
                ins.then_inc(tile_used if b and nh else proj_done, 1)

            pe.wait_ge(consts, 9)
            turn(0, Y, y_of(0))
            for l in range(DEPTH):
                t0 = LAYER_T0[l]
                for b, i in ((0, 0), (0, 1), (1, 0), (1, 1)) if l else ((0, 0), (1, 0), (0, 1), (1, 1)):
                    if l and (b, i) == (1, 0):
                        turn(4 * l, Y, y_of(3 * l), (2, 3))
                    pe.wait_ge(hT_lo, 16 * l + 2 * b + i + 1)
                    if b == 0:
                        pe.wait_ge(lo_ready, t0 + i + 1)
                    for k in range(4):
                        ins = product(ps[:, b, :], pair(hT, 4 * i + k, tokens(b)),
                                      tile_pair(t0 + i, 512, k, slice(0, 512)), i + k == 0, i == 1 and k == 3)
                    if b == NB - 1:
                        ins.then_inc(tile_used, 1)
                    elif i == 1:
                        ins.then_inc(q_done, 1)
                if l == 0:
                    turn_p(0, 4)
                t = t0 + 2
                pe.wait_ge(lo_ready, t + 1)
                for b in range(NB):
                    for k in range(KD):
                        ins = product(ps[:, 2 + b, 0:256], pair(hT, k, tokens(b)),
                                      tile_pair(t, 256, k, slice(0, 256)), k == 0, k == KD - 1)
                    if b == 0:
                        ins.then_inc(kv_done, 1)
                ins.then_inc(tile_used, 1)
                if l == 0:
                    pe.wait_ge(pT_lo, 1)
                for j, bank in enumerate((4, 5, 6, 7, 2, 3, 4, 5)):
                    t = t0 + T_CHAN + j
                    pe.wait_ge(lo_ready, t + 1)
                    if j == 4:
                        pe.wait_ge(rot_ready, 4 * (l + 1))
                        pe.wait_ge(v_ready, NB * (l + 1))
                    if j in (6, 7):
                        pe.wait_ge(c_copied, 2 * l + j - 5)
                    for c in range(2):
                        for k in range(KD):
                            ins = product(ps[:, bank, c * SEQ:(c + 1) * SEQ],
                                          tile_pair(t, 256, k, slice(c * P, (c + 1) * P)),
                                          pair(hT, k, slice(0, SEQ)), k == 0, k == KD - 1)
                    ins.then_inc(tile_used, 1)
                    if j == 5:
                        pe.wait_ge(rot_ready, 4 * (l + 1))
                        pe.wait_ge(conv_y, 2 * l + 1)
                        for c in range(CH):
                            for b in range(NB):
                                ins = pe.transpose(
                                    ps[:, 6 + c // 2, c % 2 * SEQ + b * P:c % 2 * SEQ + (b + 1) * P],
                                    q_rot[:, b, c * P:(c + 1) * P], ident[:, :])
                            if c % 2:
                                ins.then_inc(qk_turned, 1)
                        for h in range(KV_HEADS):
                            for b in range(NB):
                                ins = pe.transpose(ps[:, 0, h * SEQ + b * P:h * SEQ + (b + 1) * P],
                                                   kdup[:, b, h].rearrange("p c d -> p (c d)"), ident[:, :])
                        ins.then_inc(qk_turned, 1)
                for c in range(6):
                    r, nh = c // 2, c % 2
                    for step in range(3):
                        t = t0 + T_GATE + 3 * c + step
                        at = 3 * c + step
                        pe.wait_ge(lo_ready, t + 1)
                        if step < 2:
                            for b in range(NB):
                                if c and step == 0:
                                    pe.wait_ge(sig_ready, 12 * l + NB * (c - 1) + b + 1)
                                if c == 0 and step == 0:
                                    pe.wait_ge(chan_out, 2 * l + 1 + b)
                                for k in range(4):
                                    ins = product(ps[:, 4 + b, :], pair(hT, 4 * step + k, tokens(b)),
                                                  tile_pair(t, 512, k, slice(0, 512)),
                                                  step + k == 0, step == 1 and k == 3)
                                if step and b == 0:
                                    ins.then_inc(gate_done, 1)
                        else:
                            ready = ((conv_lo, 2 * (l + 1)), (pool_lo, 2 * (l + 1)), (att_lo, 2 * (l + 1)))[r]
                            pe.wait_ge(*ready)
                            if c == 0:
                                pe.wait_ge(kT_ready, 2 * (l + 1))
                            for b in range(NB):
                                if c:
                                    pe.wait_ge(merged, 12 * l + NB * (c - 1) + b + 1)
                                for k in range(CH):
                                    lh = [brv[:, 2 * r + s, k, tokens(b)] for s in range(2)]
                                    ins = product(ps[:, b, :], lh, tile_pair(t, 512, k, slice(0, 512)),
                                                  k == 0, k == CH - 1)
                                if b == 0:
                                    ins.then_inc(branch_done, 1)
                        ins.then_inc(tile_used, 1)
                        if at == MIX:
                            pe.wait_ge(pooled_ready, CH * (l + 1))
                            pe.wait_ge(small_in, 16 + 96 * (l + 1))
                            pe.wait_ge(conv_y, 2 * (l + 1))
                            for g in range(CH):
                                ins = pe.matmul(ps[:, 2 + g // 2, g % 2 * SEQ:(g % 2 + 1) * SEQ],
                                                poolw_sb[:, g, :], pooled[:, g, :], start=True, stop=True)
                            ins.then_inc(mixed_done, 1)
                        for stage, late in ((att_values, 4), (att_turn, 3), (att_scores, 0)):
                            if 0 <= at - ATT - late < 6:
                                stage(l, at - ATT - late)
                        if at == 15:
                            turn(4 * l + 1, M, lambda b, half: (merged, 12 * l + 8 + b + 1), (0, 1))
                wide(t0 + T_OUT, (0, 1), 4, hT, OUT_BANKS,
                     lambda b: [(merged, 12 * l + 12)] if b else [(hT_lo, 16 * l + 6)], None,
                     ((1, 0, 0, 0), lambda: turn(
                         4 * l + 1, M, lambda b, half: (merged, 12 * l + 10 + b + 1), (2, 3))))
                wide(t0 + T_OUT, (2, 3), 4, hT, OUT_BANKS, lambda b: [(hT_lo, 16 * l + 8)], out_done,
                     ((1, 3, 1, 0), lambda: turn(4 * l + 2, Y, y_of(3 * l + 1), (0, 1))))
                if l == 1:
                    pe.wait_ge(router_lo, 1)
                    proj_part(0, 0)
                    logits(0)
                    proj_part(0, 1)
                    turn(6, Y, y_of(4), (2, 3))
                    proj_part(1, 0)
                    logits(1)
                    proj_part(1, 1)
                if l == 0:
                    with pe.Fori(0, FFN_BODIES[0]) as i:
                        body(0, NB, False, t0 + T_FFN[0], i)
                else:
                    pe.wait_ge(sel_ready, 1)
                    pe.matmul(ps[:, 6, 64:80], below[:, :], sel[:, :, :].rearrange("p b e -> p (b e)"),
                              start=True, stop=False)
                    pe.matmul(ps[:, 6, 72:80], ones[:, :], sel[:, 0, :], start=False, stop=True)
                    pe.matmul(ps[:, 6, 80:88], ones[:, :], sel[:, 0, :], start=True, stop=False)
                    pe.matmul(ps[:, 6, 80:88], ones[:, :], sel[:, 1, :], start=False, stop=True
                              ).then_inc(rank_done, 1)
                    pe.wait_ge(proj_out, 2 * NB)
                    experts(1, t0 + T_FFN[1])
                    more = pe.value_load(more_i[0:1, 0:1], min_val=0, max_val=1)
                    with pe.If(more > 0):
                        pe.wait_ge(x_ffn[1], 1 + NB * EXPERTS + 4)
                        pe.sem_inc(tile_used2, BODY_TILES)
                        experts(2, BODY_TILES)
                        pe.wait_ge(x_ffn[2], 1 + NB * EXPERTS + 4)
                u = t0 + T_PLE[l]
                if l == 0:
                    wide(t0 + T_PROJ[0], (0,), 1, pT, PROJ_BANKS[0],
                         lambda b: [(x_ffn[0], 1 + 4 * (FFN_BODIES[0] - 1) + 2 * b + 2)], proj_done)
                turn(4 * l + 3, Y, y_of(3 * l + 2))
                wide(u, (0, 1), 4, hT, (0, 2),
                     lambda b: [(hT_lo, 16 * l + 12 + 2 * b + 1), (proj_out, NB * l + b + 1)])
                if l == 0:
                    turn_p(1, 6)
                wide(u, (2, 3), 4, hT, (0, 2), lambda b: [(hT_lo, 16 * l + 16)], pg_done)
                if l == 0:
                    pe.wait_ge(pT_lo, 2)
                    turn(4, Y, y_of(3), (0, 1))


_INS = ["x", "p", "positions", "norm_mix_g", "w_in", "conv_w", "pool_w", "pool_scale", "attn_sinks",
        "w_branch", "w_out", "norm_ffn_g", "ffn_w_gu", "ffn_w_down", "moe_router", "moe_w_gu",
        "moe_w_down", "norm_ple_g", "ple_w_proj", "ple_w_gate", "final_norm_g"]


def kernel(**inputs):
    import concourse.bacc as bacc
    from concourse.bass_utils import run_bass_kernel_spmd as run

    nc = bacc.Bacc("TRN2", target_bir_lowering=False, num_devices=1, dynamic_dma_scratch_size=4096)
    arrays = {name: np.ascontiguousarray(inputs[name]) for name in _INS}
    arrays["inv_freq"] = (np.float32(10000.0) ** (
        np.float32(-2.0) * np.arange(HALF, dtype=np.float32) / np.float32(HD))).astype(np.float32)[None, :]
    args = [nc.dram_tensor(f"{n}_dram", a.shape, mybir.dt.from_np(a.dtype), kind="ExternalInput").ap()
            for n, a in arrays.items()]
    out = nc.dram_tensor("out_dram", (1, SEQ, D), F32, kind="ExternalOutput").ap()
    trunk(nc, *args, out)
    r = run(nc, [{f"{n}_dram": a for n, a in arrays.items()}], core_ids=[0])
    return r.results[0]["out_dram"]
```
